# Optimizing a Trainium2 kernel written in Bass

```python
import math
import jax, jax.numpy as jnp
from jax import lax
import numpy as np
import jax
import jax.numpy as jnp

D_MODEL = 1024
BATCH = 1
SEQ = 512
DEPTH = 2

GRID_W = 64
CTX_LEN = 256
MIX_W = D_MODEL
DA_HEAD_DIM = 64
DA_W = MIX_W // 2
DA_HEADS = DA_W // (2 * DA_HEAD_DIM)
FN_W = MIX_W - DA_W
FN_GROUPS = 4
FN_GW = FN_W // FN_GROUPS
Q_BLOCK = 128
ROPE_THETA = 10000.0
ROPE_AXIS_DIM = DA_HEAD_DIM // 2
HY_FILTER_EMB = 33
HY_FILTER_HIDDEN = 64
HY_DECAY_TARGET = 1e-2
HY_FAST_DECAY = 0.3
HY_SLOW_DECAY = 1.5
FFN_HIDDEN = ((8 * D_MODEL // 3 + 127) // 128) * 128
N_MOD = 6
LN_EPS = 1e-5
F32 = jnp.float32


def layer_norm(x, g=None, b=None):
    xf = x.astype(F32)
    mu = jnp.mean(xf, -1, keepdims=True)
    var = jnp.mean(jnp.square(xf - mu), -1, keepdims=True)
    y = (xf - mu) * lax.rsqrt(var + LN_EPS)
    if g is not None:
        y = y * g.astype(F32) + b.astype(F32)
    return y.astype(x.dtype)

def ada_params(cvec, w, b):
    m = jax.nn.silu(cvec) @ w + b
    return jnp.split(m[..., None, :], N_MOD, axis=-1)

def modulate(x, shift, scale):
    return layer_norm(x) * (1 + scale) + shift

def dwconv3(u, w, b):
    up = jnp.pad(u, ((0, 0), (1, 1), (0, 0)))
    return up[:, :-2] * w[0] + up[:, 1:-1] * w[1] + up[:, 2:] * w[2] + b

def axial_rope_angles(rows):
    pos_r = jnp.repeat(jnp.arange(rows, dtype=F32), GRID_W)
    pos_c = jnp.tile(jnp.arange(GRID_W, dtype=F32), rows)
    inv = ROPE_THETA ** (-jnp.arange(0, ROPE_AXIS_DIM, 2, dtype=F32) / ROPE_AXIS_DIM)
    return jnp.concatenate([pos_r[:, None] * inv, pos_c[:, None] * inv], -1)

def _rotate(xs, ang):
    x1, x2 = jnp.split(xs, 2, axis=-1)
    cos = jnp.cos(ang)[None, :, None, :].astype(xs.dtype)
    sin = jnp.sin(ang)[None, :, None, :].astype(xs.dtype)
    return jnp.concatenate([x1 * cos - x2 * sin, x2 * cos + x1 * sin], -1)

def rope_2d(x, ang):
    n = ang.shape[-1] // 2
    xr, xc = jnp.split(x, 2, axis=-1)
    return jnp.concatenate([_rotate(xr, ang[:, :n]), _rotate(xc, ang[:, n:])], -1)

def lambda_init(layer_idx):
    return 0.8 - 0.6 * math.exp(-0.3 * layer_idx)

def _split_qk(t):
    B, L, _ = t.shape
    t = t.reshape(B, L, DA_HEADS, 2, DA_HEAD_DIM)
    return t[..., 0, :], t[..., 1, :]

def diff_attention(q1, q2, k1, k2, v, lam):
    B, Lq, H, d = q1.shape
    nb = Lq // Q_BLOCK
    scale = d ** -0.5

    def to_blocks(q):
        return q.reshape(B, nb, Q_BLOCK, H, d).transpose(1, 0, 2, 3, 4)

    def block(qs):
        a1, a2 = qs
        s1 = jnp.einsum('bqhd,bkhd->bhqk', a1, k1).astype(F32) * scale
        s2 = jnp.einsum('bqhd,bkhd->bhqk', a2, k2).astype(F32) * scale
        p = jax.nn.softmax(s1, axis=-1) - lam * jax.nn.softmax(s2, axis=-1)
        return jnp.einsum('bhqk,bkhe->bqhe', p.astype(v.dtype), v)

    o = lax.map(block, (to_blocks(q1), to_blocks(q2)))
    return o.transpose(1, 0, 2, 3, 4).reshape(B, Lq, H, v.shape[-1])

def head_rmsnorm(o, g, post):
    of = o.astype(F32)
    y = of * lax.rsqrt(jnp.mean(of * of, -1, keepdims=True) + LN_EPS) * g.astype(F32) * post
    return y.astype(o.dtype)

def fourier_mix(f):
    B, L, _ = f.shape
    g = f.astype(F32).reshape(B, L, FN_GROUPS, FN_GW)
    return jnp.fft.fftn(g, axes=(1, 3), norm='ortho').real.reshape(B, L, FN_W).astype(f.dtype)

def diff_fourier_mixer(h_lat, h_ctx, w_in, w_out, lq1, lk1, lq2, lk2, subln_g, lam_init, ang, ctx_out):
    B, L, _ = h_lat.shape
    Lc = h_ctx.shape[1]
    lam = (jnp.exp(jnp.sum(lq1.astype(F32) * lk1.astype(F32)))
           - jnp.exp(jnp.sum(lq2.astype(F32) * lk2.astype(F32))) + lam_init)
    post = 1.0 - lam_init
    kv_c = h_ctx @ w_in[:, DA_W:3 * DA_W]
    k1c, k2c = _split_qk(kv_c[..., :DA_W])
    v_c = kv_c[..., DA_W:].reshape(B, Lc, DA_HEADS, 2 * DA_HEAD_DIM)
    p = h_lat @ w_in
    q, k, v, f = jnp.split(p, [DA_W, 2 * DA_W, 3 * DA_W], axis=-1)
    q1, q2 = _split_qk(q)
    k1, k2 = _split_qk(k)
    q1, q2, k1, k2 = rope_2d(q1, ang), rope_2d(q2, ang), rope_2d(k1, ang), rope_2d(k2, ang)
    v = v.reshape(B, L, DA_HEADS, 2 * DA_HEAD_DIM)
    K1 = jnp.concatenate([k1c, k1], axis=1)
    K2 = jnp.concatenate([k2c, k2], axis=1)
    V = jnp.concatenate([v_c, v], axis=1)
    o = head_rmsnorm(diff_attention(q1, q2, K1, K2, V, lam), subln_g, post).reshape(B, L, DA_W)
    y_lat = jnp.concatenate([o, fourier_mix(f)], axis=-1) @ w_out
    y_ctx = None
    if ctx_out:
        q1c, q2c = _split_qk(h_ctx @ w_in[:, :DA_W])
        oc = head_rmsnorm(diff_attention(q1c, q2c, k1c, k2c, v_c, lam), subln_g, post).reshape(B, Lc, DA_W)
        y_ctx = jnp.concatenate([oc, fourier_mix(h_ctx @ w_in[:, 3 * DA_W:])], axis=-1) @ w_out
    return y_lat, y_ctx

def hyena_filter_freq(L, w1, b1, w2, b2, w3, b3, freq, w4):
    t = jnp.linspace(0.0, 1.0, L, dtype=F32)[:, None]
    bands = (HY_FILTER_EMB - 1) // 2
    w = 2.0 * math.pi * jnp.arange(L, dtype=F32)[:, None] / L
    fb = jnp.linspace(1e-4, bands - 1, bands, dtype=F32)[None, :]
    z = jnp.concatenate([t, jnp.cos(fb * w), -jnp.sin(fb * w)], axis=-1)
    fr = freq.astype(F32)
    hdn = jnp.sin(fr * (z @ w1.astype(F32) + b1.astype(F32)))
    hdn = jnp.sin(fr * (hdn @ w2.astype(F32) + b2.astype(F32)))
    hdn = jnp.sin(fr * (hdn @ w3.astype(F32) + b3.astype(F32)))
    h = (hdn @ w4.astype(F32)).reshape(L, 2, D_MODEL)
    min_decay = math.log(HY_DECAY_TARGET) / HY_SLOW_DECAY
    max_decay = math.log(HY_DECAY_TARGET) / HY_FAST_DECAY
    deltas = jnp.abs(jnp.linspace(min_decay, max_decay, D_MODEL, dtype=F32))
    h = h * jnp.exp(-t * deltas)[:, None, :]
    hf, hb = h[:, 0], h[:, 1]
    k2 = jnp.concatenate([hf, jnp.zeros((1, D_MODEL), F32), hb[1:][::-1]], axis=0)
    k2 = k2 / jnp.sum(jnp.abs(k2), axis=0, keepdims=True)
    return jnp.fft.rfft(k2, axis=0)

def hyena_mixer(h, w_in, conv_w, conv_b, filt, d_skip, w_out):
    L = h.shape[1]
    u = dwconv3(h @ w_in, conv_w, conv_b)
    x0, x1, v = jnp.split(u, 3, axis=-1)
    v = v * x1
    k_f = hyena_filter_freq(L, *filt)
    vf = v.astype(F32)
    y = jnp.fft.irfft(jnp.fft.rfft(vf, n=2 * L, axis=1) * k_f[None], n=2 * L, axis=1)[:, :L]
    y = (y + vf * d_skip.astype(F32)).astype(h.dtype)
    return (y * x0) @ w_out

def conv_ffn(h, w_in, conv_w, conv_b, w_out):
    u = dwconv3(h @ w_in, conv_w, conv_b)
    a, g = jnp.split(u, 2, axis=-1)
    return (jax.nn.gelu(a, approximate=False) * g) @ w_out

def first_inputs(seed: int = 0) -> dict:
    key = jax.random.key(seed)
    ks = jax.random.split(key, 34)
    n_even = (DEPTH + 1) // 2
    n_odd = DEPTH // 2
    beta = (8 * DEPTH) ** -0.25
    D = D_MODEL
    F = FFN_HIDDEN
    H = HY_FILTER_HIDDEN

    def nrm(k, shape, s):
        return jax.random.normal(k, shape, F32) * s

    return {
        'x': nrm(ks[0], (BATCH, SEQ, D), 1.0),
        'c': nrm(ks[1], (BATCH, D), 1.0),
        'ctx': nrm(ks[2], (BATCH, CTX_LEN, D), 1.0),
        'c_ctx': nrm(ks[3], (D,), 1.0),
        'mod_w': nrm(ks[4], (DEPTH, D, N_MOD * D), D ** -0.5),
        'mod_b': nrm(ks[5], (DEPTH, N_MOD * D), 0.02),
        'ln1_g': 1.0 + nrm(ks[6], (DEPTH, D), 0.02),
        'ln1_b': nrm(ks[7], (DEPTH, D), 0.02),
        'ln2_g': 1.0 + nrm(ks[8], (DEPTH, D), 0.02),
        'ln2_b': nrm(ks[9], (DEPTH, D), 0.02),
        'ffn_w_in': nrm(ks[10], (DEPTH, D, 2 * F), D ** -0.5),
        'ffn_conv_w': nrm(ks[11], (DEPTH, 3, 2 * F), 3 ** -0.5),
        'ffn_conv_b': nrm(ks[12], (DEPTH, 2 * F), 0.02),
        'ffn_w_out': nrm(ks[13], (DEPTH, F, D), beta * F ** -0.5),
        'da_w_in': nrm(ks[14], (n_even, D, 3 * DA_W + FN_W), D ** -0.5),
        'da_w_out': nrm(ks[15], (n_even, MIX_W, D), beta * MIX_W ** -0.5),
        'da_lam_q1': nrm(ks[16], (n_even, DA_HEAD_DIM), 0.1),
        'da_lam_k1': nrm(ks[17], (n_even, DA_HEAD_DIM), 0.1),
        'da_lam_q2': nrm(ks[18], (n_even, DA_HEAD_DIM), 0.1),
        'da_lam_k2': nrm(ks[19], (n_even, DA_HEAD_DIM), 0.1),
        'da_subln_g': 1.0 + nrm(ks[20], (n_even, 2 * DA_HEAD_DIM), 0.02),
        'hy_w_in': nrm(ks[21], (n_odd, D, 3 * MIX_W), D ** -0.5),
        'hy_conv_w': nrm(ks[22], (n_odd, 3, 3 * MIX_W), 3 ** -0.5),
        'hy_conv_b': nrm(ks[23], (n_odd, 3 * MIX_W), 0.02),
        'hy_f_w1': nrm(ks[24], (n_odd, HY_FILTER_EMB, H), HY_FILTER_EMB ** -0.5),
        'hy_f_b1': nrm(ks[25], (n_odd, H), 0.1),
        'hy_f_w2': nrm(ks[26], (n_odd, H, H), H ** -0.5),
        'hy_f_b2': nrm(ks[27], (n_odd, H), 0.1),
        'hy_f_w3': nrm(ks[28], (n_odd, H, H), H ** -0.5),
        'hy_f_b3': nrm(ks[29], (n_odd, H), 0.1),
        'hy_f_freq': 1.0 + nrm(ks[30], (n_odd, H), 0.1),
        'hy_f_w4': nrm(ks[31], (n_odd, H, 2 * MIX_W), H ** -0.5),
        'hy_d': nrm(ks[32], (n_odd, MIX_W), 1.0),
        'hy_w_out': nrm(ks[33], (n_odd, MIX_W, D), beta * MIX_W ** -0.5),
    }

def first_block(x, c, ctx, c_ctx, mod_w, mod_b, ln1_g, ln1_b, ln2_g, ln2_b,
              ffn_w_in, ffn_conv_w, ffn_conv_b, ffn_w_out,
              da_w_in, da_w_out, da_lam_q1, da_lam_k1, da_lam_q2, da_lam_k2, da_subln_g,
              hy_w_in, hy_conv_w, hy_conv_b, hy_f_w1, hy_f_b1, hy_f_w2, hy_f_b2,
              hy_f_w3, hy_f_b3, hy_f_freq, hy_f_w4, hy_d, hy_w_out):
    n_lat = x.shape[1]
    rows = n_lat // GRID_W
    ang = axial_rope_angles(rows)
    alpha = (2 * DEPTH) ** 0.25
    for i in range(DEPTH):
        even = i % 2 == 0
        ctx_out = any(j % 2 == 0 for j in range(i + 1, DEPTH))
        sh1, sc1, g1, sh2, sc2, g2 = ada_params(c, mod_w[i], mod_b[i])
        h_lat = modulate(x, sh1, sc1)
        if even or ctx_out:
            csh1, csc1, cg1, csh2, csc2, cg2 = ada_params(c_ctx, mod_w[i], mod_b[i])
            h_ctx = modulate(ctx, csh1, csc1)
        if even:
            e = i // 2
            y_lat, y_ctx = diff_fourier_mixer(h_lat, h_ctx, da_w_in[e], da_w_out[e],
                                              da_lam_q1[e], da_lam_k1[e], da_lam_q2[e], da_lam_k2[e],
                                              da_subln_g[e], lambda_init(i), ang, ctx_out)
        else:
            o = i // 2
            filt = (hy_f_w1[o], hy_f_b1[o], hy_f_w2[o], hy_f_b2[o], hy_f_w3[o], hy_f_b3[o],
                    hy_f_freq[o], hy_f_w4[o])
            y_lat = hyena_mixer(h_lat, hy_w_in[o], hy_conv_w[o], hy_conv_b[o], filt, hy_d[o], hy_w_out[o])
            if ctx_out:
                y_ctx = hyena_mixer(h_ctx, hy_w_in[o], hy_conv_w[o], hy_conv_b[o], filt, hy_d[o], hy_w_out[o])
        ffn = (ffn_w_in[i], ffn_conv_w[i], ffn_conv_b[i], ffn_w_out[i])
        x = layer_norm(alpha * x + g1 * y_lat, ln1_g[i], ln1_b[i])
        x = layer_norm(alpha * x + g2 * conv_ffn(modulate(x, sh2, sc2), *ffn), ln2_g[i], ln2_b[i])
        if ctx_out:
            ctx = layer_norm(alpha * ctx + cg1 * y_ctx, ln1_g[i], ln1_b[i])
            ctx = layer_norm(alpha * ctx + cg2 * conv_ffn(modulate(ctx, csh2, csc2), *ffn), ln2_g[i], ln2_b[i])
    return x


N_MIXERS = 2
N_HEADS = 8
HEAD_DIM = D_MODEL // N_HEADS
CHUNK = 64
N_GROUPS = 4
EXPERTS_PER_GROUP = 8
N_EXPERTS = N_GROUPS * EXPERTS_PER_GROUP
TOP_K = 2
D_EXPERT = D_MODEL // 2
MOE_BLOCK = 128
EPS = 1e-6


def rmsnorm(x, g):
    xf = x.astype(jnp.float32)
    y = xf * lax.rsqrt(jnp.mean(xf * xf, axis=-1, keepdims=True) + EPS)
    return (y * g.astype(jnp.float32)).astype(x.dtype)

def modulate_2(x, g, shift, scale):
    return rmsnorm(x, g) * (1 + scale) + shift

def ada_params_2(cond, w, b):
    m = jax.nn.silu(cond) @ w + b
    return jnp.split(m[..., None, :], N_MOD, axis=-1)

def conv3_seq(x, w):
    xp = jnp.pad(x, ((0, 0), (1, 1), (0, 0)))
    return xp[:, :-2] * w[0] + xp[:, 1:-1] * w[1] + xp[:, 2:] * w[2]

def conv3_grid(x, w, rows):
    b, s, ch = x.shape
    half = ch // 2
    g = x.reshape(b, rows, GRID_W, ch)
    wh, wv = w[:, :half], w[:, half:]
    ph = jnp.pad(g[..., :half], ((0, 0), (0, 0), (1, 1), (0, 0)))
    yh = ph[:, :, :-2] * wh[0] + ph[:, :, 1:-1] * wh[1] + ph[:, :, 2:] * wh[2]
    pv = jnp.pad(g[..., half:], ((0, 0), (1, 1), (0, 0), (0, 0)))
    yv = pv[:, :-2] * wv[0] + pv[:, 1:-1] * wv[1] + pv[:, 2:] * wv[2]
    return jnp.concatenate([yh, yv], axis=-1).reshape(b, s, ch)

def l2norm(t):
    return t * lax.rsqrt(jnp.sum(t * t, axis=-1, keepdims=True) + EPS)

def to_chunks(t):
    b, l, h = t.shape[:3]
    t = t.reshape(b, l // CHUNK, CHUNK, h, *t.shape[3:])
    return jnp.moveaxis(t, (1, 3), (0, 2))

def from_chunks(t):
    t = jnp.moveaxis(t, (0, 2), (1, 3))
    b, n, c, h, d = t.shape
    return t.reshape(b, n * c, h, d)

def gated_delta_scan(q, k, v, g, beta, s0, with_output):
    qc, kc, vc = to_chunks(q), to_chunks(k), to_chunks(v)
    gc = jnp.cumsum(to_chunks(g), axis=-1)
    bc = to_chunks(beta)
    pos = jnp.arange(CHUNK)
    incl = pos[:, None] >= pos[None, :]
    decay = jnp.exp(jnp.where(incl, gc[..., :, None] - gc[..., None, :], -jnp.inf))
    kb = kc * bc[..., None]
    lmat = jnp.where(pos[:, None] > pos[None, :],
                     jnp.einsum('nbhid,nbhjd->nbhij', kb, kc) * decay, 0.0)
    rhs = jnp.concatenate([vc * bc[..., None], kb * jnp.exp(gc)[..., None]], axis=-1)
    sol = lax.linalg.triangular_solve(lmat, rhs, left_side=True, lower=True, unit_diagonal=True)
    dv = vc.shape[-1]
    u, w = sol[..., :dv], sol[..., dv:]
    k_dec = kc * jnp.exp(gc[..., -1:] - gc)[..., None]
    g_last = jnp.exp(gc[..., -1])
    xs = (u, w, k_dec, g_last)
    if with_output:
        xs = xs + (qc * jnp.exp(gc)[..., None], jnp.einsum('nbhid,nbhjd->nbhij', qc, kc) * decay)

    def step(s, inp):
        u_i, w_i, kd_i, gl_i = inp[:4]
        v_new = u_i - jnp.einsum('bhcd,bhde->bhce', w_i, s)
        s_next = s * gl_i[..., None, None] + jnp.einsum('bhcd,bhce->bhde', kd_i, v_new)
        if with_output:
            qd_i, qk_i = inp[4:]
            o = jnp.einsum('bhcd,bhde->bhce', qd_i, s) + jnp.einsum('bhij,bhje->bhie', qk_i, v_new)
            return s_next, o
        return s_next, None

    s_final, o = lax.scan(step, s0, xs)
    return s_final, (from_chunks(o) if with_output else None)

def deltanet_mixer(h_lat, h_ctx, w_in, conv_w, a_log, dt_bias, onorm, w_out, ctx_out):
    d, nh, f32 = D_MODEL, N_HEADS, jnp.float32

    def project(h):
        b, l, _ = h.shape
        p = h @ w_in
        qkv = jax.nn.silu(conv3_seq(p[..., :3 * d], conv_w))
        q, k, v = (t.reshape(b, l, nh, HEAD_DIM).astype(f32) for t in jnp.split(qkv, 3, axis=-1))
        q = l2norm(q) * HEAD_DIM ** -0.5
        k = l2norm(k)
        z = p[..., 3 * d:4 * d]
        beta = jax.nn.sigmoid(p[..., 4 * d:4 * d + 2 * nh].astype(f32)).reshape(b, l, 2, nh)
        a_in = p[..., 4 * d + 2 * nh:].astype(f32).reshape(b, l, 2, nh)
        g = -jnp.exp(a_log.astype(f32)) * jax.nn.softplus(a_in + dt_bias.astype(f32))
        return q, k, v, z, beta, g

    def bidir(q, k, v, beta, g, s_f, s_b, with_output):
        flip = lambda t: t[:, ::-1]
        rf = gated_delta_scan(q, k, v, g[:, :, 0], beta[:, :, 0], s_f, with_output)
        rb = gated_delta_scan(flip(q), flip(k), flip(v), flip(g[:, :, 1]), flip(beta[:, :, 1]),
                              s_b, with_output)
        return rf, rb

    def finish(o, z):
        b, l = z.shape[:2]
        o = o * lax.rsqrt(jnp.mean(o * o, axis=-1, keepdims=True) + EPS) * onorm.astype(f32)
        y = o.astype(z.dtype) * jax.nn.silu(z).reshape(b, l, nh, HEAD_DIM)
        return y.reshape(b, l, d) @ w_out

    qc, kc, vc, zc, bc, gc = project(h_ctx)
    s_zero = jnp.zeros((h_ctx.shape[0], nh, HEAD_DIM, HEAD_DIM), f32)
    (sf, ocf), (sb, ocb) = bidir(qc, kc, vc, bc, gc, s_zero, s_zero, ctx_out)
    y_ctx = finish(ocf + ocb[:, ::-1], zc) if ctx_out else None
    ql, kl, vl, zl, bl, gl = project(h_lat)
    (_, olf), (_, olb) = bidir(ql, kl, vl, bl, gl, sf, sb, True)
    y_lat = finish(olf + olb[:, ::-1], zl)
    return y_lat, y_ctx

def shortconv_mixer(h, w_in, conv_w, w_out, rows):
    gate_b, gate_c, hx = jnp.split(h @ w_in, 3, axis=-1)
    u = gate_c * hx
    y = conv3_grid(u, conv_w, rows) if rows is not None else conv3_seq(u, conv_w)
    return (gate_b * y) @ w_out

def hier_moe(h, router_g, router_e, w1, w3, w2):
    f32 = jnp.float32
    t, d = h.shape
    hf = h.astype(f32)
    pg = jax.nn.softmax(hf @ router_g.astype(f32), axis=-1)
    gi = jnp.argmax(pg, axis=-1).astype(jnp.int32)
    pg_sel = jnp.take_along_axis(pg, gi[:, None], axis=-1)
    le = (hf @ router_e.astype(f32)).reshape(t, N_GROUPS, EXPERTS_PER_GROUP)
    le_sel = jnp.take_along_axis(le, gi[:, None, None], axis=1)[:, 0]
    pk, ik = lax.top_k(jax.nn.softmax(le_sel, axis=-1), TOP_K)
    wts = pg_sel * pk / jnp.sum(pk, axis=-1, keepdims=True)
    eid = gi[:, None] * EXPERTS_PER_GROUP + ik.astype(jnp.int32)

    n = t * TOP_K
    n_blocks = -(-n // MOE_BLOCK) + N_EXPERTS
    cap = n_blocks * MOE_BLOCK
    flat_e = eid.reshape(-1)
    flat_tok = jnp.repeat(jnp.arange(t, dtype=jnp.int32), TOP_K)
    flat_w = wts.reshape(-1)
    order = jnp.argsort(flat_e)
    se = flat_e[order]
    counts = jnp.zeros((N_EXPERTS,), jnp.int32).at[flat_e].add(1)
    padded = (counts + MOE_BLOCK - 1) // MOE_BLOCK * MOE_BLOCK
    ends_pad = jnp.cumsum(padded)
    start_pad = ends_pad - padded
    start_raw = jnp.cumsum(counts) - counts
    dest = start_pad[se] + jnp.arange(n, dtype=jnp.int32) - start_raw[se]
    buf_tok = jnp.full((cap,), t, jnp.int32).at[dest].set(flat_tok[order])
    buf_w = jnp.zeros((cap,), f32).at[dest].set(flat_w[order])
    block_e = jnp.minimum(
        jnp.searchsorted(ends_pad, jnp.arange(n_blocks, dtype=jnp.int32) * MOE_BLOCK, side='right'),
        N_EXPERTS - 1).astype(jnp.int32)
    h_pad = jnp.concatenate([h, jnp.zeros((1, d), h.dtype)], axis=0)
    xb = h_pad[buf_tok].reshape(n_blocks, MOE_BLOCK, d)

    def expert_block(args):
        xi, e = args
        return (jax.nn.silu(xi @ w1[e]) * (xi @ w3[e])) @ w2[e]

    yb = lax.map(expert_block, (xb, block_e)).reshape(cap, d)
    y = jax.ops.segment_sum(yb * buf_w[:, None].astype(yb.dtype), buf_tok, num_segments=t + 1)
    return y[:t]

def second_inputs(seed: int = 0) -> dict:
    key = jax.random.key(seed)
    ks = jax.random.split(key, 24)
    d, nh, f32 = D_MODEL, N_HEADS, jnp.float32
    n_a = (DEPTH + N_MIXERS - 1) // N_MIXERS
    n_b = DEPTH // N_MIXERS

    def nrm(k, shape, scale):
        return jax.random.normal(k, shape, f32) * scale

    dt = jnp.exp(jax.random.uniform(ks[10], (n_a, 2, nh), f32, math.log(1e-3), math.log(1e-1)))
    return {
        'x': nrm(ks[0], (BATCH, SEQ, d), 1.0),
        'c': nrm(ks[1], (BATCH, d), 1.0),
        'ctx': nrm(ks[2], (BATCH, CTX_LEN, d), 1.0),
        'c_ctx': nrm(ks[3], (d,), 1.0),
        'ada_w': nrm(ks[4], (DEPTH, d, N_MOD * d), 0.5 * d ** -0.5),
        'ada_b': nrm(ks[5], (DEPTH, N_MOD * d), 0.02),
        'norm_mix': 1.0 + nrm(ks[6], (DEPTH, d), 0.05),
        'norm_ffn': 1.0 + nrm(ks[7], (DEPTH, d), 0.05),
        'w_in_a': nrm(ks[8], (n_a, d, 4 * d + 4 * nh), d ** -0.5),
        'conv_a': nrm(ks[9], (n_a, 3, 3 * d), 3 ** -0.5),
        'a_log_a': jnp.log(jax.random.uniform(ks[11], (n_a, 2, nh), f32, 1.0, 16.0)),
        'dt_bias_a': dt + jnp.log(-jnp.expm1(-dt)),
        'onorm_a': 1.0 + nrm(ks[12], (n_a, HEAD_DIM), 0.05),
        'w_out_a': nrm(ks[13], (n_a, d, d), d ** -0.5),
        'w_in_b': nrm(ks[14], (n_b, d, 3 * d), d ** -0.5),
        'conv_b': nrm(ks[15], (n_b, 3, d), 3 ** -0.5),
        'w_out_b': nrm(ks[16], (n_b, d, d), d ** -0.5),
        'router_g': nrm(ks[17], (DEPTH, d, N_GROUPS), d ** -0.5),
        'router_e': nrm(ks[18], (DEPTH, d, N_EXPERTS), d ** -0.5),
        'w1': nrm(ks[19], (DEPTH, N_EXPERTS, d, D_EXPERT), d ** -0.5),
        'w3': nrm(ks[20], (DEPTH, N_EXPERTS, d, D_EXPERT), d ** -0.5),
        'w2': nrm(ks[21], (DEPTH, N_EXPERTS, D_EXPERT, d), D_EXPERT ** -0.5),
        'final_norm': 1.0 + nrm(ks[22], (d,), 0.05),
    }

def second_block(x, c, ctx, c_ctx, ada_w, ada_b, norm_mix, norm_ffn,
              w_in_a, conv_a, a_log_a, dt_bias_a, onorm_a, w_out_a,
              w_in_b, conv_b, w_out_b, router_g, router_e, w1, w3, w2, final_norm):
    b, s, d = x.shape
    rows = s // GRID_W
    kinds = [i % N_MIXERS for i in range(DEPTH)]
    for i in range(DEPTH):
        kind, j = kinds[i], i // N_MIXERS
        ctx_live = 0 in kinds[i + 1:]
        sh_m, sc_m, gt_m, sh_f, sc_f, gt_f = ada_params_2(c, ada_w[i], ada_b[i])
        if kind == 0 or ctx_live:
            csh_m, csc_m, cgt_m, csh_f, csc_f, cgt_f = ada_params_2(c_ctx, ada_w[i], ada_b[i])
            hc = modulate_2(ctx, norm_mix[i], csh_m, csc_m)
        h = modulate_2(x, norm_mix[i], sh_m, sc_m)
        if kind == 0:
            y, yc = deltanet_mixer(h, hc, w_in_a[j], conv_a[j], a_log_a[j], dt_bias_a[j],
                                   onorm_a[j], w_out_a[j], ctx_live)
        else:
            y = shortconv_mixer(h, w_in_b[j], conv_b[j], w_out_b[j], rows)
            yc = shortconv_mixer(hc, w_in_b[j], conv_b[j], w_out_b[j], None) if ctx_live else None
        x = x + gt_m * y
        hf = modulate_2(x, norm_ffn[i], sh_f, sc_f).reshape(b * s, d)
        if ctx_live:
            ctx = ctx + cgt_m * yc
            hcf = modulate_2(ctx, norm_ffn[i], csh_f, csc_f).reshape(-1, d)
            out = hier_moe(jnp.concatenate([hf, hcf], axis=0), router_g[i], router_e[i],
                           w1[i], w3[i], w2[i])
            x = x + gt_f * out[:b * s].reshape(b, s, d)
            ctx = ctx + cgt_f * out[b * s:].reshape(ctx.shape)
        else:
            x = x + gt_f * hier_moe(hf, router_g[i], router_e[i], w1[i], w3[i], w2[i]).reshape(b, s, d)
    return rmsnorm(x, final_norm)


def setup_inputs(seed=0):
    out = dict(first_inputs(seed))
    for name, value in second_inputs(seed + 1).items():
        if name != "x":
            out[name + "_2"] = value
    return out


def reference(
    x, c, ctx, c_ctx, mod_w, mod_b, ln1_g, ln1_b, ln2_g, ln2_b, ffn_w_in, ffn_conv_w,
    ffn_conv_b, ffn_w_out, da_w_in, da_w_out, da_lam_q1, da_lam_k1, da_lam_q2, da_lam_k2,
    da_subln_g, hy_w_in, hy_conv_w, hy_conv_b, hy_f_w1, hy_f_b1, hy_f_w2, hy_f_b2, hy_f_w3,
    hy_f_b3, hy_f_freq, hy_f_w4, hy_d, hy_w_out, c_2, ctx_2, c_ctx_2, ada_w_2, ada_b_2,
    norm_mix_2, norm_ffn_2, w_in_a_2, conv_a_2, a_log_a_2, dt_bias_a_2, onorm_a_2, w_out_a_2,
    w_in_b_2, conv_b_2, w_out_b_2, router_g_2, router_e_2, w1_2, w3_2, w2_2, final_norm_2,
):
    x = first_block(
        x, c, ctx, c_ctx, mod_w, mod_b, ln1_g, ln1_b, ln2_g, ln2_b, ffn_w_in, ffn_conv_w,
        ffn_conv_b, ffn_w_out, da_w_in, da_w_out, da_lam_q1, da_lam_k1, da_lam_q2, da_lam_k2,
        da_subln_g, hy_w_in, hy_conv_w, hy_conv_b, hy_f_w1, hy_f_b1, hy_f_w2, hy_f_b2, hy_f_w3,
        hy_f_b3, hy_f_freq, hy_f_w4, hy_d, hy_w_out,
    )
    return second_block(
        x, c_2, ctx_2, c_ctx_2, ada_w_2, ada_b_2, norm_mix_2, norm_ffn_2, w_in_a_2, conv_a_2,
        a_log_a_2, dt_bias_a_2, onorm_a_2, w_out_a_2, w_in_b_2, conv_b_2, w_out_b_2, router_g_2,
        router_e_2, w1_2, w3_2, w2_2, final_norm_2,
    )


_drawn_inputs = setup_inputs


def setup_inputs(seed=0):
    import zlib

    import numpy as np

    out = dict(_drawn_inputs(seed))
    spreads = {}
    factors = {'ffn_conv_b': 3.782,
     'da_lam_q2': 2.94,
     'da_subln_g': 8.0,
     'hy_conv_b': 3.182,
     'hy_f_b1': 3.11,
     'hy_f_freq': 4.501,
     'ctx_2': 3.297,
     'c_ctx_2': 4.459,
     'onorm_a_2': 3.862}
    for name, (base, spread) in spreads.items():
        noise = np.random.default_rng([zlib.crc32(name.encode()), seed]).standard_normal(out[name].shape)
        drawn = base * np.exp(spread * noise) if base else spread * noise
        out[name] = jnp.asarray(drawn.astype(out[name].dtype))
    for name, factor in factors.items():
        out[name] = (out[name] * factor).astype(out[name].dtype)
    return out
```

```python
import math
from contextlib import ExitStack

import numpy as np
import concourse.bass as bass
from concourse import mybir

F32 = mybir.dt.float32
I32 = mybir.dt.int32
U32 = mybir.dt.uint32
ALU = mybir.AluOpType
ACT = mybir.ActivationFunctionType
AX = mybir.AxisListType
ds = bass.ds

P = 128
D = 1024
KD = D // P
T = 512
TC = 256
FFN = 2816
NF = FFN // P
DEPTH = 2
ALPHA = (2 * DEPTH) ** 0.25
LN_EPS, RMS_EPS = 1e-5, 1e-6
HEADS = 4
DHEADS = 8
NT = T // P
NTC = TC // P
NTA = NT + NTC
KEYS = TC + T
SLOTS = 4
SLOT = KD * 512
EXPERTS, GROUPS, PER_GROUP = 32, 4, 8
BLOCKS = 2 * T // P + EXPERTS
GRID_W = 64
HID = 64
LAM_INIT = 0.8 - 0.6

_VECTORS = (
    [(f"mod_b{i}", 48) for i in range(2)]
    + [(f"{n}{i}", 8) for n in ("ln1_g", "ln1_b", "ln2_g", "ln2_b") for i in range(2)]
    + [(f"ffn_conv_w{i}{t}", 44) for i in range(2) for t in range(3)]
    + [(f"ffn_conv_b{i}", 44) for i in range(2)]
    + [("da_subln_g", 1)]
    + [(f"hy_conv_w{t}", 24) for t in range(3)] + [("hy_conv_b", 24), ("hy_d", 8)]
    + [(f"ada_b{i}", 48) for i in range(2)]
    + [(f"{n}{i}", 8) for n in ("norm_mix", "norm_ffn") for i in range(2)]
    + [(f"conv_a{t}", 24) for t in range(3)] + [("onorm_a", 1)]
    + [(f"conv_b{t}", 8) for t in range(3)] + [("final_norm", 8)]
    + [(n, 8) for n in ("c", "c_ctx", "c_2", "c_ctx_2")]
)
PAR = {}
_at = 0
for _n, _k in _VECTORS:
    PAR[_n] = (_at, _k)
    _at += _k
NPAR = _at

_CONST_COLS = {}


def _const_layout():
    at = 0
    for name, n in (("ident", P), ("ones", P), ("one_over_d", P), ("one_over_p", P), ("swap", P),
                    ("cum_f", P), ("cum_b", P), ("before", P), ("eps", 4),
                    ("iota", 64), ("iota_neg", 8)):
        _CONST_COLS[name] = (at, n)
        at += n
    return at


NCONST = _const_layout()


def _constants():
    c = np.zeros((P, NCONST), np.float32)

    def put(name, v):
        a, n = _CONST_COLS[name]
        c[:, a:a + n] = v

    j, i = np.arange(P)[:, None], np.arange(P)[None, :]
    put("ident", j == i)
    put("ones", 1.0)
    put("one_over_d", 1.0 / D)
    put("one_over_p", 1.0 / P)
    put("swap", i == (j ^ 16))
    put("cum_f", j <= i)
    put("cum_b", j >= i)
    put("before", j < i)
    put("eps", np.array([LN_EPS, RMS_EPS, 1.0, 0.0]))
    put("iota", np.arange(64)[None, :])
    levels = []
    for s in (1, 2, 4, 8, 16, 32, 64):
        same = (j // (2 * s)) == (i // (2 * s))
        levels.append(same & ((i // s) % 2 == 1) & ((j // s) % 2 == 0))
    levels += [m.T for m in levels]
    masks = np.stack(levels, 1).reshape(P, 14 * P).astype(np.float32)
    p = np.arange(P)
    inv = np.float32(10000.0) ** (-np.arange(0, 32, 2, dtype=np.float32) / np.float32(32))
    tok = np.arange(T)
    pos = np.where(((p % 64) // 32 == 0)[:, None], (tok // GRID_W)[None, :], (tok % GRID_W)[None, :])
    ang = pos.astype(np.float32) * inv.astype(np.float32)[p % 16][:, None]
    sign = np.where(p % 32 < 16, -1.0, 1.0)[:, None]
    rope = np.concatenate([np.cos(ang), sign * np.sin(ang)], 1).astype(np.float32)
    a = 2 * np.pi * (np.outer(np.arange(P), np.arange(P)) % P) / P
    cs = np.concatenate([np.cos(a), np.sin(a)], 1) / math.sqrt(T * P)
    a = 2 * np.pi * (np.outer(np.arange(T), np.arange(T)) % T) / T
    fl = np.stack([np.cos(a), -np.sin(a)]).reshape(2, NT, P, T).transpose(2, 0, 1, 3).reshape(P, -1)
    ph = 2 * np.pi * (np.outer(2 * np.arange(T) + 1, np.arange(T)) % (4 * T)) / (4 * T)
    fwd = np.stack([np.cos(ph.T), np.sin(ph.T)]).reshape(2, NT, P, T).transpose(2, 0, 1, 3).reshape(P, -1)
    back = (np.stack([np.cos(ph), np.sin(ph)]) / T).reshape(2, NT, P, T).transpose(2, 0, 1, 3).reshape(P, -1)
    t = np.linspace(0.0, 1.0, T, dtype=np.float32)[:, None]
    w = (np.float32(2.0 * math.pi) * np.arange(T, dtype=np.float32)[:, None] / np.float32(T)).astype(np.float32)
    fb = np.linspace(1e-4, 15, 16, dtype=np.float32)[None, :]
    fw = (fb * w).astype(np.float32)
    z = np.concatenate([t, np.cos(fw), -np.sin(fw)], -1).T
    deltas = np.abs(np.linspace(math.log(1e-2) / 1.5, math.log(1e-2) / 0.3, D, dtype=np.float32))
    decay = np.exp(-t * deltas).reshape(NT, P, D).transpose(1, 0, 2).reshape(P, -1)
    out = {"const": c, "masks": masks, "rope": rope, "fm_cs": cs, "fm_l": fl, "hy_fwd": fwd,
           "hy_back": back, "hy_z": z, "hy_decay": decay}
    return {k: np.ascontiguousarray(v, dtype=np.float32) for k, v in out.items()}


class Core:

    def __init__(self, nc, d, stack):
        self.nc, self.d = nc, d
        self.stack = stack
        self.names = 0
        self.arena = stack.enter_context(nc.sbuf_tensor("arena", [P, ARENA], F32))
        self.ps = stack.enter_context(nc.psum_tensor("psum", [P, 8, 512], F32))
        self.kept = {}
        self.stage_end = self.sem("stage_end")
        self.slab_in = [self.sem(f"slab_in{i}") for i in range(SLOTS)]
        self.slab_out = [self.sem(f"slab_out{i}") for i in range(SLOTS)]
        self.slabs = []
        self.arrivals = [0] * SLOTS
        self.norms = self.centred = self.tags = 0
        self.x = self.view(X0, KD, T)
        self.h = self.view(H0, KD, T)
        self.hc = self.view(HC0, KD, TC)

    def shared(self, name, n):
        if name not in self.kept:
            self.kept[name] = [self.sem(name), 0]
        s, base = self.kept[name]
        self.kept[name][1] += n
        return s, base

    def sem(self, name):
        return self.stack.enter_context(self.nc.semaphore(name))

    def view(self, at, *dims):
        n = int(np.prod(dims))
        v = self.arena[:, at:at + n]
        if len(dims) == 1:
            return v
        names = "abcde"[:len(dims)]
        return v.rearrange(f"p ({' '.join(names)}) -> p {' '.join(names)}", **dict(zip(names[:-1], dims[:-1])))

    def tag(self):
        self.tags += 1
        return self.tags

    def score(self, half):
        return self.ps.rearrange("p b n -> p (b n)")[:, 1024 * half:1024 * half + KEYS]

    def pair(self, bank, n):
        return self.ps.rearrange("p b n -> p (b n)")[:, 512 * bank:512 * bank + n]

    def const(self, name):
        a, n = _CONST_COLS[name]
        return self.arena[:, CONST0 + a:CONST0 + a + n]

    def eps(self, i):
        a = CONST0 + _CONST_COLS["eps"][0] + i
        return self.arena[:, a:a + 1]

    def par(self, name, m=0):
        a = PAR0 + PAR[name][0] + m
        return self.arena[:, a:a + 1]

    def pars(self, name):
        a, n = PAR[name]
        return self.arena[:, PAR0 + a:PAR0 + a + n]

    def ada(self, layer, what, m):
        a = ADA0 + 64 * layer + 8 * what + m
        return self.arena[:, a:a + 1]

    def slab(self, *loads):
        n = len(self.slabs)
        self.arrivals[n % SLOTS] += 16 * len(loads)
        self.slabs.append((loads, self.arrivals[n % SLOTS]))
        return n

    def slot(self, n, *dims):
        return self.view(RING0 + (n % SLOTS) * SLOT, *dims)

    def arrived(self, eng, n):
        eng.wait_ge(self.slab_in[n % SLOTS], self.slabs[n][1])

    def load_slab(self, sp, n):
        if n >= SLOTS:
            sp.wait_ge(self.slab_out[n % SLOTS], n // SLOTS)
        for (off, dims), src in self.slabs[n][0]:
            sp.dma_start(self.view(RING0 + (n % SLOTS) * SLOT + off, *dims), src)\
                .then_inc(self.slab_in[n % SLOTS], 16)

    def used(self, ins, n):
        ins.then_inc(self.slab_out[n % SLOTS], 1)


CONST0 = 0
PAR0 = CONST0 + NCONST
ADA0 = PAR0 + NPAR
X0 = ADA0 + 256
H0 = X0 + KD * T
HC0 = H0 + KD * T
RING0 = HC0 + KD * TC
W0 = RING0 + SLOTS * SLOT
ARENA = 53200
WORK = ARENA - W0


def k_slab(w, a, b):
    return ((0, (KD, b - a)), w[:, a:b].rearrange("(k p) n -> p k n", p=P))


def row_slab(w, a, b):
    return ((0, ((b - a) // P, D)), w[a:b, :].rearrange("(k p) n -> p k n", p=P))


class Stage:

    def __init__(self, core):
        self.c = core

    def tensor(self, pe): pass
    def scalar(self, act): pass
    def vector(self, dve): pass
    def gpsimd(self, pool): pass
    def sync(self, sp): pass


class Load(Stage):

    def __init__(self, core):
        super().__init__(core)
        self.loaded, _ = core.shared("loaded", 64)

    def scalar(self, act):
        c, d = self.c, self.c.d
        act.dma_start(c.view(CONST0, NCONST), d["const"]).then_inc(self.loaded, 16)
        act.dma_start(c.view(PAR0, NPAR), d["vectors"]).then_inc(self.loaded, 16)
        act.dma_start(c.x, d["x_t"].rearrange("(k p) t -> p k t", p=P)).then_inc(self.loaded, 16)
        act.dma_start(c.hc, d["ctx_t"].rearrange("(k p) t -> p k t", p=P)).then_inc(self.loaded, 16)
        act.wait_ge(self.loaded, 64)
        a, _ = PAR["c"]
        v = c.view(PAR0 + a, 32)
        act.activation(v, v, ACT.Silu)


class LoadContext(Stage):

    def __init__(self, core):
        super().__init__(core)
        self.loaded, self.base = core.shared("loaded", 16)

    def scalar(self, act):
        act.dma_start(self.c.hc, self.c.d["ctx2_t"].rearrange("(k p) t -> p k t", p=P)).then_inc(self.loaded, 16)
        act.wait_ge(self.loaded, self.base + 16)


class Modulation(Stage):

    def __init__(self, core, layer, w, bias, cond, cond_ctx):
        super().__init__(core)
        self.layer, self.bias, self.cond, self.cond_ctx = layer, bias, cond, cond_ctx
        self.n = [core.slab(k_slab(w, 512 * s, 512 * s + 512)) for s in range(12)]
        self.jobs = [(s, cond, 4 * s) for s in range(12)]
        if cond_ctx:
            self.jobs = [x for s in range(12) for x in
                         ([(s, cond, 4 * s)] + ([(s, cond_ctx, 48 + 4 * s)] if s < 4 else []))]
        self.summed, self.base = core.shared("mod_summed", len(self.jobs))
        self.turned, _ = core.shared("mod_turned", len(self.jobs))

    def vector(self, dve):
        c = self.c
        for q, (s, cond, col) in enumerate(self.jobs):
            acc = c.view(W0 + 512 * (q % 2), 512)
            w = c.slot(self.n[s], KD, 512)
            if q >= 2:
                dve.wait_ge(self.turned, self.base + q - 1)
            c.arrived(dve, self.n[s])
            ins = dve.tensor_scalar(acc, w[:, 0, :], c.par(cond, 0), None, ALU.mult)
            for k in range(1, KD):
                dve.drain()
                ins = dve.scalar_tensor_tensor(out=acc, in0=w[:, k, :], scalar=c.par(cond, k), in1=acc,
                                               op0=ALU.mult, op1=ALU.add)
            ins.then_inc(self.summed, 1)
            if q + 1 == len(self.jobs) or self.jobs[q + 1][0] != s:
                c.used(dve.drain(), self.n[s])
        dve.wait_ge(self.turned, self.base + len(self.jobs))
        n = 64 if self.cond_ctx else 48
        a = ADA0 + 64 * self.layer
        out = c.view(a, 64)
        dve.tensor_tensor(out[:, 0:48], c.ps[:, 0, 0:48], c.pars(self.bias), ALU.add)
        if n == 64:
            dve.tensor_tensor(out[:, 48:64], c.ps[:, 0, 48:64], c.pars(self.bias)[:, 0:16], ALU.add)
        dve.drain()
        for what in (1, 4) + ((7,) if n == 64 else ()):
            v = out[:, 8 * what:8 * what + 8]
            dve.tensor_scalar(v, v, 1.0, None, ALU.add)

    def tensor(self, pe):
        c = self.c
        for q, (s, cond, col) in enumerate(self.jobs):
            pe.wait_ge(self.summed, self.base + q + 1)
            for j in range(4):
                ins = pe.matmul(c.ps[:, 0, col + j:col + j + 1], c.view(W0 + 512 * (q % 2) + 128 * j, P),
                                c.const("ones")[:, 0:1], start=True, stop=True)
            ins.then_inc(self.turned, 1)


class Gains(Stage):

    def __init__(self, core, layer, gain, what):
        super().__init__(core)
        self.args = layer, gain, what

    def vector(self, dve):
        layer, gain, what = self.args
        v = self.c.view(ADA0 + 64 * layer + 8 * what, 8)
        dve.tensor_tensor(v, v, self.c.pars(gain), ALU.mult)


class Norm(Stage):
    made = 0
    sems = None

    def __init__(self, core, src, dst, tokens, centre, scale, shift, scratch=None):
        super().__init__(core)
        self.scratch = W0 if scratch is None else scratch
        self.src, self.dst, self.t, self.centre = src, dst, tokens, centre
        self.scale, self.shift = scale, shift
        self.i, core.norms = core.norms, core.norms + 1
        if self.i == 0:
            core.norm_sems = {n: core.sem("norm_" + n) for n in
                              ("mean", "centred", "squared", "var", "std", "scaled")}
        self.s = core.norm_sems
        if centre:
            self.ic, core.centred = core.centred, core.centred + 1

    def tensor(self, pe):
        c, s, t = self.c, self.s, self.t
        if self.centre:
            for k in range(KD):
                ins = pe.matmul(c.ps[:, 0, 0:t], c.const("one_over_d"), self.src[:, k, :],
                                start=(k == 0), stop=(k == KD - 1))
            ins.then_inc(s["mean"], 1)
        for k in range(KD):
            pe.wait_ge(s["squared"], KD * self.i + k + 1)
            ins = pe.matmul(c.ps[:, 1, 0:t], c.const("one_over_d"), c.view(self.scratch + 512 * k, t),
                            start=(k == 0), stop=(k == KD - 1))
        ins.then_inc(s["var"], 1)

    def vector(self, dve):
        c, s, t = self.c, self.s, self.t
        if self.centre:
            dve.wait_ge(s["mean"], self.ic + 1)
            for k in range(KD):
                dve.tensor_tensor(self.dst[:, k, :], self.src[:, k, :], c.ps[:, 0, 0:t], ALU.subtract)\
                    .then_inc(s["centred"], 1)
        rstd = c.view(self.scratch + 512 * KD, t)
        dve.wait_ge(s["std"], self.i + 1)
        dve.reciprocal(rstd, rstd)
        dve.drain()
        src = self.dst if self.centre else self.src
        for k in range(KD):
            dve.tensor_tensor(self.dst[:, k, :], src[:, k, :], rstd, ALU.mult).then_inc(s["scaled"], 1)

    def scalar(self, act):
        c, s, t = self.c, self.s, self.t
        src = self.dst if self.centre else self.src
        for k in range(KD):
            if self.centre:
                act.wait_ge(s["centred"], KD * self.ic + k + 1)
            act.activation(c.view(self.scratch + 512 * k, t), src[:, k, :], ACT.Square).then_inc(s["squared"], 1)
        act.wait_ge(s["var"], self.i + 1)
        act.activation(c.view(self.scratch + 512 * KD, t), c.ps[:, 1, 0:t], ACT.Sqrt,
                       bias=c.eps(0 if self.centre else 1)).then_inc(s["std"], 1)
        for k in range(KD):
            act.wait_ge(s["scaled"], KD * self.i + k + 1)
            v = self.dst[:, k, :]
            if self.shift is None:
                act.activation(v, v, ACT.Copy, scale=self.scale(k))
            else:
                act.activation(v, v, ACT.Identity, scale=self.scale(k), bias=self.shift(k))


class Project(Stage):
    made = 0

    def __init__(self, core, w, src, gate, keep):
        super().__init__(core)
        self.src, self.gate, self.keep = src, gate, keep
        self.n = [core.slab(k_slab(w, 512 * s, 512 * s + 512)) for s in range(2)]
        self.full, self.base = core.shared("tile_full", KD)

    def tensor(self, pe):
        c = self.c
        for m in range(KD):
            n = self.n[m // 4]
            if m % 4 == 0:
                c.arrived(pe, n)
            w = c.slot(n, KD, 512)
            for k in range(KD):
                ins = pe.matmul(c.ps[:, m, :], w[:, k, P * (m % 4):P * (m % 4) + P], self.src[:, k, :],
                                start=(k == 0), stop=(k == KD - 1))
            ins.then_inc(self.full, 1)
            if m % 4 == 3:
                c.used(pe.drain(), n)

    def vector(self, dve):
        c = self.c
        if self.keep != 1.0:
            dve.tensor_scalar(c.x, c.x, self.keep, None, ALU.mult)
            dve.drain()
        for m in range(KD):
            dve.wait_ge(self.full, self.base + m + 1)
            dve.scalar_tensor_tensor(out=c.x[:, m, :], in0=c.ps[:, m, :], scalar=self.gate(m),
                                     in1=c.x[:, m, :], op0=ALU.mult, op1=ALU.add)



A_Q = W0
A_K = A_Q + HEADS * T
A_V = A_K + HEADS * KEYS
A_F = A_V + NTA * 512
A_ROPE = A_F + 4 * T
A_RAW = A_ROPE + 2 * T
A_TMP = A_RAW + 2 * T
A_P = A_TMP + 2 * T
A_PT = A_P + 2 * KEYS
A_SMALL = A_PT + NTA * T
A_END = A_SMALL + 64
A_MIX = H0


class AttentionIn(Stage):

    def __init__(self, core):
        super().__init__(core)
        w = core.d["da_w_in"][0]
        self.n = [core.slab(k_slab(w, 512 * s, 512 * s + 512)) for s in range(4)]
        self.rope_in, self.swapped, self.table = core.sem("rope_in"), core.sem("rope_swapped"), core.sem("rope_table")
        self.tiles = [("q", m) for m in range(4)] + [("k", m) for m in range(4)] + [("kc", m) for m in range(4)]
        self.tiles += [("v", t) for t in range(NTA)] + [("f", m) for m in range(4)]
        self.full, self.base = core.shared("tile_full", len(self.tiles))
        self.free, self.freed = core.shared("tile_used", len(self.tiles))

    def tensor(self, pe):
        c = self.c

        def swap(r):
            pe.wait_ge(self.rope_in, r + 1)
            pe.matmul(c.ps[:, 4 + r % 2, :], c.const("swap"), c.view(A_RAW + 512 * (r % 2), T),
                      start=True, stop=True).then_inc(self.swapped, 1)

        for i, (kind, m) in enumerate(self.tiles):
            n = self.n["q k v f".split().index(kind[0])]
            c.arrived(pe, n)
            w = c.slot(n, KD, 512)
            if i >= 4:
                pe.wait_ge(self.free, self.freed + i - 3)
            for k in range(KD):
                if kind == "v":
                    src = c.hc[:, k, P * m:P * m + P] if m < NTC else c.h[:, k, P * (m - NTC):P * (m - NTC) + P]
                    out, lhs, rhs = c.ps[:, i % 4, :], src, w[:, k, :]
                else:
                    rhs = c.hc[:, k, :] if kind == "kc" else c.h[:, k, :]
                    out, lhs = c.ps[:, i % 4, 0:rhs.shape[1]], w[:, k, P * m:P * m + P]
                ins = pe.matmul(out, lhs, rhs, start=(k == 0), stop=(k == KD - 1))
            ins.then_inc(self.full, 1)
            if (kind, m) in (("q", 3), ("kc", 3), ("v", NTA - 1), ("f", 3)):
                c.used(pe.drain(), n)
            if 1 <= i <= 8:
                swap(i - 1)

    def scalar(self, act):
        act.dma_start(self.c.view(A_ROPE, 2 * T), self.c.d["rope"]).then_inc(self.table, 16)

    def vector(self, dve):
        c = self.c
        cos, sin = c.view(A_ROPE, T), c.view(A_ROPE + T, T)
        dve.wait_ge(self.table, 16)

        def rotate(r):
            m = r % 4
            dst = c.view(A_Q + T * m, T) if r < 4 else c.view(A_K + KEYS * m + TC, T)
            tmp = c.view(A_TMP + 512 * (r % 2), T)
            dve.wait_ge(self.swapped, r + 1)
            dve.tensor_tensor(tmp, c.ps[:, 4 + r % 2, :], sin, ALU.mult)
            dve.tensor_tensor(dst, c.view(A_RAW + 512 * (r % 2), T), cos, ALU.mult)
            dve.drain()
            dve.tensor_tensor(dst, dst, tmp, ALU.add)

        for i, (kind, m) in enumerate(self.tiles):
            dve.wait_ge(self.full, self.base + i + 1)
            ps = c.ps[:, i % 4, :]
            if kind in ("q", "k"):
                if i >= 2:
                    dve.drain()
                dve.tensor_copy(c.view(A_RAW + 512 * (i % 2), T), ps).then_inc(self.free, 1)
                dve.drain().then_inc(self.rope_in, 1)
            elif kind == "kc":
                dve.tensor_copy(c.view(A_K + KEYS * m, TC), ps[:, 0:TC]).then_inc(self.free, 1)
            elif kind == "v":
                dve.tensor_copy(c.view(A_V + 512 * m, 512), ps).then_inc(self.free, 1)
            else:
                dve.tensor_copy(c.view(A_F + T * m, T), ps).then_inc(self.free, 1)
            if 1 <= i <= 8:
                rotate(i - 1)


class Attention(Stage):

    def __init__(self, core):
        super().__init__(core)
        (self.lam_in, self.lam_prod, self.lam_sum, self.lam_exp, self.scores, self.negmax, self.exp,
         self.probs, self.turned, self.copied, self.out, self.square, self.ms, self.std, self.out_used) = (
            core.sem("att_" + n) for n in ("lam_in", "lam_prod", "lam_sum", "lam_exp", "scores", "negmax",
                "exp", "probs", "turned", "copied", "out", "square", "ms", "std", "out_used"))
        self.lam4 = core.view(A_SMALL, 4)
        self.lamp = core.view(A_SMALL + 4, 2)
        self.lame = core.view(A_SMALL + 6, 2)
        self.lamc = core.view(A_SMALL + 8, 1)
        self.mx = core.view(A_SMALL + 10, 2)
        self.nm = core.view(A_SMALL + 12, 2)
        self.sm = core.view(A_SMALL + 14, 2)
        self.gain = core.view(A_SMALL + 16, 1)

    def tensor(self, pe):
        c = self.c
        pe.wait_ge(self.lam_prod, 1)
        pe.matmul(c.ps[:, 7, 0:2], c.const("ones")[0:64, :], self.lamp[0:64, :], start=True, stop=True)\
            .then_inc(self.lam_sum, 1)
        pe.wait_ge(self.lam_exp, 1)
        for h in range(HEADS):
            for t in range(NT):
                i = NT * h + t
                if i >= 1:
                    pe.wait_ge(self.exp, i)
                for half in range(2):
                    q = c.view(A_Q + T * h + P * t, P)[64 * half:64 * half + 64, :]
                    k = c.view(A_K + KEYS * h, KEYS)[64 * half:64 * half + 64, :]
                    pe.matmul(c.ps[:, 2 * half, 0:512], q, k[:, 0:512], start=True, stop=True)
                    ins = pe.matmul(c.ps[:, 2 * half + 1, 0:KEYS - 512], q, k[:, 512:KEYS], start=True, stop=True)
                ins.then_inc(self.scores, 1)
                pe.wait_ge(self.probs, i + 1)
                if i >= 1:
                    pe.wait_ge(self.copied, i)
                for kt in range(NTA):
                    ins = pe.transpose(c.ps[:, 4 + kt // 4, P * (kt % 4):P * (kt % 4) + P],
                                       c.view(A_P + P * kt, P), c.const("ident"))
                ins.then_inc(self.turned, 1)
            pe.wait_ge(self.copied, NT * (h + 1))
            if h >= 1:
                pe.wait_ge(self.out_used, h)
            for kt in range(NTA):
                ins = pe.matmul(c.ps[:, 6, :], c.view(A_V + 512 * kt + P * h, P), c.view(A_PT + T * kt, T),
                                start=(kt == 0), stop=(kt == NTA - 1))
            ins.then_inc(self.out, 1)
            pe.wait_ge(self.square, h + 1)
            pe.matmul(c.ps[:, 7, :], c.const("one_over_p"), c.view(A_TMP, T), start=True, stop=True)\
                .then_inc(self.ms, 1)

    def scalar(self, act):
        c = self.c
        for i, n in enumerate(("da_lam_q1", "da_lam_k1", "da_lam_q2", "da_lam_k2")):
            act.dma_start(self.lam4[0:64, i:i + 1], c.d[n].rearrange("a (p b) -> (a p) b", b=1)).then_inc(self.lam_in, 16)
        act.wait_ge(self.lam_sum, 1)
        act.activation(self.lame, c.ps[:, 7, 0:2], ACT.Exp).then_inc(self.lam_exp, 1)
        for h in range(HEADS):
            for t in range(NT):
                i = NT * h + t
                act.wait_ge(self.negmax, i + 1)
                for half in range(2):
                    ins = act.activation(c.view(A_P + KEYS * half, KEYS), c.score(half), ACT.Exp,
                                         bias=self.nm[:, half:half + 1], scale=64 ** -0.5,
                                         accum_out=self.sm[:, half:half + 1])
                act.drain().then_inc(self.exp, 1)
                act.wait_ge(self.turned, i + 1)
                for kt in range(NTA):
                    act.activation(c.view(A_PT + T * kt + P * t, P),
                                   c.ps[:, 4 + kt // 4, P * (kt % 4):P * (kt % 4) + P], ACT.Copy)
                act.drain().then_inc(self.copied, 1)
            act.wait_ge(self.out, h + 1)
            act.activation(c.view(A_TMP, T), c.ps[:, 6, :], ACT.Square).then_inc(self.square, 1)
            act.wait_ge(self.ms, h + 1)
            act.activation(c.view(A_TMP + T, T), c.ps[:, 7, :], ACT.Sqrt, bias=c.eps(0)).then_inc(self.std, 1)

    def vector(self, dve):
        c = self.c
        dve.wait_ge(self.lam_in, 64)
        l4 = self.lam4[0:64, :].rearrange("p (a b) -> p a b", b=2)
        dve.tensor_tensor(self.lamp[0:64, :], l4[:, :, 0], l4[:, :, 1], ALU.mult).then_inc(self.lam_prod, 1)
        dve.tensor_scalar(self.gain, c.par("da_subln_g"), 1.0 - LAM_INIT, None, ALU.mult)
        dve.wait_ge(self.lam_exp, 1)
        dve.tensor_tensor(self.lamc, self.lame[:, 0:1], self.lame[:, 1:2], ALU.subtract)
        dve.drain()
        dve.tensor_scalar(self.lamc, self.lamc, LAM_INIT, None, ALU.add)
        dve.drain()
        for h in range(HEADS):
            for t in range(NT):
                i = NT * h + t
                dve.wait_ge(self.scores, i + 1)
                for half in range(2):
                    dve.tensor_reduce(self.mx[:, half:half + 1], c.score(half), AX.X, ALU.max)
                dve.drain()
                dve.tensor_scalar(self.nm, self.mx, -(64 ** -0.5), None, ALU.mult).then_inc(self.negmax, 1)
                dve.wait_ge(self.exp, i + 1)
                dve.reciprocal(self.sm, self.sm)
                dve.drain()
                dve.tensor_tensor(self.sm[:, 1:2], self.sm[:, 1:2], self.lamc, ALU.mult)
                dve.drain()
                e1, e2 = c.view(A_P, KEYS), c.view(A_P + KEYS, KEYS)
                dve.tensor_scalar(e2, e2, self.sm[:, 1:2], None, ALU.mult)
                dve.drain()
                dve.scalar_tensor_tensor(out=e1, in0=e1, scalar=self.sm[:, 0:1], in1=e2,
                                         op0=ALU.mult, op1=ALU.subtract)
                dve.drain().then_inc(self.probs, 1)
            rstd = c.view(A_TMP + T, T)
            dve.wait_ge(self.std, h + 1)
            dve.reciprocal(rstd, rstd)
            dve.drain()
            dst = c.view(A_MIX + T * h, T)
            dve.tensor_tensor(dst, c.ps[:, 6, :], rstd, ALU.mult)
            dve.drain()
            dve.tensor_scalar(dst, dst, self.gain, None, ALU.mult).then_inc(self.out_used, 1)


class FourierMix(Stage):
    CS = A_P
    AB = A_PT - 0
    L = 0

    def __init__(self, core):
        super().__init__(core)
        self.table, self.full, self.free, self.done = (core.sem("fm_" + n) for n in ("table", "full", "free", "done"))
        self.cs = core.view(A_Q, 256)
        self.ab = core.view(A_K, NT, 4, 256)
        self.l = core.view(A_ROPE, 2, NT, T)

    def scalar(self, act):
        act.dma_start(self.cs, self.c.d["fm_cs"]).then_inc(self.table, 16)
        act.dma_start(self.l, self.c.d["fm_l"].rearrange("p (a b t) -> p a b t", a=2, b=NT)).then_inc(self.table, 16)

    def tensor(self, pe):
        c = self.c
        pe.wait_ge(self.table, 32)
        for i in range(16):
            g, t = i // NT, i % NT
            if i >= 4:
                pe.wait_ge(self.free, i - 3)
            pe.matmul(c.ps[:, i % 4, 0:256], c.view(A_F + T * g + P * t, P), self.cs, start=True, stop=True)\
                .then_inc(self.full, 1)
        pe.wait_ge(self.free, 16)
        for g in range(4):
            for t in range(NT):
                for part in range(2):
                    ins = pe.matmul(c.ps[:, 4 + g, :], self.ab[:, t, g, P * part:P * part + P], self.l[:, part, t, :],
                                    start=(t + part == 0), stop=(t == NT - 1 and part == 1))
            ins.then_inc(self.done, 1)

    def vector(self, dve):
        c = self.c
        for i in range(16):
            g, t = i // NT, i % NT
            dve.wait_ge(self.full, i + 1)
            dve.tensor_copy(self.ab[:, t, g, :], c.ps[:, i % 4, 0:256]).then_inc(self.free, 1)
        for g in range(4):
            dve.wait_ge(self.done, g + 1)
            dve.tensor_copy(c.view(A_MIX + T * (4 + g), T), c.ps[:, 4 + g, :])



F_ACT = W0
F_BUF = F_ACT + NF * T


def conv3(dve, out, u, w0, w2, n):
    dve.scalar_tensor_tensor(out=out[:, 1:n], in0=u[:, 0:n - 1], scalar=w0, in1=out[:, 1:n],
                             op0=ALU.mult, op1=ALU.add)
    dve.drain()
    return dve.scalar_tensor_tensor(out=out[:, 0:n - 1], in0=u[:, 1:n], scalar=w2, in1=out[:, 0:n - 1],
                                    op0=ALU.mult, op1=ALU.add)


class FfnIn(Stage):

    def __init__(self, core, i):
        super().__init__(core)
        self.i = i
        w = core.d["ffn_w_in"][i]
        self.n = []
        for s in range(NF // 2):
            self.n.append(core.slab(*[
                ((half * KD * 256, (KD, 256)),
                 w[:, FFN * half + 256 * s:FFN * half + 256 * s + 256].rearrange("(k p) n -> p k n", p=P))
                for half in range(2)]))
        self.tiles = [(s, q) for s in range(NF // 2) for q in range(4)]
        self.full, self.full0 = core.shared("tile_full", 2 * NF)
        self.centre, self.centre0 = core.shared("tile_centre", 2 * NF)
        self.conv, self.conv0 = core.shared("tile_used", 2 * NF)
        self.gelu, self.gelu0 = core.shared("gelu", NF)

    def tensor(self, pe):
        c = self.c
        for j, (s, q) in enumerate(self.tiles):
            n = self.n[s]
            if q == 0:
                c.arrived(pe, n)
            w = c.slot(n, 2, KD, 256)
            if j >= 8:
                pe.wait_ge(self.conv, self.conv0 + j - 7)
            for k in range(KD):
                ins = pe.matmul(c.ps[:, j % 8, :], w[:, q // 2, k, P * (q % 2):P * (q % 2) + P], c.h[:, k, :],
                                start=(k == 0), stop=(k == KD - 1))
            ins.then_inc(self.full, 1)
            if q == 3:
                c.used(pe.drain(), n)

    def scalar(self, act):
        c, i = self.c, self.i
        for j, (s, q) in enumerate(self.tiles):
            m = 2 * s + q % 2 + NF * (q // 2)
            act.wait_ge(self.full, self.full0 + j + 1)
            if j >= 4:
                act.wait_ge(self.conv, self.conv0 + j - 3)
            if s and q < 2:
                act.wait_ge(self.gelu, self.gelu0 + 2 * s - 1 + q)
            buf = c.view(F_BUF + T * q, T)
            act.activation(buf, c.ps[:, j % 8, :], ACT.Identity, scale=c.par(f"ffn_conv_w{i}1", m),
                           bias=c.par(f"ffn_conv_b{i}", m)).then_inc(self.centre, 1)
            if q >= 2:
                a = 4 * s + q - 2
                act.wait_ge(self.conv, self.conv0 + a + 1)
                act.activation(c.view(F_ACT + T * (2 * s + q - 2), T), c.view(F_BUF + T * (q - 2), T), ACT.Gelu)\
                    .then_inc(self.gelu, 1)

    def vector(self, dve):
        c, i = self.c, self.i
        for j, (s, q) in enumerate(self.tiles):
            m = 2 * s + q % 2 + NF * (q // 2)
            dve.wait_ge(self.centre, self.centre0 + j + 1)
            buf = c.view(F_BUF + T * q, T)
            ins = conv3(dve, buf, c.ps[:, j % 8, :], c.par(f"ffn_conv_w{i}0", m), c.par(f"ffn_conv_w{i}2", m), T)
            if q >= 2:
                g = 2 * s + q - 2
                dve.wait_ge(self.gelu, self.gelu0 + g + 1)
                dve.drain()
                dst = c.view(F_ACT + T * g, T)
                ins = dve.tensor_tensor(dst, dst, buf, ALU.mult)
            ins.then_inc(self.conv, 1)


class FfnOut(Stage):

    def __init__(self, core, i, gate):
        super().__init__(core)
        self.gate = gate
        w = core.d["ffn_w_out"][i]
        self.n = [core.slab(row_slab(w, 512 * s, min(512 * s + 512, FFN))) for s in range(6)]
        self.full, self.base = core.shared("tile_full", KD)

    def tensor(self, pe):
        c = self.c
        for s, n in enumerate(self.n):
            rows = min(4, NF - 4 * s)
            w = c.slot(n, 4, D)
            c.arrived(pe, n)
            for k in range(rows):
                kt = 4 * s + k
                for m in range(KD):
                    ins = pe.matmul(c.ps[:, m, :], w[:, k, P * m:P * m + P], c.view(F_ACT + T * kt, T),
                                    start=(kt == 0), stop=(kt == NF - 1))
                    if kt == NF - 1:
                        ins.then_inc(self.full, 1)
            c.used(pe.drain(), n)

    def vector(self, dve):
        c = self.c
        dve.tensor_scalar(c.x, c.x, ALPHA, None, ALU.mult)
        dve.drain()
        for m in range(KD):
            dve.wait_ge(self.full, self.base + m + 1)
            dve.scalar_tensor_tensor(out=c.x[:, m, :], in0=c.ps[:, m, :], scalar=self.gate(m),
                                     in1=c.x[:, m, :], op0=ALU.mult, op1=ALU.add)



Y_K = W0
Y_TAB = Y_K + 2 * NT * D
Y_HF = Y_TAB + 2 * NT * T
Y_HB = Y_HF + NT * D
Y_VT = H0
Y_BUF = Y_HB + NT * D
Y_HID = H0
TWO_PI_HI = 6.28125
TWO_PI_LO = 2 * math.pi - 6.28125
ROUND = 1.5 * 2.0 ** 23


class HyenaFilter(Stage):

    def __init__(self, core):
        super().__init__(core)
        (self.inputs, self.tables, self.lin, self.reduced, self.sine, self.raw, self.windowed,
         self.absolute, self.summed, self.sumdiff, self.spec, self.spec_out) = (
            core.sem("hyf_" + n) for n in ("inputs", "tables", "lin", "reduced", "sine", "raw", "windowed",
                "absolute", "summed", "sumdiff", "spec", "spec_out"))
        o = Y_HID
        self.z = core.view(o, T); o += T
        self.w1 = core.view(o, HID); o += HID
        self.w23 = core.view(o, 2, HID); o += 2 * HID
        self.vec = core.view(o, 4); o += 4
        self.arg = core.view(o, T); o += T
        self.turns = core.view(o, T); o += T
        self.hid = core.view(o, T); o += T
        self.w4 = core.view(o, 2 * D); o += 2 * D
        self.decay = core.view(Y_K, NT, D)
        self.absum = core.view(Y_K + NT * D, NT, D)
        self.hf, self.hb = core.view(Y_HF, NT, D), core.view(Y_HB, NT, D)
        self.tab = core.view(Y_TAB, 2, NT, T)
        self.abs_b = core.view(o, D)
        core.hy_norm = core.view(ADA0 + 256 - 16, KD)
        self.k = core.view(Y_K, 2, NT, D)

    def scalar(self, act):
        c, d = self.c, self.c.d
        s = self.inputs
        act.dma_start(self.z[0:33, :], d["hy_z"]).then_inc(s, 16)
        act.dma_start(self.w1[0:33, :], d["hy_f_w1"][0]).then_inc(s, 16)
        act.dma_start(self.w23[0:HID, 0, :], d["hy_f_w2"][0]).then_inc(s, 16)
        act.dma_start(self.w23[0:HID, 1, :], d["hy_f_w3"][0]).then_inc(s, 16)
        act.dma_start(self.w4[0:HID, :], d["hy_f_w4"][0]).then_inc(s, 16)
        for i, n in enumerate(("hy_f_b1", "hy_f_b2", "hy_f_b3", "hy_f_freq")):
            act.dma_start(self.vec[0:HID, i:i + 1], d[n].rearrange("a (p b) -> (a p) b", b=1)).then_inc(s, 16)
        act.dma_start(self.decay, d["hy_decay"].rearrange("p (k n) -> p k n", k=NT)).then_inc(self.tables, 16)
        act.dma_start(self.tab, d["hy_fwd"].rearrange("p (a k n) -> p a k n", a=2, k=NT)).then_inc(self.tables, 16)
        for layer in range(3):
            act.wait_ge(self.reduced, layer + 1)
            act.activation(self.hid[0:HID, :], self.arg[0:HID, :], ACT.Sin).then_inc(self.sine, 1)
        for t in range(NT):
            act.wait_ge(self.windowed, 4 * (t + 1))
            act.activation(self.absum[:, t, :], self.hf[:, t, :], ACT.Abs)
            if t >= 1:
                act.wait_ge(self.summed, t)
            act.activation(self.abs_b, self.hb[:, t, :], ACT.Abs)
            act.drain().then_inc(self.absolute, 1)

    def vector(self, dve):
        c = self.c
        freq = self.vec[0:HID, 3:4]
        arg, turns = self.arg[0:HID, :], self.turns[0:HID, :]
        dve.wait_ge(self.inputs, 16 * 9)
        for layer in range(3):
            dve.wait_ge(self.lin, layer + 1)
            dve.tensor_scalar(arg, c.ps[0:HID, 0, :], self.vec[0:HID, layer:layer + 1], freq, ALU.add, ALU.mult)
            dve.drain()
            dve.tensor_scalar(turns, arg, 1.0 / (2 * math.pi), ROUND, ALU.mult, ALU.add)
            dve.drain()
            dve.tensor_scalar(turns, turns, -ROUND, None, ALU.add)
            dve.drain()
            dve.scalar_tensor_tensor(out=arg, in0=turns, scalar=-TWO_PI_HI, in1=arg, op0=ALU.mult, op1=ALU.add)
            dve.drain()
            dve.scalar_tensor_tensor(out=arg, in0=turns, scalar=-TWO_PI_LO, in1=arg, op0=ALU.mult, op1=ALU.add)
            dve.drain()
            dve.tensor_scalar(arg, arg, math.pi, -math.pi, ALU.min, ALU.max).then_inc(self.reduced, 1)
        dve.wait_ge(self.tables, 32)
        for t in range(NT):
            for q in range(4):
                i = 4 * t + q
                dst = (self.hf if q < 2 else self.hb)[:, t, 512 * (q % 2):512 * (q % 2) + 512]
                dve.wait_ge(self.raw, i + 1)
                ins = dve.tensor_tensor(dst, c.ps[:, i % 4, :], self.decay[:, t, 512 * (q % 2):512 * (q % 2) + 512],
                                        ALU.mult)
                if t == 0 and q >= 2:
                    dve.drain()
                    ins = dve.memset(dst[0:1, :], 0.0)
                ins.then_inc(self.windowed, 1)
        for t in range(NT):
            dve.wait_ge(self.absolute, t + 1)
            dve.tensor_tensor(self.absum[:, t, :], self.absum[:, t, :], self.abs_b, ALU.add)\
                .then_inc(self.summed, 1)
            s = c.view(Y_HID, D)
            dve.drain()
            dve.tensor_tensor(s, self.hf[:, t, :], self.hb[:, t, :], ALU.add)
            dve.tensor_tensor(self.hb[:, t, :], self.hb[:, t, :], self.hf[:, t, :], ALU.subtract)
            dve.drain()
            dve.tensor_copy(self.hf[:, t, :], s).then_inc(self.sumdiff, 1)
        dve.wait_ge(self.spec, 1)
        dve.reciprocal(c.hy_norm, c.ps[:, 7, 0:KD])
        for j in range(16):
            part, f, half = j // 8, j // 2 % 4, j % 2
            dve.wait_ge(self.spec, j + 2)
            dve.tensor_copy(self.k[:, part, f, 512 * half:512 * half + 512], c.ps[:, j % 4, :]).then_inc(self.spec_out, 1)

    def tensor(self, pe):
        c = self.c
        pe.wait_ge(self.inputs, 16 * 9)
        pe.matmul(c.ps[0:HID, 0, :], self.w1[0:33, :], self.z[0:33, :], start=True, stop=True).then_inc(self.lin, 1)
        for layer in range(2):
            pe.wait_ge(self.sine, layer + 1)
            pe.matmul(c.ps[0:HID, 0, :], self.w23[0:HID, layer, :], self.hid[0:HID, :], start=True, stop=True)\
                .then_inc(self.lin, 1)
        pe.wait_ge(self.sine, 3)
        for i in range(16):
            t, q = i // 4, i % 4
            if i >= 4:
                pe.wait_ge(self.windowed, i - 3)
            pe.matmul(c.ps[:, i % 4, :], self.hid[0:HID, P * t:P * t + P], self.w4[0:HID, 512 * q:512 * q + 512],
                      start=True, stop=True).then_inc(self.raw, 1)
        pe.wait_ge(self.summed, NT)
        for m in range(KD):
            for t in range(NT):
                ins = pe.matmul(c.ps[:, 7, m:m + 1], self.absum[:, t, P * m:P * m + P], c.const("ones")[:, 0:1],
                                start=(t == 0), stop=(t == NT - 1))
        ins.then_inc(self.spec, 1)
        pe.wait_ge(self.sumdiff, NT)
        for j in range(16):
            part, f, half = j // 8, j // 2 % 4, j % 2
            if j >= 4:
                pe.wait_ge(self.spec_out, j - 3)
            src = self.hf if part == 0 else self.hb
            for t in range(NT):
                ins = pe.matmul(c.ps[:, j % 4, :], self.tab[:, part, t, P * f:P * f + P],
                                src[:, t, 512 * half:512 * half + 512], start=(t == 0), stop=(t == NT - 1))
            ins.then_inc(self.spec, 1)


class HyenaIn(Stage):

    def __init__(self, core):
        super().__init__(core)
        w = core.d["hy_w_in"][0]
        self.order = [m for part in (1, 2, 0) for m in range(8 * part, 8 * part + 8)]
        self.n = [core.slab(k_slab(w, P * self.order[4 * s], P * self.order[4 * s] + 512)) for s in range(6)]
        self.full, self.full0 = core.shared("tile_full", 24)
        self.centre, self.centre0 = core.shared("tile_centre", 24)
        self.conv, self.conv0 = core.shared("tile_used", 24)

    def dst(self, j):
        c = self.c
        if j < 8:
            return c.view(Y_HB + T * j, T)
        if j < 16:
            return c.view(Y_BUF + T * (j % 2), T)
        return c.view(Y_HF + T * (j - 16), T)

    def tensor(self, pe):
        c = self.c
        for j, m in enumerate(self.order):
            n = self.n[j // 4]
            if j % 4 == 0:
                c.arrived(pe, n)
            w = c.slot(n, KD, 512)
            if j >= 8:
                pe.wait_ge(self.conv, self.conv0 + j - 7)
            for k in range(KD):
                ins = pe.matmul(c.ps[:, j % 8, :], w[:, k, P * (j % 4):P * (j % 4) + P], c.h[:, k, :],
                                start=(k == 0), stop=(k == KD - 1))
            ins.then_inc(self.full, 1)
            if j % 4 == 3:
                c.used(pe.drain(), n)

    def scalar(self, act):
        c = self.c
        for j, m in enumerate(self.order):
            act.wait_ge(self.full, self.full0 + j + 1)
            if 10 <= j < 16:
                act.wait_ge(self.conv, self.conv0 + j - 1)
            act.activation(self.dst(j), c.ps[:, j % 8, :], ACT.Identity, scale=c.par("hy_conv_w1", m),
                           bias=c.par("hy_conv_b", m)).then_inc(self.centre, 1)

    def vector(self, dve):
        c = self.c
        for j, m in enumerate(self.order):
            dve.wait_ge(self.centre, self.centre0 + j + 1)
            ins = conv3(dve, self.dst(j), c.ps[:, j % 8, :], c.par("hy_conv_w0", m), c.par("hy_conv_w2", m), T)
            if 8 <= j < 16:
                dve.drain()
                x1 = self.dst(j - 8)
                ins = dve.tensor_tensor(x1, x1, self.dst(j), ALU.mult)
            ins.then_inc(self.conv, 1)


class HyenaConv(Stage):

    def __init__(self, core):
        super().__init__(core)
        (self.table, self.turned, self.turned_out, self.spec, self.prod, self.y, self.y_out) = (
            core.sem("hyc_" + n) for n in ("table", "turned", "turned_out", "spec", "prod", "y", "y_out"))
        self.v, self.x0 = core.view(Y_HB, KD, T), core.view(Y_HF, KD, T)
        self.vt = core.view(Y_VT, NT, D)
        self.tab = core.view(Y_TAB, 2, NT, T)
        self.k = core.view(Y_K, 2, NT, D)
        core.mix = self.x0

    def scalar(self, act):
        act.wait_ge(self.prod, 8)
        act.dma_start(self.tab, self.c.d["hy_back"].rearrange("p (a k n) -> p a k n", a=2, k=NT)).then_inc(self.table, 16)

    def tensor(self, pe):
        c = self.c
        for i in range(8):
            t, half = i // 2, i % 2
            if i >= 4:
                pe.wait_ge(self.turned_out, i - 3)
            for m in range(4):
                ins = pe.transpose(c.ps[:, i % 4, P * m:P * m + P], self.v[:, 4 * half + m, P * t:P * t + P],
                                   c.const("ident"))
            ins.then_inc(self.turned, 1)
        pe.wait_ge(self.turned_out, 8)
        for i in range(8):
            f, half = i // 2, i % 2
            if i >= 2:
                pe.wait_ge(self.prod, i - 1)
            for part in range(2):
                for t in range(NT):
                    ins = pe.matmul(c.ps[:, 4 + 2 * (i % 2) + part, :], self.tab[:, part, t, P * f:P * f + P],
                                    self.vt[:, t, 512 * half:512 * half + 512], start=(t == 0), stop=(t == NT - 1))
            ins.then_inc(self.spec, 1)
        pe.wait_ge(self.table, 16)
        for m in range(KD):
            if m >= 4:
                pe.wait_ge(self.y_out, m - 3)
            for f in range(NT):
                for part in range(2):
                    ins = pe.matmul(c.ps[:, m % 4, :], self.k[:, part, f, P * m:P * m + P], self.tab[:, part, f, :],
                                    start=(f + part == 0), stop=(f == NT - 1 and part == 1))
            ins.then_inc(self.y, 1)

    def vector(self, dve):
        c = self.c
        for i in range(8):
            t, half = i // 2, i % 2
            dve.wait_ge(self.turned, i + 1)
            dve.tensor_copy(self.vt[:, t, 512 * half:512 * half + 512], c.ps[:, i % 4, :]).then_inc(self.turned_out, 1)
        t1, t2 = c.view(Y_BUF, T), c.view(Y_BUF + T, T)
        for i in range(8):
            f, half = i // 2, i % 2
            cols = slice(512 * half, 512 * half + 512)
            kre, kim = self.k[:, 0, f, cols], self.k[:, 1, f, cols]
            vre, vs = c.ps[:, 4 + 2 * (i % 2), :], c.ps[:, 5 + 2 * (i % 2), :]
            dve.wait_ge(self.spec, i + 1)
            dve.tensor_tensor(t1, kim, vs, ALU.mult)
            dve.tensor_tensor(t2, kim, vre, ALU.mult)
            dve.drain()
            dve.tensor_tensor(kim, kre, vs, ALU.mult)
            dve.tensor_tensor(kre, kre, vre, ALU.mult)
            dve.drain()
            dve.tensor_tensor(kre, kre, t1, ALU.add)
            dve.tensor_tensor(kim, kim, t2, ALU.subtract)
            dve.drain().then_inc(self.prod, 1)
        for m in range(KD):
            dve.wait_ge(self.y, m + 1)
            dve.tensor_scalar(t1, c.ps[:, m % 4, :], c.hy_norm[:, m:m + 1], None, ALU.mult)
            dve.drain()
            dve.scalar_tensor_tensor(out=t1, in0=self.v[:, m, :], scalar=c.par("hy_d", m), in1=t1,
                                     op0=ALU.mult, op1=ALU.add)
            dve.drain()
            dve.tensor_tensor(self.x0[:, m, :], self.x0[:, m, :], t1, ALU.mult).then_inc(self.y_out, 1)
            dve.drain()



B_U = W0
B_Y = B_U + KD * T


class ShortConv(Stage):

    def __init__(self, core):
        super().__init__(core)
        w = core.d["w_in_b_2"][0]
        self.order = [m for part in (1, 2, 0) for m in range(8 * part, 8 * part + 8)]
        self.n = [core.slab(k_slab(w, P * self.order[4 * s], P * self.order[4 * s] + 512)) for s in range(6)]
        self.full, self.full0 = core.shared("tile_full", 24)
        self.free, self.free0 = core.shared("tile_used", 24)

    def tensor(self, pe):
        c = self.c
        for j, m in enumerate(self.order):
            n = self.n[j // 4]
            if j % 4 == 0:
                c.arrived(pe, n)
            w = c.slot(n, KD, 512)
            if j >= 8:
                pe.wait_ge(self.free, self.free0 + j - 7)
            for k in range(KD):
                ins = pe.matmul(c.ps[:, j % 8, :], w[:, k, P * (j % 4):P * (j % 4) + P], c.h[:, k, :],
                                start=(k == 0), stop=(k == KD - 1))
            ins.then_inc(self.full, 1)
            if j % 4 == 3:
                c.used(pe.drain(), n)

    def vector(self, dve):
        c = self.c
        rows = T // GRID_W
        for j in range(24):
            m = j % 8
            ps = c.ps[:, j % 8, :]
            u, y = c.view(B_U + T * m, T), c.view(B_Y + T * m, T)
            dve.wait_ge(self.full, self.full0 + j + 1)
            if j < 8:
                dve.tensor_copy(u, ps).then_inc(self.free, 1)
                continue
            dve.drain()
            if j >= 16:
                dve.tensor_tensor(y, y, ps, ALU.mult).then_inc(self.free, 1)
                continue
            dve.tensor_tensor(u, u, ps, ALU.mult).then_inc(self.free, 1)
            dve.drain()
            dve.tensor_scalar(y, u, c.par("conv_b1", m), None, ALU.mult)
            for tap, name in ((-1, "conv_b0"), (1, "conv_b2")):
                dve.drain()
                if m < 4:
                    uv = u.rearrange("p (r g) -> p r g", r=rows)
                    yv = y.rearrange("p (r g) -> p r g", r=rows)
                    src = uv[:, :, 0:GRID_W - 1] if tap < 0 else uv[:, :, 1:GRID_W]
                    dst = yv[:, :, 1:GRID_W] if tap < 0 else yv[:, :, 0:GRID_W - 1]
                else:
                    src = u[:, 0:T - GRID_W] if tap < 0 else u[:, GRID_W:T]
                    dst = y[:, GRID_W:T] if tap < 0 else y[:, 0:T - GRID_W]
                dve.scalar_tensor_tensor(out=dst, in0=src, scalar=c.par(name, m), in1=dst,
                                         op0=ALU.mult, op1=ALU.add)



G_MASK = W0
G_GATE = G_MASK + 14 * P
G_G, G_BETA, G_GC = G_GATE, G_GATE + 96, G_GATE + 192
G_T1, G_T2 = G_GATE + 288, G_GATE + 384
G_ROW = G_GATE + 480
G_Z = G_GATE + 512
G_Q = G_Z + T
G_K = G_Q + T
G_V = G_K + KEYS
G_KT = G_V + KEYS
G_VT = G_KT + KEYS
G_COL = G_VT + KEYS
G_TAPS = G_COL + 60
G_S = G_COL + 72
G_O = G_S + 2 * 4 * P
G_LANE = G_O + T
L_T, L_A, L_KBG, L_M, L_L, L_TT = (KEYS * i for i in range(6))
L_QD, L_QK = 6 * KEYS, 6 * KEYS + T
LANE = 6 * KEYS + 2 * T
G_MIX = G_LANE + 2 * LANE
LEVELS = 7


class DeltaGates(Stage):

    def __init__(self, core):
        super().__init__(core)
        self.n = core.slab(k_slab(core.d["w_in_a_2"][0], 4 * D, 4 * D + 32))
        (self.rows, self.full, self.sigmoid, self.shifted, self.soft, self.gate, self.summed) = (
            core.sem("gate_" + n) for n in ("rows", "full", "sigmoid", "shifted", "soft", "gate", "summed"))
        v = core.view
        self.g, self.beta, self.gcum = v(G_G, NTA, 16), v(G_BETA, NTA, 16), v(G_GC, NTA, 16)
        self.t1, self.t2 = v(G_T1, NTA, 16), v(G_T2, NTA, 16)
        self.alog, self.dt = v(G_ROW, 16), v(G_ROW + 16, 16)

    def tensor(self, pe):
        c = self.c
        c.arrived(pe, self.n)
        w = c.slot(self.n, KD, 32)
        for t in range(NTA):
            for k in range(KD):
                src = c.hc[:, k, P * t:P * t + P] if t < NTC else c.h[:, k, P * (t - NTC):P * (t - NTC) + P]
                ins = pe.matmul(c.ps[:, 0, 32 * t:32 * t + 32], src, w[:, k, :], start=(k == 0), stop=(k == KD - 1))
        ins.then_inc(self.full, 1)
        c.used(pe.drain(), self.n)
        pe.wait_ge(self.gate, 1)
        pe.matmul(c.ps[:, 1, 0:96], c.const("cum_f"), c.view(G_G, 96), start=True, stop=True)
        pe.matmul(c.ps[:, 2, 0:96], c.const("cum_b"), c.view(G_G, 96), start=True, stop=True).then_inc(self.summed, 1)

    def scalar(self, act):
        c, d = self.c, self.c.d
        act.dma_start(self.alog, d["a_log_a_2"].rearrange("a b c -> (a b c)").partition_broadcast(P)).then_inc(self.rows, 16)
        act.dma_start(self.dt, d["dt_bias_a_2"].rearrange("a b c -> (a b c)").partition_broadcast(P)).then_inc(self.rows, 16)
        act.dma_start(c.view(G_MASK, 14 * P), d["masks"]).then_inc(self.rows, 16)
        act.wait_ge(self.rows, 48)
        act.activation(self.alog, self.alog, ACT.Exp)
        act.wait_ge(self.full, 1)
        ba = c.ps[:, 0, 0:32 * NTA].rearrange("p (t n) -> p t n", n=32)
        act.activation(self.beta, ba[:, :, 0:16], ACT.Sigmoid).then_inc(self.sigmoid, 1)
        act.wait_ge(self.shifted, 1)
        act.activation(self.t2, self.t1, ACT.Abs)
        act.drain()
        act.activation(self.t2, self.t2, ACT.Exp, scale=-1.0)
        act.drain()
        act.activation(self.t2, self.t2, ACT.Ln, bias=c.eps(2)).then_inc(self.soft, 1)

    def vector(self, dve):
        c = self.c

        def row(v):
            return v.unsqueeze(1).to_broadcast([P, NTA, 16])

        dve.wait_ge(self.rows, 48)
        dve.wait_ge(self.sigmoid, 1)
        ba = c.ps[:, 0, 0:32 * NTA].rearrange("p (t n) -> p t n", n=32)
        dve.tensor_tensor(self.t1, ba[:, :, 16:32], row(self.dt), ALU.add).then_inc(self.shifted, 1)
        dve.wait_ge(self.soft, 1)
        dve.scalar_tensor_tensor(out=self.t1, in0=self.t1, scalar=0.0, in1=self.t2, op0=ALU.max, op1=ALU.add)
        dve.drain()
        dve.tensor_tensor(self.t1, self.t1, row(self.alog), ALU.mult)
        dve.drain()
        dve.tensor_scalar(self.g, self.t1, -1.0, None, ALU.mult).then_inc(self.gate, 1)
        dve.wait_ge(self.summed, 1)
        for b in range(2):
            dve.tensor_copy(self.gcum[:, :, 8 * b:8 * b + 8],
                            c.ps[:, 1 + b, 0:96].rearrange("p (t n) -> p t n", n=16)[:, :, 8 * b:8 * b + 8])


class DeltaHeads(Stage):
    PER = {"slab": 64, "slab_free": 1, "full": 6, "centre": 5, "conv": 5, "silu": 5, "square": 3, "sumsq": 3,
           "std": 3, "unit": 2, "turned": 2, "turned_out": 2, "cols": 1, "rows": 2, "grown": 2, "kb": 2, "darg": 2,
           "dexp": 2, "kk": 2, "lt": 2, "kdarg": 2, "mt": 14, "a": 14, "a_out": 12, "x": 12, "upd": 15,
           "z": 12, "r": 12, "vn": 12, "vn_out": 13, "vnd": 12, "su": 12, "s": 13, "o": 1,
           "end": 3}

    def __init__(self, core):
        super().__init__(core)
        self.s = {n: core.sem("dn_" + n) for n in self.PER}
        v = core.view
        self.z, self.q, self.k, self.v = v(G_Z, T), v(G_Q, T), v(G_K, KEYS), v(G_V, KEYS)
        self.kt, self.vt = v(G_KT, NTA, P), v(G_VT, NTA, P)
        self.g, self.beta, self.gcum, self.kd, self.gl = (v(G_COL + 12 * i, 2, NTA) for i in range(5))
        self.order = [[0, 1, 2, 3, 4, 5], [1, 0, 5, 4, 3, 2]]
        self.o = v(G_O, T)
        self.taps = v(G_TAPS, 3, 3)
        core.mix = v(G_MIX, KD, T)
        self.before = len(core.slabs)

    def lane(self, l, at, *dims):
        return self.c.view(G_LANE + LANE * l + at, *dims)

    def st(self, l, i):
        return self.c.view(G_S + P * (4 * l + i), P)

    def wait(self, eng, h, name, n):
        eng.wait_ge(self.s[name], h * self.PER[name] + n)

    def end(self, eng, h):
        eng.drain().then_inc(self.s["end"], 1)
        self.wait(eng, h, "end", 3)

    TILES = [(0, False), (1, True), (1, False), (2, True), (2, False), (3, False)]

    def slab_dst(self):
        return self.c.view(RING0 + SLOT * (self.before % SLOTS), 4, KD, P)

    def sync(self, sp):
        c = self.c
        w = c.d["w_in_a_2"][0]
        slot = self.before % SLOTS
        if self.before >= SLOTS:
            sp.wait_ge(c.slab_out[slot], self.before // SLOTS)
        with sp.Fori(0, DHEADS) as h:
            self.wait(sp, h, "slab_free", 0)
            for part in range(4):
                sp.dma_start(self.slab_dst()[:, part], w[:, ds(h * P + D * part, P)].rearrange("(k p) n -> p k n", p=P))\
                    .then_inc(self.s["slab"], 16)
        self.wait(sp, DHEADS - 1, "slab_free", 1)

    def tensor(self, pe):
        with pe.Fori(0, DHEADS) as h:
            self.tensor_head(pe, h)

    def vector(self, dve):
        with dve.Fori(0, DHEADS) as h:
            self.vector_head(dve, h)

    def scalar(self, act):
        with act.Fori(0, DHEADS) as h:
            self.scalar_head(act, h)

    def tensor_head(self, pe, h):
        c, s = self.c, self.s
        w = self.slab_dst()
        ones, ident = c.const("ones"), c.const("ident")
        self.wait(pe, h, "slab", 64)
        for i, (part, ctx) in enumerate(self.TILES):
            src, n = (c.hc, TC) if ctx else (c.h, T)
            for k in range(KD):
                ins = pe.matmul(c.ps[:, i, 0:n], w[:, part, k, :], src[:, k, :], start=(k == 0), stop=(k == KD - 1))
            ins.then_inc(s["full"], 1)
        pe.drain().then_inc(s["slab_free"], 1)
        for i, (dst, at) in enumerate(((0, L_L), (2, L_L))):
            self.wait(pe, h, "square", i + 1)
            n = (T, KEYS)[i]
            sq = self.lane(i, L_L, n)
            ins = pe.matmul(c.ps[:, dst, 0:512], ones, sq[:, 0:512], start=True, stop=True)
            if i:
                ins = pe.matmul(c.ps[:, 3, 0:256], ones, sq[:, 512:768], start=True, stop=True)
            ins.then_inc(s["sumsq"], 1)
        self.wait(pe, h, "silu", 5)
        for t in range(NTA):
            ins = pe.transpose(c.pair(4, KEYS)[:, P * t:P * t + P], self.v[:, P * t:P * t + P], ident)
        ins.then_inc(s["turned"], 1)
        self.wait(pe, h, "unit", 2)
        for t in range(NTA):
            ins = pe.transpose(c.pair(6, KEYS)[:, P * t:P * t + P], self.k[:, P * t:P * t + P], ident)
        ins.then_inc(s["turned"], 1)
        self.wait(pe, h, "cols", 1)
        self.wait(pe, h, "turned_out", 2)
        for l in range(2):
            for t in range(NTA):
                pe.matmul(c.pair(4 * l, KEYS)[:, P * t:P * t + P], self.g[:, l, t:t + 1].to_broadcast([P, P]),
                          c.const(("cum_f", "cum_b")[l]), start=True, stop=True)
                ins = pe.matmul(c.pair(4 * l + 2, KEYS)[:, P * t:P * t + P],
                                self.beta[:, l, t:t + 1].to_broadcast([P, P]), ident, start=True, stop=True)
            ins.then_inc(s["rows"], 1)
        for l in range(2):
            self.wait(pe, h, "kb", l + 1)
            self.wait(pe, h, "grown", l + 1)
            self.wait(pe, h, "kdarg", l + 1)
            for t in range(NTA):
                cols = slice(P * t, P * t + P)
                ins = pe.matmul(c.pair(4 * l, KEYS)[:, cols], self.k[:, cols], self.lane(l, L_T, KEYS)[:, cols],
                                start=True, stop=True)
                if t >= NTC:
                    ins = pe.matmul(c.ps[:, 4 * l + 2, P * (t - NTC):P * (t - NTC) + P], self.k[:, cols],
                                    self.q[:, P * (t - NTC):P * (t - NTC) + P], start=True, stop=True)
            ins.then_inc(s["kk"], 1)
        for v in range(LEVELS):
            for l in range(2):
                i = 2 * v + l
                T_, TT, A, M = (self.lane(l, a, NTA, P) for a in (L_T, L_TT, L_A, L_M))
                self.wait(pe, h, "mt", i + 1)
                if v:
                    self.wait(pe, h, "upd", i - 1)
                for t in range(NTA):
                    ins = pe.matmul(c.pair(4 * l, KEYS)[:, P * t:P * t + P], M[:, t, :], T_[:, t, :] if v else ident,
                                    start=True, stop=True)
                ins.then_inc(s["a"], 1)
            if v == 0:
                continue
            for l in range(2):
                i = 2 * v + l
                T_, TT, A, M = (self.lane(l, a, NTA, P) for a in (L_T, L_TT, L_A, L_M))
                self.wait(pe, h, "a_out", i - 1)
                for t in range(NTA):
                    if v < LEVELS - 1:
                        pe.matmul(c.pair(4 * l + 2, KEYS)[:, P * t:P * t + P], TT[:, t, :], A[:, t, :], start=True, stop=True)
                    ins = pe.matmul(c.pair(4 * l, KEYS)[:, P * t:P * t + P], A[:, t, :], TT[:, t, :], start=True, stop=True)
                ins.then_inc(s["x"], 1)
        for step in range(NTA):
            for l in range(2):
                i = 2 * step + l
                t = self.order[l][step]
                if step == 0:
                    self.wait(pe, h, "upd", 13 + l)
                    self.wait(pe, h, "upd", 15)
                else:
                    self.wait(pe, h, "s", i - 1)
                pe.matmul(c.ps[:, 4 * l, 0:P], self.lane(l, L_KBG, NTA, P)[:, t, :], self.st(l, 0), start=True, stop=True)\
                    .then_inc(s["z"], 1)
            for l in range(2):
                i = 2 * step + l
                t = self.order[l][step]
                self.wait(pe, h, "r", i + 1)
                pe.matmul(c.ps[:, 4 * l + 1, 0:P], self.lane(l, L_TT, NTA, P)[:, t, :], self.st(l, 1), start=True, stop=True)\
                    .then_inc(s["vn"], 1)
            for l in range(2):
                i = 2 * step + l
                t = self.order[l][step]
                if t >= NTC:
                    out = c.ps[:, 4 * l + 3, P * (t - NTC):P * (t - NTC) + P]
                    cols = slice(P * (t - NTC), P * (t - NTC) + P)
                    pe.matmul(out, self.st(l, 0), self.lane(l, L_QD, T)[:, cols], start=True, stop=False)
                self.wait(pe, h, "vn_out", i + 1)
                if t >= NTC:
                    pe.matmul(out, self.st(l, 2), self.lane(l, L_QK, T)[:, cols], start=False, stop=True)
                self.wait(pe, h, "vnd", i + 1)
                pe.matmul(c.ps[:, 4 * l + 2, 0:P], self.kt[:, t, :], self.st(l, 3), start=True, stop=True)\
                    .then_inc(s["su"], 1)
        pe.drain().then_inc(s["o"], 1)
        self.wait(pe, h, "square", 3)
        pe.matmul(c.ps[:, 0, :], c.const("one_over_p"), self.lane(0, L_L, T), start=True, stop=True).then_inc(s["sumsq"], 1)
        self.end(pe, h)

    def dest(self, i):
        return (self.q, self.k[:, 0:TC], self.k[:, TC:KEYS], self.v[:, 0:TC], self.v[:, TC:KEYS])[i]

    def col(self, tap, part):
        return self.taps[:, tap, part:part + 1]

    def scalar_head(self, act, h):
        c, s = self.c, self.s
        self.wait(act, h, "cols", 1)
        for i, (part, ctx) in enumerate(self.TILES[:5]):
            n = TC if ctx else T
            self.wait(act, h, "full", i + 1)
            act.activation(self.dest(i), c.ps[:, i, 0:n], ACT.Copy, scale=self.col(1, part))\
                .then_inc(s["centre"], 1)
        self.wait(act, h, "full", 6)
        act.activation(self.z, c.ps[:, 5, :], ACT.Silu)
        for i in range(5):
            self.wait(act, h, "conv", i + 1)
            act.activation(self.dest(i), self.dest(i), ACT.Silu).then_inc(s["silu"], 1)
        act.drain()
        for i, v in enumerate((self.q, self.k)):
            act.activation(self.lane(i, L_L, (T, KEYS)[i]), v, ACT.Square).then_inc(s["square"], 1)
        for i in range(2):
            self.wait(act, h, "sumsq", i + 1)
            n = (T, KEYS)[i]
            act.activation(self.lane(i, L_M, n), c.pair(2 * i, n), ACT.Sqrt, bias=c.eps(1)).then_inc(s["std"], 1)
        self.wait(act, h, "turned", 2)
        act.activation(self.kt.rearrange("p t n -> p (t n)"), c.pair(6, KEYS), ACT.Copy).then_inc(s["turned_out"], 1)
        for l in range(2):
            self.wait(act, h, "rows", l + 1)
            act.activation(self.lane(l, L_A, KEYS), c.pair(4 * l, KEYS), ACT.Exp)
            act.drain().then_inc(s["grown"], 1)
        for l in range(2):
            self.wait(act, h, "darg", l + 1)
            m = self.lane(l, L_M, KEYS)
            act.activation(m, m, ACT.Exp)
            self.wait(act, h, "kdarg", l + 1)
            act.activation(self.kd[:, l, :], self.kd[:, l, :], ACT.Exp)
            act.drain().then_inc(s["dexp"], 1)
        for v in range(1, LEVELS):
            for l in range(2):
                i = 2 * v + l
                self.wait(act, h, "a", i + 1)
                act.activation(self.lane(l, L_A, KEYS), c.pair(4 * l, KEYS), ACT.Copy).then_inc(s["a_out"], 1)
        for i in range(2 * NTA):
            l = i % 2
            self.wait(act, h, "vn", i + 1)
            act.activation(self.st(l, 2), c.ps[:, 4 * l + 1, 0:P], ACT.Copy).then_inc(s["vn_out"], 1)
        self.wait(act, h, "o", 1)
        act.activation(self.o, c.ps[:, 3, :], ACT.Copy).then_inc(s["vn_out"], 1)
        self.wait(act, h, "s", 13)
        act.activation(self.lane(0, L_L, T), self.o, ACT.Square).then_inc(s["square"], 1)
        self.wait(act, h, "sumsq", 3)
        act.activation(self.lane(0, L_A, T), c.ps[:, 0, :], ACT.Sqrt, bias=c.eps(1)).then_inc(s["std"], 1)
        self.end(act, h)

    def vector_head(self, dve, h):
        c, s = self.c, self.s
        for dst, src in ((self.g, G_G), (self.beta, G_BETA), (self.gcum, G_GC)):
            v = c.view(src, NTA, 2, DHEADS)
            for l in range(2):
                dve.tensor_copy(dst[:, l, :].unsqueeze(2), v[:, :, l, ds(h, 1)])
        taps = c.view(PAR0 + PAR["conv_a0"][0], 3, 3, DHEADS)
        for tap in range(3):
            dve.tensor_copy(self.taps[:, tap, :].unsqueeze(2), taps[:, tap, :, ds(h, 1)])
        dve.drain().then_inc(s["cols"], 1)
        for i, (part, ctx) in enumerate(self.TILES[:5]):
            n = TC if ctx else T
            self.wait(dve, h, "centre", i + 1)
            conv3(dve, self.dest(i), c.ps[:, i, :], self.col(0, part), self.col(2, part), n)\
                .then_inc(s["conv"], 1)
        for i, v in enumerate((self.q, self.k)):
            r = self.lane(i, L_M, (T, KEYS)[i])
            self.wait(dve, h, "std", i + 1)
            dve.reciprocal(r, r)
            dve.drain()
            dve.scalar_tensor_tensor(out=v, in0=v, scalar=(P ** -0.5, 1.0)[i], in1=r, op0=ALU.mult, op1=ALU.mult)\
                .then_inc(s["unit"], 1)
        self.wait(dve, h, "turned", 1)
        dve.tensor_copy(self.vt.rearrange("p t n -> p (t n)"), c.pair(4, KEYS)).then_inc(s["turned_out"], 1)
        for l in range(2):
            kb, m = self.lane(l, L_T, KEYS), self.lane(l, L_M, NTA, P)
            rows = c.pair(4 * l, KEYS).rearrange("p (t n) -> p t n", n=P)
            self.wait(dve, h, "rows", l + 1)
            dve.tensor_tensor(kb, self.k, c.pair(4 * l + 2, KEYS), ALU.mult).then_inc(s["kb"], 1)
            self.wait(dve, h, "grown", l + 1)
            for t in range(NTA):
                dve.tensor_scalar(m[:, t, :], rows[:, t, :], self.gcum[:, l, t:t + 1], 0.0, ALU.subtract, ALU.min)
            dve.drain().then_inc(s["darg"], 1)
            last = P - 1 if l == 0 else 0
            dve.tensor_tensor(self.kd[:, l, :], rows[:, :, last], self.gcum[:, l, :], ALU.subtract)
            dve.drain().then_inc(s["kdarg"], 1)
        for l in range(2):
            kb, kbg, grown = self.lane(l, L_T, KEYS), self.lane(l, L_KBG, KEYS), self.lane(l, L_A, KEYS)
            last = P - 1 if l == 0 else 0
            dve.tensor_tensor(kbg, kb, grown, ALU.mult)
            dve.tensor_tensor(self.lane(l, L_QD, T), self.q, grown[:, TC:KEYS], ALU.mult)
            dve.tensor_copy(self.gl[:, l, :], grown.rearrange("p (t n) -> p t n", n=P)[:, :, last])
            self.wait(dve, h, "dexp", l + 1)
            m = self.lane(l, L_M, NTA, P)
            tri = c.const(("cum_f", "cum_b")[l]).unsqueeze(1).to_broadcast([P, NTA, P])
            dve.tensor_tensor(m, m, tri, ALU.mult)
            dve.drain()
            self.wait(dve, h, "kk", l + 1)
            flat = self.lane(l, L_M, KEYS)
            dve.tensor_tensor(self.lane(l, L_L, KEYS), flat, c.pair(4 * l, KEYS), ALU.mult)
            dve.tensor_tensor(self.lane(l, L_QK, T), flat[:, TC:KEYS], c.ps[:, 4 * l + 2, :], ALU.mult)
            dve.drain().then_inc(s["lt"], 1)
        ident = c.const("ident").unsqueeze(1).to_broadcast([P, NTA, P])
        for v in range(LEVELS):
            for l in range(2):
                i = 2 * v + l
                mask = c.view(G_MASK + P * (7 * l + v), P).unsqueeze(1).to_broadcast([P, NTA, P])
                if v:
                    dve.drain()
                    self.wait(dve, h, "a", i - 1)
                dve.tensor_tensor(self.lane(l, L_M, NTA, P), self.lane(l, L_L, NTA, P), mask, ALU.mult)\
                    .then_inc(s["mt"], 1)
            for l in range(2):
                i = 2 * v + l
                T_, TT, M = (self.lane(l, a, NTA, P) for a in (L_T, L_TT, L_M))
                ax, xx = (c.pair(4 * l + b, KEYS).rearrange("p (t n) -> p t n", n=P) for b in (0, 2))
                if v == 0:
                    dve.drain()
                    self.wait(dve, h, "a", i + 1)
                    dve.tensor_tensor(TT, ident, M, ALU.subtract)
                    dve.tensor_tensor(T_, ident, ax, ALU.subtract)
                else:
                    self.wait(dve, h, "x", i - 1)
                    if v < LEVELS - 1:
                        dve.tensor_tensor(T_, T_, xx, ALU.subtract)
                    dve.tensor_tensor(TT, TT, ax, ALU.subtract)
                dve.drain().then_inc(s["upd"], 1)
        for l in range(2):
            dve.memset(self.st(l, 0), 0.0)
        dve.drain().then_inc(s["upd"], 1)
        for step in range(NTA):
            for l in range(2):
                i = 2 * step + l
                t = self.order[l][step]
                self.wait(dve, h, "z", i + 1)
                dve.scalar_tensor_tensor(out=self.st(l, 1), in0=self.vt[:, t, :], scalar=self.beta[:, l, t:t + 1],
                                         in1=c.ps[:, 4 * l, 0:P], op0=ALU.mult, op1=ALU.subtract).then_inc(s["r"], 1)
            for l in range(2):
                i = 2 * step + l
                t = self.order[l][step]
                self.wait(dve, h, "vn_out", i + 1)
                dve.tensor_scalar(self.st(l, 3), self.st(l, 2), self.kd[:, l, t:t + 1], None, ALU.mult)\
                    .then_inc(s["vnd"], 1)
            for l in range(2):
                i = 2 * step + l
                t = self.order[l][step]
                self.wait(dve, h, "su", i + 1)
                dve.scalar_tensor_tensor(out=self.st(l, 0), in0=self.st(l, 0), scalar=self.gl[:, l, t:t + 1],
                                         in1=c.ps[:, 4 * l + 2, 0:P], op0=ALU.mult, op1=ALU.add).then_inc(s["s"], 1)
        self.wait(dve, h, "vn_out", 13)
        dve.tensor_tensor(self.o, self.o, c.ps[:, 7, :], ALU.add).then_inc(s["s"], 1)
        self.wait(dve, h, "std", 3)
        r = self.lane(0, L_A, T)
        dve.reciprocal(r, r)
        dve.drain()
        dve.tensor_tensor(self.o, self.o, r, ALU.mult)
        dve.drain()
        dve.scalar_tensor_tensor(out=c.arena[:, ds(h * T + G_MIX, T)], in0=self.o, scalar=c.par("onorm_a"),
                                 in1=self.z, op0=ALU.mult, op1=ALU.mult)
        self.end(dve, h)



R_HT = W0
R_W = R_HT + NT * D
R_SM = R_W + KD * 36
R_END = R_SM + 3600
M_KEEP = W0 + WORK - 256
M_WT = M_KEEP
M_PLAN = M_KEEP + 8
M_IDX = M_KEEP + 112
M_GI = M_KEEP + 200
M_SLOT = W0
M_G = M_SLOT + 2 * SLOT
M_GT = M_G + 2 * D
M_S = M_GT + D
M_HH = M_S + 512
M_HT = M_HH + 512
M_Y = M_HT + 512
PAD = 1 << 20
TABLE = (BLOCKS + 2) * P


class Route(Stage):

    def __init__(self, core, i):
        super().__init__(core)
        self.i = i
        self.per = {"w": 32, "turned": 8, "turned_out": 8, "stored": 16, "logits": 1, "gsub": 1, "gexp": 1,
                    "esub": 1, "eexp": 1, "rank": 1, "filled": 16, "placed": 128, "back": 16,
                    "hot_done": 1, "dest_done": 1, "vals_done": 1}
        self.base = {}
        for n, k in self.per.items():
            self.base[n] = core.shared("route_" + n, k)[1]
        (self.w, self.turned, self.turned_out, self.stored, self.logits, self.gsub, self.gexp, self.esub,
         self.eexp, self.rank, self.filled, self.placed, self.back, self.hot_done, self.dest_done,
         self.vals_done) = (
            core.shared("route_" + n, 0)[0] for n in ("w", "turned", "turned_out", "stored", "logits",
                "gsub", "gexp", "esub", "eexp", "rank", "filled", "placed", "back", "hot_done",
                "dest_done", "vals_done"))
        v = core.view
        at = [R_SM]

        def new(*dims):
            a = at[0]
            at[0] += int(np.prod(dims))
            return v(a, *dims)

        self.new = new
        self.lg = new(NT, 36)
        self.eg, self.e8 = new(NT, GROUPS), new(NT, PER_GROUP)
        self.hot = new(2, NT, EXPERTS)
        self.both = new(NT, EXPERTS)
        self.destf = new(2, NT)
        self.dest = new(2, NT).bitcast(U32)
        self.vals = new(2, NT, 2).bitcast(I32)
        self.padv = new(2 * (BLOCKS + 2)).bitcast(I32)
        self.ht = v(R_HT, NT, D)
        self.rw = v(R_W, KD, 36)

    def scalar(self, act):
        c, d = self.c, self.c.d
        act.dma_start(self.rw[:, :, 0:GROUPS], d["router_g_2"][self.i].rearrange("(k p) n -> p k n", p=P)).then_inc(self.w, 16)
        act.dma_start(self.rw[:, :, GROUPS:36], d["router_e_2"][self.i].rearrange("(k p) n -> p k n", p=P)).then_inc(self.w, 16)
        act.wait_ge(self.gsub, self.base["gsub"] + 1)
        act.activation(self.eg, self.eg, ACT.Exp).then_inc(self.gexp, 1)
        act.wait_ge(self.esub, self.base["esub"] + 1)
        act.activation(self.e8, self.e8, ACT.Exp).then_inc(self.eexp, 1)
        act.wait_ge(self.turned_out, self.base["turned_out"] + 8)
        act.dma_start(c.d["h_rows"].rearrange("(t p) n -> p t n", p=P), self.ht).then_inc(self.stored, 16)
        act.wait_ge(self.stored, self.base["stored"] + 16)
        act.wait_ge(self.placed, self.base["placed"] + 16 * 8)
        act.dma_start(c.view(M_IDX, BLOCKS + 2, 2).bitcast(I32), c.d["table"].rearrange("(b p) c -> p b c", p=P))\
            .then_inc(self.back, 16)
        act.wait_ge(self.back, self.base["back"] + 16)

    def gpsimd(self, pool):
        c = self.c
        for k in range(2):
            for j in range(2):
                pool.iota(self.vals[:, k, :, j], [[P, NT]], base=T * k * j, channel_multiplier=1)
        pool.memset(self.padv, PAD)
        pool.drain().then_inc(self.vals_done, 1)
        pool.wait_ge(self.vals_done, self.base["vals_done"] + 1)
        pool.dma_start(c.d["table"].rearrange("(p b) c -> p (b c)", p=P), self.padv).then_inc(self.filled, 16)
        pool.wait_ge(self.filled, self.base["filled"] + 16)
        pool.wait_ge(self.dest_done, self.base["dest_done"] + 1)
        for k in range(2):
            for t in range(NT):
                pool.indirect_dma_start(c.d["table"], bass.IndirectOffsetOnAxis(ap=self.dest[:, k, t:t + 1], axis=0),
                                        self.vals[:, k, t, :], None).then_inc(self.placed, 16)
        pool.wait_ge(self.placed, self.base["placed"] + 16 * 8)

    def tensor(self, pe):
        c = self.c
        pe.wait_ge(self.w, self.base["w"] + 32)
        for t in range(NT):
            for k in range(KD):
                ins = pe.matmul(c.ps[:, 6, 36 * t:36 * t + 36], c.h[:, k, P * t:P * t + P], self.rw[:, k, :],
                                start=(k == 0), stop=(k == KD - 1))
        ins.then_inc(self.logits, 1)
        for i in range(8):
            t, half = i // 2, i % 2
            if i >= 4:
                pe.wait_ge(self.turned_out, self.base["turned_out"] + i - 3)
            for m in range(4):
                ins = pe.transpose(c.ps[:, i % 4, P * m:P * m + P], c.h[:, 4 * half + m, P * t:P * t + P], c.const("ident"))
            ins.then_inc(self.turned, 1)
        pe.wait_ge(self.hot_done, self.base["hot_done"] + 1)
        for t in range(NT):
            for b in range(t + 1):
                pe.matmul(c.ps[:, 7, 32 * t:32 * t + 32], c.const("before" if b == t else "ones"), self.both[:, b, :],
                          start=(b == 0), stop=(b == t))
        for t in range(NT):
            ins = pe.matmul(c.ps[:, 7, 128:160], c.const("ones"), self.both[:, t, :], start=(t == 0), stop=(t == NT - 1))
        ins.then_inc(self.rank, 1)

    def vector(self, dve):
        c, new = self.c, self.new
        iota = c.const("iota")

        def row(v, n, m):
            return v.unsqueeze(1).to_broadcast([P, n, m])

        def col(v, m):
            return v.unsqueeze(2).to_broadcast([P, v.shape[1], m])

        def tt(out, a, b, op):
            dve.tensor_tensor(out, a, b, op)
            dve.drain()

        def ts(out, a, s1, s2, op0, op1=ALU.bypass):
            if s2 is None:
                dve.tensor_scalar(out, a, s1, None, op0)
            else:
                dve.tensor_scalar(out, a, s1, s2, op0, op1)
            dve.drain()

        def reduce(out, a, op):
            dve.tensor_reduce(out, a, AX.X, op)
            dve.drain()

        def first_max(e, n):
            top, idx, hot = new(NT), new(NT), new(NT, n)
            reduce(top, e, ALU.max)
            tt(hot, e, col(top, n), ALU.is_ge)
            ts(hot, hot, -100.0, 100.0, ALU.mult, ALU.add)
            tt(hot, hot, row(iota[:, 0:n], NT, n), ALU.add)
            reduce(idx, hot, ALU.min)
            tt(hot, row(iota[:, 0:n], NT, n), col(idx, n), ALU.is_equal)
            return top, idx, hot

        dve.wait_ge(self.logits, self.base["logits"] + 1)
        dve.tensor_copy(self.lg, c.ps[:, 6, 0:36 * NT].rearrange("p (t n) -> p t n", t=NT))
        dve.drain()
        mg, sg, group_w = new(NT), new(NT), new(NT)
        reduce(mg, self.lg[:, :, 0:GROUPS], ALU.max)
        dve.tensor_tensor(self.eg, self.lg[:, :, 0:GROUPS], col(mg, GROUPS), ALU.subtract).then_inc(self.gsub, 1)
        for i in range(8):
            dve.wait_ge(self.turned, self.base["turned"] + i + 1)
            dve.tensor_copy(self.ht[:, i // 2, 512 * (i % 2):512 * (i % 2) + 512], c.ps[:, i % 4, :]).then_inc(self.turned_out, 1)
        dve.wait_ge(self.gexp, self.base["gexp"] + 1)
        reduce(sg, self.eg, ALU.add)
        top, gi, ghot = first_max(self.eg, GROUPS)
        dve.reciprocal(sg, sg)
        dve.drain()
        tt(group_w, top, sg, ALU.mult)
        pick, le, m8 = new(NT, GROUPS, PER_GROUP), new(NT, PER_GROUP), new(NT)
        for t in range(NT):
            dve.tensor_tensor(pick[:, t], self.lg[:, t, GROUPS:36].rearrange("p (g e) -> p g e", g=GROUPS),
                              ghot[:, t, :].unsqueeze(2).to_broadcast([P, GROUPS, PER_GROUP]), ALU.mult)
        dve.drain()
        for t in range(NT):
            dve.tensor_reduce(le[:, t, :], pick[:, t].rearrange("p g e -> p e g"), AX.X, ALU.add)
        dve.drain()
        reduce(m8, le, ALU.max)
        dve.tensor_tensor(self.e8, le, col(m8, PER_GROUP), ALU.subtract).then_inc(self.esub, 1)
        dve.wait_ge(self.eexp, self.base["eexp"] + 1)
        e1, i1, h1 = first_max(self.e8, PER_GROUP)
        ts(h1, h1, -2.0, None, ALU.mult)
        tt(self.e8, self.e8, h1, ALU.add)
        e2, i2, h2 = first_max(self.e8, PER_GROUP)
        den = new(NT)
        tt(den, e1, e2, ALU.add)
        dve.reciprocal(den, den)
        dve.drain()
        tt(den, den, group_w, ALU.mult)
        wt = c.view(M_WT, NT, 2)
        tt(wt[:, :, 0], den, e1, ALU.mult)
        tt(wt[:, :, 1], den, e2, ALU.mult)
        for k, idx in enumerate((i1, i2)):
            eid = new(NT)
            dve.scalar_tensor_tensor(out=eid, in0=gi, scalar=float(PER_GROUP), in1=idx, op0=ALU.mult, op1=ALU.add)
            dve.drain()
            tt(self.hot[:, k], row(iota[:, 0:EXPERTS], NT, EXPERTS), col(eid, EXPERTS), ALU.is_equal)
        tt(self.both, self.hot[:, 0], self.hot[:, 1], ALU.add)
        dve.drain().then_inc(self.hot_done, 1)
        dve.wait_ge(self.rank, self.base["rank"] + 1)
        cnt, nb, part, ends, base = new(EXPERTS), new(EXPERTS), new(EXPERTS), new(EXPERTS), new(NT, EXPERTS)
        dve.tensor_copy(cnt, c.ps[:, 7, 128:160])
        dve.tensor_copy(base, c.ps[:, 7, 0:128].rearrange("p (t e) -> p t e", t=NT))
        dve.drain()
        ts(nb, cnt, 0.0, None, ALU.is_gt)
        for b in range(1, NT):
            ts(part, cnt, float(P * b), None, ALU.is_gt)
            tt(nb, nb, part, ALU.add)
        dve.tensor_tensor_scan(ends, c.const("ones")[:, 0:EXPERTS], nb, 0.0, ALU.mult, ALU.add)
        dve.drain()
        tt(part, ends, nb, ALU.subtract)
        ts(part, part, float(P), None, ALU.mult)
        tt(base, base, row(part, NT, EXPERTS), ALU.add)
        for k in range(2):
            tt(self.hot[:, k], self.hot[:, k], base, ALU.mult)
            reduce(self.destf[:, k, :], self.hot[:, k], ALU.add)
        dve.tensor_copy(self.dest, self.destf)
        dve.drain().then_inc(self.dest_done, 1)
        planf, cmp = new(48), c.view(R_HT, BLOCKS, EXPERTS)
        dve.wait_ge(self.stored, self.base["stored"] + 16)
        tt(cmp, row(ends, BLOCKS, EXPERTS), col(iota[:, 0:BLOCKS], EXPERTS), ALU.is_le)
        reduce(planf[:, 0:BLOCKS], cmp, ALU.add)
        ts(planf[:, 0:BLOCKS], planf[:, 0:BLOCKS], float(EXPERTS - 1), None, ALU.min)
        even = new(BLOCKS // 2)
        ts(even, iota[:, 0:BLOCKS:2], ends[:, EXPERTS - 1:EXPERTS], None, ALU.is_lt)
        reduce(planf[:, BLOCKS:BLOCKS + 1], even, ALU.add)
        dve.tensor_copy(c.view(M_PLAN + 48 * self.i, BLOCKS + 1).bitcast(I32), planf[:, 0:BLOCKS + 1])


class Experts(Stage):

    def __init__(self, core, i, weights, before):
        super().__init__(core)
        self.i, self.before = i, before
        self.w1, self.w3, self.w2 = (core.d[w][i] for w in weights)
        self.w_in = [core.shared(f"expert_in{j}", 0)[0] for j in range(6)]
        self.w_out = [core.shared(f"expert_out{j}", 0)[0] for j in range(6)]
        self.gather = [core.shared(f"expert_gather{b}", 0)[0] for b in range(2)]
        self.scatter = [core.shared(f"expert_scatter{b}", 0)[0] for b in range(2)]
        (self.clear, self.turned, self.gt, self.h1, self.h3, self.silu, self.prod, self.hturned, self.ht,
         self.y, self.y_out, self.gidx, self.sidx, self.settled) = (
            core.shared("expert_" + n, 0)[0] for n in ("clear", "turned", "gt", "h1", "h3", "silu", "prod",
                "hturned", "ht", "y", "y_out", "gidx", "sidx", "settled"))
        v = core.view
        self.g, self.y_sb = v(M_G, 2, D), v(M_Y, 2, D)
        self.gt_sb, self.s_sb, self.hh, self.ht_sb = v(M_GT, KD, P), v(M_S, 512), v(M_HH, 512), v(M_HT, 4, P)
        self.plan = v(M_PLAN + 48 * i, BLOCKS + 1).bitcast(I32)
        self.plan_first = v(M_PLAN, BLOCKS + 1).bitcast(I32)
        self.idx = v(M_IDX, BLOCKS + 2, 2).bitcast(I32)
        self.gi = v(M_GI, 2).bitcast(I32)
        self.si = v(M_GI + 2, 2).bitcast(I32)

    def slot(self, j, *dims):
        return self.c.view(RING0 + SLOT * j if j < SLOTS else M_SLOT + SLOT * (j - SLOTS), *dims)

    def steps(self, eng):
        n = eng.value_load(self.plan[0:1, BLOCKS:BLOCKS + 1], min_val=1, max_val=BLOCKS // 2)
        if self.i == 0:
            return 0, n
        first = eng.value_load(self.plan_first[0:1, BLOCKS:BLOCKS + 1], min_val=1, max_val=BLOCKS // 2)
        return first, n

    def sync(self, sp):
        sp.wait_ge(self.c.stage_end, 4 * self.before)
        first, n = self.steps(sp)
        with sp.Fori(0, n) as step:
            i = first + step
            for b in range(2):
                e = sp.value_load(self.plan[0:1, ds(2 * step + b, 1)], min_val=0, max_val=EXPERTS - 1)
                for j, w in enumerate((self.w1, self.w3, self.w2)):
                    s = 3 * b + j
                    sp.wait_ge(self.w_out[s], i + 1)
                    src = w[ds(e, 1)].rearrange("a (k p) n -> p (a k) n", p=P)
                    sp.dma_start(self.slot(s, *((KD, 512) if j < 2 else (4, D))), src).then_inc(self.w_in[s], 16)

    def open_room(self, eng, *sems):
        if self.i == 0:
            for s in sems:
                eng.sem_inc(s, 1)

    def settle(self, pool):
        pool.sem_inc(self.settled, 1)

    def gather_block(self, pool, b, block, i):
        pool.tensor_copy(self.gi[:, b:b + 1].unsqueeze(1), self.idx[:, ds(block, 1), 0:1]).then_inc(self.gidx, 1)
        pool.wait_ge(self.gidx, 2 * (i + self.i) + b + 1)
        self.settle(pool)
        pool.indirect_dma_start(self.g[:, b, :], None, self.c.d["h_rows"],
                                bass.IndirectOffsetOnAxis(ap=self.gi[:, b:b + 1].bitcast(U32), axis=0),
                                bounds_check=T - 1, oob_is_err=False).then_inc(self.gather[b], 16)

    def scatter_block(self, pool, b):
        pool.indirect_dma_start(self.c.d["pair_rows"],
                                bass.IndirectOffsetOnAxis(ap=self.si[:, b:b + 1].bitcast(U32), axis=0),
                                self.y_sb[:, b, :], None,
                                bounds_check=2 * T - 1, oob_is_err=False).then_inc(self.scatter[b], 16)

    def gpsimd(self, pool):
        pool.memset(self.g, 0.0)
        if self.i == 0:
            pool.memset(self.si, PAD)
            pool.memset(self.y_sb, 0.0)
        pool.drain().then_inc(self.clear, 1)
        pool.wait_ge(self.clear, self.i + 1)
        first, n = self.steps(pool)
        if self.i == 0:
            for b in range(2):
                self.scatter_block(pool, b)
        for b in range(2):
            self.gather_block(pool, b, b, first)
        with pool.Fori(0, n) as step:
            i = first + step
            for b in range(2):
                pool.wait_ge(self.gather[b], 16 * (i + self.i) + 16)
                pool.wait_ge(self.turned, 2 * i + b + 1 + self.i)
                self.gather_block(pool, b, 2 * step + 2 + b, i + 1)
                pool.wait_ge(self.scatter[b], 16 * i + 16)
                pool.tensor_copy(self.si[:, b:b + 1].unsqueeze(1), self.idx[:, ds(2 * step + b, 1), 1:2]).then_inc(self.sidx, 1)
                pool.wait_ge(self.sidx, 2 * i + b + 1)
                pool.wait_ge(self.y_out, 4 * i + 2 * b + 3)
                self.settle(pool)
                self.scatter_block(pool, b)
        for b in range(2):
            pool.wait_ge(self.gather[b], 16 * (first + n + self.i) + 16)
            pool.wait_ge(self.scatter[b], 16 * (first + n) + 16)
        self.settle(pool)

    def tensor(self, pe):
        c = self.c
        ident = c.const("ident")

        def turn(b, i, r):
            pe.wait_ge(self.gather[b], 16 * (i + self.i) + 16)
            pe.wait_ge(self.gt, 2 * (r + self.i) + 1)
            for k in range(KD):
                ins = pe.transpose(c.ps[:, k // 4, P * (k % 4):P * (k % 4) + P], self.g[:, b, P * k:P * k + P], ident)
            ins.then_inc(self.turned, 1)

        first, n = self.steps(pe)
        self.open_room(pe, *self.w_out, self.hturned)
        turn(0, first, 2 * first)
        with pe.Fori(0, n) as step:
            i = first + step
            for b in range(2):
                r = 2 * i + b
                pe.wait_ge(self.gt, 2 * (r + self.i) + 3)
                for j, full in enumerate((self.h1, self.h3)):
                    s = 3 * b + j
                    w = self.slot(s, KD, 512)
                    pe.wait_ge(self.w_in[s], 16 * i + 16)
                    pe.wait_ge((self.silu, self.prod)[j], r + 1)
                    for k in range(KD):
                        ins = pe.matmul(c.ps[:, 2 + j, :], self.gt_sb[:, k, :], w[:, k, :], start=(k == 0), stop=(k == KD - 1))
                    ins.then_inc(full, 1)
                if b == 0:
                    turn(1, i, r + 1)
                else:
                    turn(0, i + 1, r + 1)
                pe.wait_ge(self.prod, r + 2)
                pe.sem_inc(self.w_out[3 * b], 1)
                pe.sem_inc(self.w_out[3 * b + 1], 1)
                pe.wait_ge(self.ht, r + 1)
                for k in range(4):
                    ins = pe.transpose(c.ps[:, 4, P * k:P * k + P], self.hh[:, P * k:P * k + P], ident)
                ins.then_inc(self.hturned, 1)
                s = 3 * b + 2
                w = self.slot(s, 4, D)
                pe.wait_ge(self.w_in[s], 16 * i + 16)
                pe.wait_ge(self.ht, r + 2)
                pe.wait_ge(self.y_out, 2 * r + 1)
                for half in range(2):
                    for k in range(4):
                        ins = pe.matmul(c.ps[:, 5 + half, :], self.ht_sb[:, k, :], w[:, k, 512 * half:512 * half + 512],
                                        start=(k == 0), stop=(k == 3))
                    ins.then_inc(self.y, 1)
                pe.drain().then_inc(self.w_out[s], 1)

    def scalar(self, act):
        c = self.c
        first, n = self.steps(act)

        def gt(r):
            act.wait_ge(self.turned, r + self.i + 1)
            act.activation(self.gt_sb[:, 0:4, :].rearrange("p k n -> p (k n)"), c.ps[:, 0, :], ACT.Copy).then_inc(self.gt, 1)

        self.open_room(act, self.silu, self.gt, self.ht, self.y_out)
        gt(2 * first)
        with act.Fori(0, n) as step:
            i = first + step
            for b in range(2):
                r = 2 * i + b
                act.wait_ge(self.h1, r + 1)
                act.wait_ge(self.prod, r + 1)
                act.activation(self.s_sb, c.ps[:, 2, :], ACT.Silu).then_inc(self.silu, 1)
                gt(r + 1)
                act.wait_ge(self.hturned, r + 2)
                act.activation(self.ht_sb.rearrange("p k n -> p (k n)"), c.ps[:, 4, :], ACT.Copy).then_inc(self.ht, 1)
                act.wait_ge(self.y, 2 * r + 2)
                act.wait_ge(self.scatter[b], 16 * i + 16)
                act.activation(self.y_sb[:, b, 512:D], c.ps[:, 6, :], ACT.Copy).then_inc(self.y_out, 1)

    def vector(self, dve):
        c = self.c
        first, n = self.steps(dve)

        def gt(r):
            dve.wait_ge(self.turned, r + self.i + 1)
            dve.tensor_copy(self.gt_sb[:, 4:8, :].rearrange("p k n -> p (k n)"), c.ps[:, 1, :]).then_inc(self.gt, 1)

        self.open_room(dve, self.prod)
        gt(2 * first)
        with dve.Fori(0, n) as step:
            i = first + step
            for b in range(2):
                r = 2 * i + b
                dve.wait_ge(self.silu, r + 2)
                dve.wait_ge(self.h3, r + 1)
                dve.wait_ge(self.hturned, r + 1)
                dve.tensor_tensor(self.hh, self.s_sb, c.ps[:, 3, :], ALU.mult).then_inc(self.prod, 1)
                gt(r + 1)
                dve.wait_ge(self.y, 2 * r + 1)
                dve.wait_ge(self.scatter[b], 16 * i + 16)
                dve.tensor_copy(self.y_sb[:, b, 0:512], c.ps[:, 5, :]).then_inc(self.y_out, 1)


class Combine(Stage):

    def __init__(self, core, i, gate):
        super().__init__(core)
        self.i, self.gate = i, gate
        self.rows, self.rows0 = core.shared("combine_rows", 16 * NT)
        self.sum, self.sum0 = core.shared("combine_sum", NT)
        self.turned, self.turned0 = core.shared("combine_turned", KD)
        self.y = core.view(W0, NT, 2, D)

    def scalar(self, act):
        rows = self.c.d["pair_rows"].rearrange("(k t p) n -> p t k n", k=2, t=NT)
        for t in range(NT):
            act.dma_start(self.y[:, t], rows[:, t]).then_inc(self.rows, 16)

    def vector(self, dve):
        c = self.c
        wt = c.view(M_WT, NT, 2)
        dve.wait_ge(self.rows, self.rows0 + 16 * NT)
        for t in range(NT):
            a, b = self.y[:, t, 0, :], self.y[:, t, 1, :]
            dve.tensor_scalar(a, a, wt[:, t, 0:1], None, ALU.mult)
            dve.drain()
            dve.scalar_tensor_tensor(out=a, in0=b, scalar=wt[:, t, 1:2], in1=a, op0=ALU.mult, op1=ALU.add).then_inc(self.sum, 1)
        for m in range(KD):
            dve.wait_ge(self.turned, self.turned0 + m + 1)
            dve.scalar_tensor_tensor(out=c.x[:, m, :], in0=c.ps[:, m, :], scalar=self.gate(m), in1=c.x[:, m, :],
                                     op0=ALU.mult, op1=ALU.add)

    def tensor(self, pe):
        c = self.c
        pe.wait_ge(self.sum, self.sum0 + NT)
        for m in range(KD):
            for t in range(NT):
                ins = pe.transpose(c.ps[:, m, P * t:P * t + P], self.y[:, t, 0, P * m:P * m + P], c.const("ident"))
            ins.then_inc(self.turned, 1)


class Store(Stage):

    def __init__(self, core):
        super().__init__(core)
        self.stored, self.base = core.shared("loaded", 16)

    def scalar(self, act):
        act.dma_start(self.c.d["out"].rearrange("(k p) t -> p k t", p=P), self.c.h).then_inc(self.stored, 16)
        act.wait_ge(self.stored, self.base + 16)


def stages(core):
    c, d = core, core.d
    out = []

    def add(s):
        s.number = len(out)
        out.append(s)

    def g(layer, what):
        return lambda m: c.ada(layer, what, m)

    def p(name):
        return lambda m: c.par(name, m)

    add(Load(c))
    for i in range(2):
        add(Modulation(c, i, d["mod_w"][i], f"mod_b{i}", "c", "c_ctx" if i == 0 else None))
        if i == 1:
            add(HyenaFilter(c))
        add(Norm(c, c.x, c.h, T, True, g(i, 1), g(i, 0), scratch=Y_HF if i else W0))
        if i == 0:
            add(Norm(c, c.hc, c.hc, TC, True, g(0, 7), g(0, 6)))
            add(AttentionIn(c))
            add(Attention(c))
            add(FourierMix(c))
            mix, w = c.view(A_MIX, KD, T), d["da_w_out"][0]
        else:
            add(HyenaIn(c))
            add(HyenaConv(c))
            mix, w = c.mix, d["hy_w_out"][0]
        add(Project(c, w, mix, g(i, 2), ALPHA))
        add(Norm(c, c.x, c.x, T, True, p(f"ln1_g{i}"), p(f"ln1_b{i}")))
        add(Norm(c, c.x, c.h, T, True, g(i, 4), g(i, 3)))
        add(FfnIn(c, i))
        add(FfnOut(c, i, g(i, 5)))
        add(Norm(c, c.x, c.x, T, True, p(f"ln2_g{i}"), p(f"ln2_b{i}")))
    for i in range(2):
        l = 2 + i
        add(Modulation(c, l, d["ada_w_2"][i], f"ada_b{i}", "c_2", "c_ctx_2" if i == 0 else None))
        add(Gains(c, l, f"norm_mix{i}", 1))
        add(Gains(c, l, f"norm_ffn{i}", 4))
        if i == 0:
            add(Gains(c, l, "norm_mix0", 7))
            add(LoadContext(c))
            add(Norm(c, c.hc, c.hc, TC, False, g(l, 7), g(l, 6)))
        add(Norm(c, c.x, c.h, T, False, g(l, 1), g(l, 0)))
        if i == 0:
            add(DeltaGates(c))
            add(DeltaHeads(c))
            mix, w = c.mix, d["w_out_a_2"][0]
        else:
            add(ShortConv(c))
            mix, w = c.view(B_Y, KD, T), d["w_out_b_2"][0]
        add(Project(c, w, mix, g(l, 2), 1.0))
        add(Norm(c, c.x, c.h, T, False, g(l, 4), g(l, 3)))
        add(Route(c, i))
        ex = Experts(c, i, ("w1_2", "w3_2", "w2_2"), len(out))
        ex.at = len(c.slabs)
        add(ex)
        add(Combine(c, i, g(l, 5)))
    add(Norm(c, c.x, c.h, T, False, p("final_norm"), None))
    add(Store(c))
    return out


def build(nc, d, until=None, dump=None):
    with ExitStack() as stack:
        core = Core(nc, d, stack)
        plan = stages(core)
        if until is not None:
            plan = plan[:until]
            core.until = until
        block = stack.enter_context(nc.Block())

        def meet(eng, s):
            eng.drain().then_inc(core.stage_end, 1)
            eng.wait_ge(core.stage_end, 4 * (s.number + 1))

        @block.sync
        def _(sp):
            n = 0
            for s in plan:
                if isinstance(s, DeltaHeads):
                    while n < s.before:
                        core.load_slab(sp, n)
                        n += 1
                    s.sync(sp)
                if isinstance(s, Experts):
                    while n < s.at:
                        core.load_slab(sp, n)
                        n += 1
                    s.sync(sp)
                    sp.wait_ge(core.stage_end, 4 * (s.number + 1))
            while n < len(core.slabs):
                core.load_slab(sp, n)
                n += 1
            if dump is not None:
                sp.wait_ge(core.stage_end, 4 * len(plan))
                dump(sp, core)

        @block.tensor
        def _(pe):
            for s in plan:
                s.tensor(pe)
                meet(pe, s)

        @block.scalar
        def _(act):
            for s in plan:
                s.scalar(act)
                meet(act, s)

        @block.vector
        def _(dve):
            for s in plan:
                s.vector(dve)
                meet(dve, s)

        @block.gpsimd
        def _(pool):
            for s in plan:
                s.gpsimd(pool)
                meet(pool, s)


_WEIGHTS = ("mod_w", "ffn_w_in", "ffn_w_out", "da_w_in", "da_w_out", "da_lam_q1", "da_lam_k1", "da_lam_q2",
            "da_lam_k2", "hy_w_in", "hy_f_w1", "hy_f_b1", "hy_f_w2", "hy_f_b2", "hy_f_w3", "hy_f_b3",
            "hy_f_freq", "hy_f_w4", "hy_w_out", "ada_w_2", "w_in_a_2", "a_log_a_2", "dt_bias_a_2",
            "w_out_a_2", "w_in_b_2", "w_out_b_2", "router_g_2", "router_e_2", "w1_2", "w3_2", "w2_2")


def layout(inputs):
    a = {k: np.asarray(v) for k, v in inputs.items()}
    vec = {}
    for i in range(2):
        vec[f"mod_b{i}"], vec[f"ada_b{i}"] = a["mod_b"][i], a["ada_b_2"][i]
        for n in ("ln1_g", "ln1_b", "ln2_g", "ln2_b"):
            vec[f"{n}{i}"] = a[n][i]
        for t in range(3):
            vec[f"ffn_conv_w{i}{t}"] = a["ffn_conv_w"][i, t]
        vec[f"ffn_conv_b{i}"] = a["ffn_conv_b"][i]
        vec[f"norm_mix{i}"], vec[f"norm_ffn{i}"] = a["norm_mix_2"][i], a["norm_ffn_2"][i]
    for t in range(3):
        vec[f"hy_conv_w{t}"], vec[f"conv_a{t}"], vec[f"conv_b{t}"] = (
            a["hy_conv_w"][0, t], a["conv_a_2"][0, t], a["conv_b_2"][0, t])
    vec["da_subln_g"], vec["hy_conv_b"], vec["hy_d"] = a["da_subln_g"][0], a["hy_conv_b"][0], a["hy_d"][0]
    vec["onorm_a"], vec["final_norm"] = a["onorm_a_2"][0], a["final_norm_2"]
    vec["c"], vec["c_ctx"], vec["c_2"], vec["c_ctx_2"] = a["c"][0], a["c_ctx"], a["c_2"][0], a["c_ctx_2"]
    rows = np.concatenate([vec[n].reshape(k, P) for n, k in _VECTORS])
    arrays = {n: np.ascontiguousarray(a[n]) for n in _WEIGHTS}
    arrays["vectors"] = np.ascontiguousarray(rows.T)
    arrays["x_t"] = np.ascontiguousarray(a["x"][0].T)
    arrays["ctx_t"] = np.ascontiguousarray(a["ctx"][0].T)
    arrays["ctx2_t"] = np.ascontiguousarray(a["ctx_2"][0].T)
    arrays.update(_constants())
    return arrays


def tensors(nc, arrays):
    d = {n: nc.dram_tensor(f"in_{n}", a.shape, mybir.dt.from_np(a.dtype), kind="ExternalInput").ap()
         for n, a in arrays.items()}
    d["out"] = nc.dram_tensor("out_t", (D, T), F32, kind="ExternalOutput").ap()
    d["h_rows"] = nc.dram_tensor("h_rows", (T, D), F32).ap()
    d["pair_rows"] = nc.dram_tensor("pair_rows", (2 * T, D), F32).ap()
    d["table"] = nc.dram_tensor("table", (TABLE, 2), I32).ap()
    return d


def kernel(**inputs):
    import concourse.bacc as _bacc
    from concourse.bass_utils import run_bass_kernel_spmd as _run

    nc = _bacc.Bacc("TRN2", target_bir_lowering=False, num_devices=1)
    arrays = layout(inputs)
    d = tensors(nc, arrays)
    build(nc, d)
    r = _run(nc, [{f"in_{n}": a for n, a in arrays.items()}], core_ids=[0])
    return np.ascontiguousarray(r.results[0]["out_t"].T)[None]
```

```python
import math
from contextlib import ExitStack

import numpy as np
import concourse.bass as bass
from concourse import mybir

F32 = mybir.dt.float32
F32R = mybir.dt.float32r
I32 = mybir.dt.int32
U32 = mybir.dt.uint32
ALU = mybir.AluOpType
ACT = mybir.ActivationFunctionType
AX = mybir.AxisListType
ds = bass.ds

P = 128
D = 1024
KD = D // P
T = 512
TC = 256
FFN = 2816
NF = FFN // P
DEPTH = 2
ALPHA = (2 * DEPTH) ** 0.25
LN_EPS, RMS_EPS = 1e-5, 1e-6
HEADS = 4
DHEADS = 8
NT = T // P
NTC = TC // P
NTA = NT + NTC
KEYS = TC + T
SLOTS = 4
SLOT = KD * 512
EXPERTS, GROUPS, PER_GROUP = 32, 4, 8
BLOCKS = 2 * T // P + EXPERTS
GRID_W = 64
HID = 64
LAM_INIT = 0.8 - 0.6

_VECTORS = (
    [(f"mod_b{i}", 48) for i in range(2)]
    + [(f"{n}{i}", 8) for n in ("ln1_g", "ln1_b", "ln2_g", "ln2_b") for i in range(2)]
    + [(f"ffn_conv_w{i}{t}", 44) for i in range(2) for t in range(3)]
    + [(f"ffn_conv_b{i}", 44) for i in range(2)]
    + [("da_subln_g", 1)]
    + [(f"hy_conv_w{t}", 24) for t in range(3)] + [("hy_conv_b", 24), ("hy_d", 8)]
    + [(f"ada_b{i}", 48) for i in range(2)]
    + [(f"{n}{i}", 8) for n in ("norm_mix", "norm_ffn") for i in range(2)]
    + [(f"conv_a{t}", 24) for t in range(3)] + [("onorm_a", 1)]
    + [(f"conv_b{t}", 8) for t in range(3)] + [("final_norm", 8)]
    + [(n, 8) for n in ("c", "c_ctx", "c_2", "c_ctx_2")]
)
PAR = {}
_at = 0
for _n, _k in _VECTORS:
    PAR[_n] = (_at, _k)
    _at += _k
NPAR = _at

_CONST_COLS = {}


def _const_layout():
    at = 0
    for name, n in (("ident", P), ("ones", P), ("one_over_d", P), ("one_over_p", P), ("swap", P),
                    ("cum_f", P), ("cum_b", P), ("before", P), ("eps", 4),
                    ("iota", 64), ("iota_neg", 8)):
        _CONST_COLS[name] = (at, n)
        at += n
    return at


NCONST = _const_layout()


def _constants():
    c = np.zeros((P, NCONST), np.float32)

    def put(name, v):
        a, n = _CONST_COLS[name]
        c[:, a:a + n] = v

    j, i = np.arange(P)[:, None], np.arange(P)[None, :]
    put("ident", j == i)
    put("ones", 1.0)
    put("one_over_d", 1.0 / D)
    put("one_over_p", 1.0 / P)
    put("swap", i == (j ^ 16))
    put("cum_f", j <= i)
    put("cum_b", j >= i)
    put("before", j < i)
    put("eps", np.array([LN_EPS, RMS_EPS, 1.0, 0.0]))
    put("iota", np.arange(64)[None, :])
    levels = []
    for s in (1, 2, 4, 8, 16, 32, 64):
        same = (j // (2 * s)) == (i // (2 * s))
        levels.append(same & ((i // s) % 2 == 1) & ((j // s) % 2 == 0))
    levels += [m.T for m in levels]
    masks = np.stack(levels, 1).reshape(P, 14 * P).astype(np.float32)
    p = np.arange(P)
    inv = np.float32(10000.0) ** (-np.arange(0, 32, 2, dtype=np.float32) / np.float32(32))
    tok = np.arange(T)
    pos = np.where(((p % 64) // 32 == 0)[:, None], (tok // GRID_W)[None, :], (tok % GRID_W)[None, :])
    ang = pos.astype(np.float32) * inv.astype(np.float32)[p % 16][:, None]
    sign = np.where(p % 32 < 16, -1.0, 1.0)[:, None]
    rope = np.concatenate([np.cos(ang), sign * np.sin(ang)], 1).astype(np.float32)
    a = 2 * np.pi * (np.outer(np.arange(P), np.arange(P)) % P) / P
    cs = np.concatenate([np.cos(a), np.sin(a)], 1) / math.sqrt(T * P)
    a = 2 * np.pi * (np.outer(np.arange(T), np.arange(T)) % T) / T
    fl = np.stack([np.cos(a), -np.sin(a)]).reshape(2, NT, P, T).transpose(2, 0, 1, 3).reshape(P, -1)
    ph = 2 * np.pi * (np.outer(2 * np.arange(T) + 1, np.arange(T)) % (4 * T)) / (4 * T)
    fwd = np.stack([np.cos(ph.T), np.sin(ph.T)]).reshape(2, NT, P, T).transpose(2, 0, 1, 3).reshape(P, -1)
    back = (np.stack([np.cos(ph), np.sin(ph)]) / T).reshape(2, NT, P, T).transpose(2, 0, 1, 3).reshape(P, -1)
    t = np.linspace(0.0, 1.0, T, dtype=np.float32)[:, None]
    w = (np.float32(2.0 * math.pi) * np.arange(T, dtype=np.float32)[:, None] / np.float32(T)).astype(np.float32)
    fb = np.linspace(1e-4, 15, 16, dtype=np.float32)[None, :]
    fw = (fb * w).astype(np.float32)
    z = np.concatenate([t, np.cos(fw), -np.sin(fw)], -1).T
    deltas = np.abs(np.linspace(math.log(1e-2) / 1.5, math.log(1e-2) / 0.3, D, dtype=np.float32))
    decay = np.exp(-t * deltas).reshape(NT, P, D).transpose(1, 0, 2).reshape(P, -1)
    out = {"const": c, "masks": masks, "rope": rope, "fm_cs": cs, "fm_l": fl, "hy_fwd": fwd,
           "hy_back": back, "hy_z": z, "hy_decay": decay}
    return {k: np.ascontiguousarray(v, dtype=np.float32) for k, v in out.items()}


class Core:

    def __init__(self, nc, d, stack):
        self.nc, self.d = nc, d
        self.stack = stack
        parts = (("fixed", 0, RING0), ("ring", RING0, W0), ("work", W0, ARENA))
        with ExitStack() as names:
            self.typed = {n: names.enter_context(nc.sbuf_tensor(n + "_rounded", [P, b - a], F32R)) for n, a, b in parts}
        self.areas = [(a, b, stack.enter_context(nc.sbuf_tensor(n, [P, b - a], F32))) for n, a, b in parts]
        self.ps = stack.enter_context(nc.psum_tensor("psum", [P, 8, 512], F32))
        self.kept = {}
        self.stage_end = self.sem("stage_end")
        self.slab_in = [self.sem(f"slab_in{i}") for i in range(SLOTS)]
        self.slab_out = [self.sem(f"slab_out{i}") for i in range(SLOTS)]
        self.slabs = []
        self.arrivals = [0] * SLOTS
        self.norms = self.centred = 0
        self.x = self.view(X0, KD, T)
        self.h = self.view(H0, KD, T)
        self.hc = self.view(HC0, KD, TC)

    def shared(self, name, n):
        if name not in self.kept:
            self.kept[name] = [self.sem(name), 0]
        s, base = self.kept[name]
        self.kept[name][1] += n
        return s, base

    def sem(self, name):
        return self.stack.enter_context(self.nc.semaphore(name))

    def columns(self, at, n):
        for a, b, area in self.areas:
            if a <= at and at + n <= b:
                return area[:, at - a:at - a + n]

    def view(self, at, *dims):
        n = int(np.prod(dims))
        v = self.columns(at, n)
        if len(dims) == 1:
            return v
        names = "abcde"[:len(dims)]
        return v.rearrange(f"p ({' '.join(names)}) -> p {' '.join(names)}", **dict(zip(names[:-1], dims[:-1])))

    def rounded(self, v):
        return bass.AP(tensor=self.typed[v.tensor.name], offset=v.offset, ap=v.ap)

    def score(self, half):
        return self.ps.rearrange("p b n -> p (b n)")[:, 1024 * half:1024 * half + KEYS]

    def pair(self, bank, n):
        return self.ps.rearrange("p b n -> p (b n)")[:, 512 * bank:512 * bank + n]

    def const(self, name):
        a, n = _CONST_COLS[name]
        return self.columns(CONST0 + a, n)

    def eps(self, i):
        a = CONST0 + _CONST_COLS["eps"][0] + i
        return self.columns(a, 1)

    def par(self, name, m=0):
        a = PAR0 + PAR[name][0] + m
        return self.columns(a, 1)

    def pars(self, name):
        a, n = PAR[name]
        return self.columns(PAR0 + a, n)

    def ada(self, layer, what, m):
        a = ADA0 + 64 * layer + 8 * what + m
        return self.columns(a, 1)

    def slab(self, *loads):
        n = len(self.slabs)
        self.arrivals[n % SLOTS] += 16 * len(loads)
        self.slabs.append((loads, self.arrivals[n % SLOTS]))
        return n

    def slot(self, n, *dims):
        return self.view(RING0 + (n % SLOTS) * SLOT, *dims)

    def arrived(self, eng, n):
        eng.wait_ge(self.slab_in[n % SLOTS], self.slabs[n][1])

    def load_slab(self, sp, n):
        if n >= SLOTS:
            sp.wait_ge(self.slab_out[n % SLOTS], n // SLOTS)
        for (off, dims), src in self.slabs[n][0]:
            sp.dma_start(self.view(RING0 + (n % SLOTS) * SLOT + off, *dims), src)\
                .then_inc(self.slab_in[n % SLOTS], 16)

    def used(self, ins, n):
        ins.then_inc(self.slab_out[n % SLOTS], 1)


CONST0 = 0
PAR0 = CONST0 + NCONST
ADA0 = PAR0 + NPAR
X0 = ADA0 + 256
H0 = X0 + KD * T
HC0 = H0 + KD * T
RING0 = HC0 + KD * TC
W0 = RING0 + SLOTS * SLOT
ARENA = 53200
WORK = ARENA - W0


def k_slab(w, a, b):
    return ((0, (KD, b - a)), w[:, a:b].rearrange("(k p) n -> p k n", p=P))


def row_slab(w, a, b):
    return ((0, ((b - a) // P, D)), w[a:b, :].rearrange("(k p) n -> p k n", p=P))


class Stage:

    def __init__(self, core):
        self.c = core

    def tensor(self, pe): pass
    def scalar(self, act): pass
    def vector(self, dve): pass
    def gpsimd(self, pool): pass
    def sync(self, sp): pass


class Load(Stage):

    def __init__(self, core):
        super().__init__(core)
        self.loaded, _ = core.shared("loaded", 64)

    def scalar(self, act):
        c, d = self.c, self.c.d
        act.dma_start(c.view(CONST0, NCONST), d["const"]).then_inc(self.loaded, 16)
        act.dma_start(c.view(PAR0, NPAR), d["vectors"]).then_inc(self.loaded, 16)
        act.wait_ge(self.loaded, 32)
        act.dma_start(c.x, d["x_t"].rearrange("(k p) t -> p k t", p=P)).then_inc(self.loaded, 16)
        act.dma_start(c.hc, d["ctx_t"].rearrange("(k p) t -> p k t", p=P)).then_inc(self.loaded, 16)
        a, _ = PAR["c"]
        v = c.view(PAR0 + a, 32)
        act.activation(v, v, ACT.Silu)


class Loaded(Stage):

    def scalar(self, act):
        act.wait_ge(self.c.shared("loaded", 0)[0], 64)


class LoadContext(Stage):

    def __init__(self, core):
        super().__init__(core)
        self.loaded, self.base = core.shared("loaded", 16)

    def scalar(self, act):
        act.dma_start(self.c.hc, self.c.d["ctx2_t"].rearrange("(k p) t -> p k t", p=P)).then_inc(self.loaded, 16)
        act.wait_ge(self.loaded, self.base + 16)


class Modulation(Stage):

    def __init__(self, core, layer, w, bias, cond, cond_ctx, acc=None, slabs=(0, 12)):
        super().__init__(core)
        self.layer, self.bias, self.w = layer, bias, w
        self.acc = W0 if acc is None else acc
        self.first, self.slabs = slabs[0], slabs[1] - slabs[0]
        self.jobs = [[(cond, 4 * s)] + ([(cond_ctx, 48 + 4 * s)] if cond_ctx and s < 4 else []) for s in range(*slabs)]
        self.n = []
        if acc is None:
            for s in range(self.slabs):
                self.add_slab()
        self.summed, self.base = core.shared("mod_summed", self.before(self.slabs))
        self.turned, _ = core.shared("mod_turned", self.before(self.slabs))

    def add_slab(self):
        s = self.first + len(self.n)
        self.n.append(self.c.slab(k_slab(self.w, 512 * s, 512 * s + 512)))

    def before(self, s):
        return sum(len(x) for x in self.jobs[:s])

    def vector_slab(self, dve, s):
        c = self.c
        w = c.slot(self.n[s], KD, 512)
        c.arrived(dve, self.n[s])
        q = self.before(s)
        pairs = []
        for i, (cond, _) in enumerate(self.jobs[s]):
            if q + i >= 4:
                dve.wait_ge(self.turned, self.base + q + i - 3)
            pairs.append((cond, c.view(self.acc + 512 * ((q + i) % 4), 512)))
        for cond, acc in pairs:
            dve.tensor_scalar(acc, w[:, 0, :], c.par(cond, 0), None, ALU.mult)
        for k in range(1, KD):
            dve.drain()
            for cond, acc in pairs:
                ins = dve.scalar_tensor_tensor(out=acc, in0=w[:, k, :], scalar=c.par(cond, k), in1=acc,
                                               op0=ALU.mult, op1=ALU.add)
                if k == KD - 1:
                    ins.then_inc(self.summed, 1)
        c.used(dve.drain(), self.n[s])

    def tensor_slab(self, pe, s):
        c = self.c
        q = self.before(s)
        for i, (_, col) in enumerate(self.jobs[s]):
            pe.wait_ge(self.summed, self.base + q + i + 1)
            for j in range(4):
                ins = pe.matmul(c.ps[:, 7, col + j:col + j + 1], c.view(self.acc + 512 * ((q + i) % 4) + 128 * j, P),
                                c.const("ones")[:, 0:1], start=True, stop=True)
            ins.then_inc(self.turned, 1)

    def finish(self, dve):
        c = self.c
        dve.wait_ge(self.turned, self.base + self.before(self.slabs))
        out = c.view(ADA0 + 64 * self.layer, 64)
        a, b = 4 * self.first, 4 * (self.first + self.slabs)
        dve.tensor_tensor(out[:, a:b], c.ps[:, 7, a:b], c.pars(self.bias)[:, a:b], ALU.add)
        contexts = len(self.jobs[0]) == 2
        if contexts:
            dve.tensor_tensor(out[:, 48:64], c.ps[:, 7, 48:64], c.pars(self.bias)[:, 0:16], ALU.add)
        dve.drain()
        for what in (1, 4) + ((7,) if contexts else ()):
            if what == 7 or a <= 8 * what < b:
                v = out[:, 8 * what:8 * what + 8]
                dve.tensor_scalar(v, v, 1.0, None, ALU.add)

    def vector(self, dve):
        for s in range(self.slabs):
            self.vector_slab(dve, s)
        self.finish(dve)

    def tensor(self, pe):
        for s in range(self.slabs):
            self.tensor_slab(pe, s)


class Gains(Stage):

    def __init__(self, core, layer, gain, what):
        super().__init__(core)
        self.args = layer, gain, what

    def vector(self, dve):
        layer, gain, what = self.args
        v = self.c.view(ADA0 + 64 * layer + 8 * what, 8)
        dve.tensor_tensor(v, v, self.c.pars(gain), ALU.mult)


class Norm(Stage):

    def __init__(self, core, src, dst, tokens, centre, scale, shift, scratch=None):
        super().__init__(core)
        self.scratch = W0 if scratch is None else scratch
        self.src, self.dst, self.t, self.centre = src, dst, tokens, centre
        self.scale, self.shift = scale, shift
        self.i, core.norms = core.norms, core.norms + 1
        if self.i == 0:
            core.norm_sems = {n: core.sem("norm_" + n) for n in
                              ("mean", "centred", "squared", "var", "std", "scaled")}
        self.s = core.norm_sems
        if centre:
            self.ic, core.centred = core.centred, core.centred + 1

    def tensor(self, pe):
        c, s, t = self.c, self.s, self.t
        if self.centre:
            for k in range(KD):
                ins = pe.matmul(c.ps[:, 0, 0:t], c.const("one_over_d"), self.src[:, k, :],
                                start=(k == 0), stop=(k == KD - 1))
            ins.then_inc(s["mean"], 1)
        for k in range(KD):
            pe.wait_ge(s["squared"], KD * self.i + k + 1)
            ins = pe.matmul(c.ps[:, 1, 0:t], c.const("one_over_d"), c.view(self.scratch + 512 * k, t),
                            start=(k == 0), stop=(k == KD - 1))
        ins.then_inc(s["var"], 1)

    def vector(self, dve):
        c, s, t = self.c, self.s, self.t
        if self.centre:
            dve.wait_ge(s["mean"], self.ic + 1)
            for k in range(KD):
                dve.tensor_tensor(self.dst[:, k, :], self.src[:, k, :], c.ps[:, 0, 0:t], ALU.subtract)\
                    .then_inc(s["centred"], 1)
        rstd = c.view(self.scratch + 512 * KD, t)
        dve.wait_ge(s["std"], self.i + 1)
        dve.reciprocal(rstd, rstd)
        dve.drain()
        src = self.dst if self.centre else self.src
        for k in range(KD):
            dve.tensor_tensor(self.dst[:, k, :], src[:, k, :], rstd, ALU.mult).then_inc(s["scaled"], 1)

    def scalar(self, act):
        c, s, t = self.c, self.s, self.t
        src = self.dst if self.centre else self.src
        for k in range(KD):
            if self.centre:
                act.wait_ge(s["centred"], KD * self.ic + k + 1)
            act.activation(c.view(self.scratch + 512 * k, t), src[:, k, :], ACT.Square).then_inc(s["squared"], 1)
        act.wait_ge(s["var"], self.i + 1)
        act.activation(c.view(self.scratch + 512 * KD, t), c.ps[:, 1, 0:t], ACT.Sqrt,
                       bias=c.eps(0 if self.centre else 1)).then_inc(s["std"], 1)
        for k in range(KD):
            act.wait_ge(s["scaled"], KD * self.i + k + 1)
            v = self.dst[:, k, :]
            if self.shift is None:
                act.activation(v, v, ACT.Copy, scale=self.scale(k))
            else:
                act.activation(v, v, ACT.Identity, scale=self.scale(k), bias=self.shift(k))


UNITS = 3


def high(c, dve, out, v):
    return dve.tensor_copy(c.rounded(out), v)


def low(c, eng, v, v_high):
    return eng.tensor_tensor(c.rounded(v), v, c.rounded(v_high), ALU.subtract)


def three(c, pe, out, w_high, w_low, x_high, x_low, start, stop):
    for i, (w, x) in enumerate(((w_high, x_high), (w_high, x_low), (w_low, x_high))):
        ins = pe.matmul(out, c.rounded(w), c.rounded(x), start=(start and i == 0), stop=(stop and i == 2))
    return ins


class Parts:

    def __init__(self, core, room, src, count):
        self.c, self.src = core, src
        self.src_high, self.ring = core.view(room, KD, T), room + KD * T
        self.cut, self.cut0 = core.shared("parts_cut", KD)
        self.made, self.made0 = core.shared("parts_high", count)
        self.low, self.low0 = core.shared("parts_low", count)

    def unit_high(self, u):
        return self.c.view(self.ring + KD * P * (u % UNITS), KD, P)

    def cut_source(self, dve):
        for k in range(KD):
            high(self.c, dve, self.src_high[:, k, :], self.src[:, k, :])
            dve.drain()
            low(self.c, dve, self.src[:, k, :], self.src_high[:, k, :]).then_inc(self.cut, 1)

    def make_high(self, dve, u, w, full, done):
        if u >= UNITS:
            dve.wait_ge(full, done + u - UNITS + 1)
        high(self.c, dve, self.unit_high(u), w).then_inc(self.made, 1)

    def make_low(self, pool, u, w):
        pool.wait_ge(self.made, self.made0 + u + 1)
        low(self.c, pool, w, self.unit_high(u)).then_inc(self.low, 1)

    def product(self, pe, out, u, w):
        pe.wait_ge(self.low, self.low0 + u + 1)
        for k in range(KD):
            if u == 0:
                pe.wait_ge(self.cut, self.cut0 + k + 1)
            ins = three(self.c, pe, out, self.unit_high(u)[:, k, :], w[:, k, :], self.src_high[:, k, :], self.src[:, k, :],
                        k == 0, k == KD - 1)
        return ins


class Project(Stage):

    def __init__(self, core, w, src, gate, keep, room):
        super().__init__(core)
        self.gate, self.keep = gate, keep
        self.n = [core.slab(k_slab(w, 512 * s, 512 * s + 512)) for s in range(2)]
        self.full, self.base = core.shared("tile_full", KD)
        self.parts = Parts(core, room, src, KD)

    def unit(self, m):
        return self.c.slot(self.n[m // 4], KD, 512)[:, :, P * (m % 4):P * (m % 4) + P]

    def tensor(self, pe):
        c = self.c
        for m in range(KD):
            self.parts.product(pe, c.ps[:, m, :], m, self.unit(m)).then_inc(self.full, 1)
            if m % 4 == 3:
                c.used(pe.drain(), self.n[m // 4])

    def gpsimd(self, pool):
        for m in range(KD):
            self.parts.make_low(pool, m, self.unit(m))

    def vector(self, dve):
        c = self.c

        def make_high(m):
            if m < KD:
                if m % 4 == 0:
                    c.arrived(dve, self.n[m // 4])
                self.parts.make_high(dve, m, self.unit(m), self.full, self.base)

        for m in range(UNITS):
            make_high(m)
        self.parts.cut_source(dve)
        if self.keep != 1.0:
            dve.tensor_scalar(c.x, c.x, self.keep, None, ALU.mult)
            dve.drain()
        for m in range(KD):
            dve.wait_ge(self.full, self.base + m + 1)
            make_high(m + UNITS)
            dve.scalar_tensor_tensor(out=c.x[:, m, :], in0=c.ps[:, m, :], scalar=self.gate(m),
                                     in1=c.x[:, m, :], op0=ALU.mult, op1=ALU.add)



A_Q = W0
A_K = A_Q + HEADS * T
A_V = A_K + HEADS * KEYS
A_F = A_V + NTA * 512
A_ROPE = A_F + 4 * T
A_RAW = A_ROPE + 2 * T
A_TMP = A_RAW + 2 * T
A_P = A_TMP + 2 * T
A_PT = A_P + 2 * KEYS
A_SMALL = A_PT + NTA * T
A_P2 = A_SMALL + 64
A_MIX = H0


class AttentionIn(Stage):
    BESIDE = [2, 5, 8, 13, 15, 18, 19, 20]

    def __init__(self, core, side):
        super().__init__(core)
        self.side = side
        w = core.d["da_w_in"][0]
        self.n = []
        for s in range(4):
            self.n.append(core.slab(k_slab(w, 512 * s, 512 * s + 512)))
            for _ in range((1, 2, 2, 3)[s]):
                side.add_slab()
        self.rope_in, self.swapped, self.table = core.sem("rope_in"), core.sem("rope_swapped"), core.sem("rope_table")
        self.tiles = [("q", m) for m in range(4)] + [("k", m) for m in range(4)] + [("kc", m) for m in range(4)]
        self.tiles += [("v", t) for t in range(NTA)] + [("f", m) for m in range(4)]
        self.full, self.base = core.shared("tile_full", len(self.tiles))
        self.free, self.freed = core.shared("tile_used", len(self.tiles))

    def tensor(self, pe):
        c = self.c

        def swap(r):
            pe.wait_ge(self.rope_in, r + 1)
            pe.matmul(c.ps[:, 4 + r % 2, :], c.const("swap"), c.view(A_RAW + 512 * (r % 2), T),
                      start=True, stop=True).then_inc(self.swapped, 1)

        for i, (kind, m) in enumerate(self.tiles):
            n = self.n["q k v f".split().index(kind[0])]
            c.arrived(pe, n)
            w = c.slot(n, KD, 512)
            if i >= 4:
                pe.wait_ge(self.free, self.freed + i - 3)
            for k in range(KD):
                if kind == "v":
                    src = c.hc[:, k, P * m:P * m + P] if m < NTC else c.h[:, k, P * (m - NTC):P * (m - NTC) + P]
                    out, lhs, rhs = c.ps[:, i % 4, :], src, w[:, k, :]
                else:
                    rhs = c.hc[:, k, :] if kind == "kc" else c.h[:, k, :]
                    out, lhs = c.ps[:, i % 4, 0:rhs.shape[1]], w[:, k, P * m:P * m + P]
                ins = pe.matmul(out, lhs, rhs, start=(k == 0), stop=(k == KD - 1))
            ins.then_inc(self.full, 1)
            if (kind, m) in (("q", 3), ("kc", 3), ("v", NTA - 1), ("f", 3)):
                c.used(pe.drain(), n)
            if 1 <= i <= 8:
                swap(i - 1)
            if i - 3 in self.BESIDE:
                self.side.tensor_slab(pe, self.BESIDE.index(i - 3))
        for k in (6, 7):
            self.side.tensor_slab(pe, k)

    def scalar(self, act):
        c = self.c
        act.dma_start(c.view(A_ROPE, 2 * T), c.d["rope"]).then_inc(self.table, 16)
        lam_in = c.shared("att_lam_in", 64)[0]
        for i, n in enumerate(("da_lam_q1", "da_lam_k1", "da_lam_q2", "da_lam_k2")):
            act.dma_start(c.view(A_SMALL, 4)[0:64, i:i + 1], c.d[n].rearrange("a (p b) -> (a p) b", b=1)).then_inc(lam_in, 16)

    def vector(self, dve):
        c = self.c
        cos, sin = c.view(A_ROPE, T), c.view(A_ROPE + T, T)
        dve.wait_ge(self.table, 16)

        def rotate(r):
            m = r % 4
            dst = c.view(A_Q + T * m, T) if r < 4 else c.view(A_K + KEYS * m + TC, T)
            tmp = c.view(A_TMP + 512 * (r % 2), T)
            dve.wait_ge(self.swapped, r + 1)
            dve.tensor_tensor(tmp, c.ps[:, 4 + r % 2, :], sin, ALU.mult)
            dve.tensor_tensor(dst, c.view(A_RAW + 512 * (r % 2), T), cos, ALU.mult)
            dve.drain()
            dve.tensor_tensor(dst, dst, tmp, ALU.add)

        for i, (kind, m) in enumerate(self.tiles):
            dve.wait_ge(self.full, self.base + i + 1)
            ps = c.ps[:, i % 4, :]
            if kind in ("q", "k"):
                if i >= 2:
                    dve.drain()
                dve.tensor_copy(c.view(A_RAW + 512 * (i % 2), T), ps).then_inc(self.free, 1)
                dve.drain().then_inc(self.rope_in, 1)
            elif kind == "kc":
                dve.tensor_copy(c.view(A_K + KEYS * m, TC), ps[:, 0:TC]).then_inc(self.free, 1)
            elif kind == "v":
                dve.tensor_copy(c.view(A_V + 512 * m, 512), ps).then_inc(self.free, 1)
            else:
                dve.tensor_copy(c.view(A_F + T * m, T), ps).then_inc(self.free, 1)
            if 1 <= i <= 8:
                rotate(i - 1)
            if i in self.BESIDE:
                self.side.vector_slab(dve, self.BESIDE.index(i))
        self.side.finish(dve)


class Attention(Stage):

    def __init__(self, core):
        super().__init__(core)
        self.lam_in = core.shared("att_lam_in", 0)[0]
        (self.lam_prod, self.lam_sum, self.lam_exp, self.scores, self.negmax, self.exp,
         self.probs, self.turned, self.copied, self.out, self.square, self.ms, self.std, self.out_used) = (
            core.sem("att_" + n) for n in ("lam_prod", "lam_sum", "lam_exp", "scores", "negmax",
                "exp", "probs", "turned", "copied", "out", "square", "ms", "std", "out_used"))
        self.lam4 = core.view(A_SMALL, 4)
        self.lamp = core.view(A_SMALL + 4, 2)
        self.lame = core.view(A_SMALL + 6, 2)
        self.lamc = core.view(A_SMALL + 8, 1)
        self.mx = core.view(A_SMALL + 10, 2)
        self.nm = core.view(A_SMALL + 12, 2)
        self.sm = core.view(A_SMALL + 14, 2)
        self.gain = core.view(A_SMALL + 16, 1)

    def e(self, i, half):
        return self.c.view((A_P, A_P2)[i % 2] + KEYS * half, KEYS)

    def make_scores(self, pe, i):
        c = self.c
        h, t = i // NT, i % NT
        if i >= 1:
            pe.wait_ge(self.exp, i)
        for half in range(2):
            q = c.view(A_Q + T * h + P * t, P)[64 * half:64 * half + 64, :]
            k = c.view(A_K + KEYS * h, KEYS)[64 * half:64 * half + 64, :]
            pe.matmul(c.ps[:, 2 * half, 0:512], q, k[:, 0:512], start=True, stop=True)
            ins = pe.matmul(c.ps[:, 2 * half + 1, 0:KEYS - 512], q, k[:, 512:KEYS], start=True, stop=True)
        ins.then_inc(self.scores, 1)

    def exponentials(self, act, i):
        act.wait_ge(self.negmax, i + 1)
        if i >= 2:
            act.wait_ge(self.turned, i - 1)
        for half in range(2):
            act.activation(self.e(i, half), self.c.score(half), ACT.Exp, bias=self.nm[:, half:half + 1],
                           scale=64 ** -0.5, accum_out=self.sm[:, half:half + 1])
        act.drain().then_inc(self.exp, 1)

    def maxima(self, dve, i):
        dve.wait_ge(self.scores, i + 1)
        for half in range(2):
            dve.tensor_reduce(self.mx[:, half:half + 1], self.c.score(half), AX.X, ALU.max)
        dve.drain()
        dve.tensor_scalar(self.nm, self.mx, -(64 ** -0.5), None, ALU.mult).then_inc(self.negmax, 1)

    def tensor(self, pe):
        c = self.c
        pe.wait_ge(self.lam_prod, 1)
        pe.matmul(c.ps[:, 7, 0:2], c.const("ones")[0:64, :], self.lamp[0:64, :], start=True, stop=True)\
            .then_inc(self.lam_sum, 1)
        pe.wait_ge(self.lam_exp, 1)
        self.make_scores(pe, 0)
        for h in range(HEADS):
            for t in range(NT):
                i = NT * h + t
                if i + 1 < HEADS * NT:
                    self.make_scores(pe, i + 1)
                pe.wait_ge(self.probs, i + 1)
                if i >= 1:
                    pe.wait_ge(self.copied, i)
                for kt in range(NTA):
                    ins = pe.transpose(c.ps[:, 4 + kt // 4, P * (kt % 4):P * (kt % 4) + P],
                                       self.e(i, 0)[:, P * kt:P * kt + P], c.const("ident"))
                ins.then_inc(self.turned, 1)
            pe.wait_ge(self.copied, NT * (h + 1))
            if h >= 1:
                pe.wait_ge(self.out_used, h)
            for kt in range(NTA):
                ins = pe.matmul(c.ps[:, 6, :], c.view(A_V + 512 * kt + P * h, P), c.view(A_PT + T * kt, T),
                                start=(kt == 0), stop=(kt == NTA - 1))
            ins.then_inc(self.out, 1)
            pe.wait_ge(self.square, h + 1)
            pe.matmul(c.ps[:, 7, :], c.const("one_over_p"), c.view(A_TMP, T), start=True, stop=True)\
                .then_inc(self.ms, 1)

    def scalar(self, act):
        c = self.c
        act.wait_ge(self.lam_sum, 1)
        act.activation(self.lame, c.ps[:, 7, 0:2], ACT.Exp).then_inc(self.lam_exp, 1)
        self.exponentials(act, 0)
        for h in range(HEADS):
            for t in range(NT):
                i = NT * h + t
                act.wait_ge(self.turned, i + 1)
                for kt in range(NTA):
                    act.activation(c.view(A_PT + T * kt + P * t, P),
                                   c.ps[:, 4 + kt // 4, P * (kt % 4):P * (kt % 4) + P], ACT.Copy)
                act.drain().then_inc(self.copied, 1)
                if i + 1 < HEADS * NT:
                    self.exponentials(act, i + 1)
            act.wait_ge(self.out, h + 1)
            act.activation(c.view(A_TMP, T), c.ps[:, 6, :], ACT.Square).then_inc(self.square, 1)
            act.wait_ge(self.ms, h + 1)
            act.activation(c.view(A_TMP + T, T), c.ps[:, 7, :], ACT.Sqrt, bias=c.eps(0)).then_inc(self.std, 1)

    def vector(self, dve):
        c = self.c
        dve.wait_ge(self.lam_in, 64)
        l4 = self.lam4[0:64, :].rearrange("p (a b) -> p a b", b=2)
        dve.tensor_tensor(self.lamp[0:64, :], l4[:, :, 0], l4[:, :, 1], ALU.mult).then_inc(self.lam_prod, 1)
        dve.tensor_scalar(self.gain, c.par("da_subln_g"), 1.0 - LAM_INIT, None, ALU.mult)
        dve.wait_ge(self.lam_exp, 1)
        dve.tensor_tensor(self.lamc, self.lame[:, 0:1], self.lame[:, 1:2], ALU.subtract)
        dve.drain()
        dve.tensor_scalar(self.lamc, self.lamc, LAM_INIT, None, ALU.add)
        dve.drain()
        self.maxima(dve, 0)
        for h in range(HEADS):
            for t in range(NT):
                i = NT * h + t
                dve.wait_ge(self.exp, i + 1)
                dve.reciprocal(self.sm, self.sm)
                dve.drain()
                dve.tensor_tensor(self.sm[:, 1:2], self.sm[:, 1:2], self.lamc, ALU.mult)
                dve.drain()
                e1, e2 = self.e(i, 0), self.e(i, 1)
                dve.tensor_scalar(e2, e2, self.sm[:, 1:2], None, ALU.mult)
                dve.drain()
                dve.scalar_tensor_tensor(out=e1, in0=e1, scalar=self.sm[:, 0:1], in1=e2,
                                         op0=ALU.mult, op1=ALU.subtract)
                dve.drain().then_inc(self.probs, 1)
                if i + 1 < HEADS * NT:
                    self.maxima(dve, i + 1)
            rstd = c.view(A_TMP + T, T)
            dve.wait_ge(self.std, h + 1)
            dve.reciprocal(rstd, rstd)
            dve.drain()
            dst = c.view(A_MIX + T * h, T)
            dve.tensor_tensor(dst, c.ps[:, 6, :], rstd, ALU.mult)
            dve.drain()
            dve.tensor_scalar(dst, dst, self.gain, None, ALU.mult).then_inc(self.out_used, 1)


class FourierMix(Stage):

    def __init__(self, core):
        super().__init__(core)
        self.table, self.full, self.free, self.done = (core.sem("fm_" + n) for n in ("table", "full", "free", "done"))
        self.cs = core.view(A_Q, 256)
        self.ab = core.view(A_K, NT, 4, 256)
        self.l = core.view(A_ROPE, 2, NT, T)

    def scalar(self, act):
        act.dma_start(self.cs, self.c.d["fm_cs"]).then_inc(self.table, 16)
        act.dma_start(self.l, self.c.d["fm_l"].rearrange("p (a b t) -> p a b t", a=2, b=NT)).then_inc(self.table, 16)

    def tensor(self, pe):
        c = self.c
        pe.wait_ge(self.table, 32)
        for i in range(16):
            g, t = i // NT, i % NT
            if i >= 4:
                pe.wait_ge(self.free, i - 3)
            pe.matmul(c.ps[:, i % 4, 0:256], c.view(A_F + T * g + P * t, P), self.cs, start=True, stop=True)\
                .then_inc(self.full, 1)
        pe.wait_ge(self.free, 16)
        for g in range(4):
            for t in range(NT):
                for part in range(2):
                    ins = pe.matmul(c.ps[:, 4 + g, :], self.ab[:, t, g, P * part:P * part + P], self.l[:, part, t, :],
                                    start=(t + part == 0), stop=(t == NT - 1 and part == 1))
            ins.then_inc(self.done, 1)

    def vector(self, dve):
        c = self.c
        for i in range(16):
            g, t = i // NT, i % NT
            dve.wait_ge(self.full, i + 1)
            dve.tensor_copy(self.ab[:, t, g, :], c.ps[:, i % 4, 0:256]).then_inc(self.free, 1)
        for g in range(4):
            dve.wait_ge(self.done, g + 1)
            dve.tensor_copy(c.view(A_MIX + T * (4 + g), T), c.ps[:, 4 + g, :])



F_ACT = W0
F_BUF = F_ACT + NF * T
F_ACC = F_BUF + 4 * T
F_PARTS = F_ACC + 4 * T


def conv3(dve, out, u, w0, w2, n):
    dve.scalar_tensor_tensor(out=out[:, 1:n], in0=u[:, 0:n - 1], scalar=w0, in1=out[:, 1:n],
                             op0=ALU.mult, op1=ALU.add)
    dve.drain()
    return dve.scalar_tensor_tensor(out=out[:, 0:n - 1], in0=u[:, 1:n], scalar=w2, in1=out[:, 0:n - 1],
                                    op0=ALU.mult, op1=ALU.add)


class FfnIn(Stage):

    def __init__(self, core, i, side):
        super().__init__(core)
        self.i, self.side = i, side
        w = core.d["ffn_w_in"][i]
        self.n = []
        self.beside = [[s + 1] for s in range(9)] + [[10, 11], []]
        side.add_slab()
        for s in range(NF // 2):
            self.n.append(core.slab(*[
                ((half * KD * 256, (KD, 256)),
                 w[:, FFN * half + 256 * s:FFN * half + 256 * s + 256].rearrange("(k p) n -> p k n", p=P))
                for half in range(2)]))
            for _ in self.beside[s]:
                side.add_slab()
        self.tiles = [(s, q) for s in range(NF // 2) for q in range(4)]
        self.full, self.full0 = core.shared("tile_full", 2 * NF)
        self.centre, self.centre0 = core.shared("tile_centre", 2 * NF)
        self.conv, self.conv0 = core.shared("tile_used", 2 * NF)
        self.gelu, self.gelu0 = core.shared("gelu", NF)
        self.parts = Parts(core, F_PARTS, core.h, 2 * NF)

    def unit(self, j):
        s, q = self.tiles[j]
        return self.c.slot(self.n[s], 2, KD, 256)[:, q // 2, :, P * (q % 2):P * (q % 2) + P]

    def tensor(self, pe):
        c = self.c
        for j, (s, q) in enumerate(self.tiles):
            n = self.n[s]
            if j >= 7:
                pe.wait_ge(self.conv, self.conv0 + j - 6)
            self.parts.product(pe, c.ps[:, j % 7, :], j, self.unit(j)).then_inc(self.full, 1)
            if q == 2 and s:
                for q_side in ([0] if s == 1 else []) + self.beside[s - 1]:
                    self.side.tensor_slab(pe, q_side)
            if q == 3:
                c.used(pe.drain(), n)

    def scalar(self, act):
        c, i = self.c, self.i
        for j, (s, q) in enumerate(self.tiles):
            m = 2 * s + q % 2 + NF * (q // 2)
            act.wait_ge(self.full, self.full0 + j + 1)
            if j >= 4:
                act.wait_ge(self.conv, self.conv0 + j - 3)
            if s and q < 2:
                act.wait_ge(self.gelu, self.gelu0 + 2 * s - 1 + q)
            buf = c.view(F_BUF + T * q, T)
            act.activation(buf, c.ps[:, j % 7, :], ACT.Identity, scale=c.par(f"ffn_conv_w{i}1", m),
                           bias=c.par(f"ffn_conv_b{i}", m)).then_inc(self.centre, 1)
            if q >= 2:
                a = 4 * s + q - 2
                act.wait_ge(self.conv, self.conv0 + a + 1)
                act.activation(c.view(F_ACT + T * (2 * s + q - 2), T), c.view(F_BUF + T * (q - 2), T), ACT.Gelu)\
                    .then_inc(self.gelu, 1)

    def gpsimd(self, pool):
        for j in range(2 * NF):
            self.parts.make_low(pool, j, self.unit(j))

    def vector(self, dve):
        c, i = self.c, self.i

        def make_high(j):
            if j < 2 * NF:
                if j % 4 == 0:
                    c.arrived(dve, self.n[j // 4])
                self.parts.make_high(dve, j, self.unit(j), self.full, self.full0)

        for j in range(UNITS):
            make_high(j)
        self.parts.cut_source(dve)
        self.side.vector_slab(dve, 0)
        for j, (s, q) in enumerate(self.tiles):
            m = 2 * s + q % 2 + NF * (q // 2)
            make_high(j + UNITS)
            dve.wait_ge(self.centre, self.centre0 + j + 1)
            buf = c.view(F_BUF + T * q, T)
            ins = conv3(dve, buf, c.ps[:, j % 7, :], c.par(f"ffn_conv_w{i}0", m), c.par(f"ffn_conv_w{i}2", m), T)
            if q >= 2:
                g = 2 * s + q - 2
                dve.wait_ge(self.gelu, self.gelu0 + g + 1)
                dve.drain()
                dst = c.view(F_ACT + T * g, T)
                ins = dve.tensor_tensor(dst, dst, buf, ALU.mult)
            ins.then_inc(self.conv, 1)
            if q == 3:
                for n in self.beside[s]:
                    self.side.vector_slab(dve, n)
        self.side.finish(dve)


class FfnOut(Stage):

    def __init__(self, core, i, gate):
        super().__init__(core)
        self.gate = gate
        w = core.d["ffn_w_out"][i]
        self.n = [core.slab(row_slab(w, 512 * s, min(512 * s + 512, FFN))) for s in range(6)]
        self.full, self.base = core.shared("tile_full", KD)
        self.cut, self.cut0 = core.shared("parts_cut", NF)
        self.low, self.low0 = core.shared("parts_low", NF)
        self.made, self.made0 = core.shared("parts_high", NF)
        self.free, self.free0 = core.shared("parts_free", NF - 1)

    def row(self, kt):
        return self.c.slot(self.n[kt // 4], 4, D)[:, kt % 4, :]

    def row_high(self, kt):
        return self.c.view(F_BUF + D * (kt % UNITS), D)

    def src(self, kt):
        return self.c.view(F_ACT + T * kt, T)

    def src_high(self, kt):
        return self.c.view(F_BUF + D * UNITS + T * (kt % UNITS), T)

    def gpsimd(self, pool):
        for kt in range(NF):
            pool.wait_ge(self.made, self.made0 + kt + 1)
            low(self.c, pool, self.row(kt), self.row_high(kt)).then_inc(self.low, 1)

    def tensor(self, pe):
        c = self.c
        for kt in range(NF):
            pe.wait_ge(self.cut, self.cut0 + kt + 1)
            pe.wait_ge(self.low, self.low0 + kt + 1)
            for m in range(KD):
                cols = slice(P * m, P * m + P)
                ins = three(c, pe, c.ps[:, m, :], self.row_high(kt)[:, cols], self.row(kt)[:, cols],
                            self.src_high(kt), self.src(kt), kt == 0, kt == NF - 1)
                if kt == NF - 1:
                    ins.then_inc(self.full, 1)
            if kt < NF - 1:
                ins.then_inc(self.free, 1)
            if kt % 4 == 3 or kt == NF - 1:
                c.used(pe.drain(), self.n[kt // 4])

    def vector(self, dve):
        c = self.c
        for kt in range(NF):
            if kt % 4 == 0:
                c.arrived(dve, self.n[kt // 4])
            if kt >= UNITS:
                dve.wait_ge(self.free, self.free0 + kt - UNITS + 1)
            high(c, dve, self.row_high(kt), self.row(kt)).then_inc(self.made, 1)
            high(c, dve, self.src_high(kt), self.src(kt))
            dve.drain()
            low(c, dve, self.src(kt), self.src_high(kt)).then_inc(self.cut, 1)
        dve.tensor_scalar(c.x, c.x, ALPHA, None, ALU.mult)
        dve.drain()
        for m in range(KD):
            dve.wait_ge(self.full, self.base + m + 1)
            dve.scalar_tensor_tensor(out=c.x[:, m, :], in0=c.ps[:, m, :], scalar=self.gate(m),
                                     in1=c.x[:, m, :], op0=ALU.mult, op1=ALU.add)



Y_K = W0
Y_TAB = Y_K + 2 * NT * D
Y_HF = Y_TAB + 2 * NT * T
Y_HB = Y_HF + NT * D
Y_VT = H0
Y_BUF = Y_HB + NT * D
Y_ACC = Y_BUF + 2 * T
Y_HID = H0
TWO_PI_HI = 6.28125
TWO_PI_LO = 2 * math.pi - 6.28125
ROUND = 1.5 * 2.0 ** 23


class HyenaFilter(Stage):

    def __init__(self, core):
        super().__init__(core)
        (self.inputs, self.tables, self.lin, self.reduced, self.sine, self.raw, self.windowed,
         self.absolute, self.summed, self.sumdiff, self.spec, self.spec_out) = (
            core.sem("hyf_" + n) for n in ("inputs", "tables", "lin", "reduced", "sine", "raw", "windowed",
                "absolute", "summed", "sumdiff", "spec", "spec_out"))
        o = Y_HID
        self.z = core.view(o, T); o += T
        self.w1 = core.view(o, HID); o += HID
        self.w23 = core.view(o, 2, HID); o += 2 * HID
        self.vec = core.view(o, 4); o += 4
        self.arg = core.view(o, T); o += T
        self.turns = core.view(o, T); o += T
        self.hid = core.view(o, T); o += T
        self.w4 = core.view(o, 2 * D); o += 2 * D
        self.decay = core.view(Y_K, NT, D)
        self.absum = core.view(Y_K + NT * D, NT, D)
        self.hf, self.hb = core.view(Y_HF, NT, D), core.view(Y_HB, NT, D)
        self.tab = core.view(Y_TAB, 2, NT, T)
        self.abs_b = core.view(o, D)
        core.hy_norm = core.view(ADA0 + 256 - 16, KD)
        self.k = core.view(Y_K, 2, NT, D)

    def scalar(self, act):
        c, d = self.c, self.c.d
        s = self.inputs
        act.dma_start(self.z[0:33, :], d["hy_z"]).then_inc(s, 16)
        act.dma_start(self.w1[0:33, :], d["hy_f_w1"][0]).then_inc(s, 16)
        act.dma_start(self.w23[0:HID, 0, :], d["hy_f_w2"][0]).then_inc(s, 16)
        act.dma_start(self.w23[0:HID, 1, :], d["hy_f_w3"][0]).then_inc(s, 16)
        act.dma_start(self.w4[0:HID, :], d["hy_f_w4"][0]).then_inc(s, 16)
        for i, n in enumerate(("hy_f_b1", "hy_f_b2", "hy_f_b3", "hy_f_freq")):
            act.dma_start(self.vec[0:HID, i:i + 1], d[n].rearrange("a (p b) -> (a p) b", b=1)).then_inc(s, 16)
        act.dma_start(self.decay, d["hy_decay"].rearrange("p (k n) -> p k n", k=NT)).then_inc(self.tables, 16)
        act.dma_start(self.tab, d["hy_fwd"].rearrange("p (a k n) -> p a k n", a=2, k=NT)).then_inc(self.tables, 16)
        for layer in range(3):
            act.wait_ge(self.reduced, layer + 1)
            act.activation(self.hid[0:HID, :], self.arg[0:HID, :], ACT.Sin).then_inc(self.sine, 1)
        for t in range(NT):
            act.wait_ge(self.windowed, 4 * (t + 1))
            act.activation(self.absum[:, t, :], self.hf[:, t, :], ACT.Abs)
            if t >= 1:
                act.wait_ge(self.summed, t)
            act.activation(self.abs_b, self.hb[:, t, :], ACT.Abs)
            act.drain().then_inc(self.absolute, 1)

    def vector(self, dve):
        c = self.c
        freq = self.vec[0:HID, 3:4]
        arg, turns = self.arg[0:HID, :], self.turns[0:HID, :]
        dve.wait_ge(self.inputs, 16 * 9)
        for layer in range(3):
            dve.wait_ge(self.lin, layer + 1)
            dve.tensor_scalar(arg, c.ps[0:HID, 0, :], self.vec[0:HID, layer:layer + 1], freq, ALU.add, ALU.mult)
            dve.drain()
            dve.tensor_scalar(turns, arg, 1.0 / (2 * math.pi), ROUND, ALU.mult, ALU.add)
            dve.drain()
            dve.tensor_scalar(turns, turns, -ROUND, None, ALU.add)
            dve.drain()
            dve.scalar_tensor_tensor(out=arg, in0=turns, scalar=-TWO_PI_HI, in1=arg, op0=ALU.mult, op1=ALU.add)
            dve.drain()
            dve.scalar_tensor_tensor(out=arg, in0=turns, scalar=-TWO_PI_LO, in1=arg, op0=ALU.mult, op1=ALU.add)
            dve.drain()
            dve.tensor_scalar(arg, arg, math.pi, -math.pi, ALU.min, ALU.max).then_inc(self.reduced, 1)
        dve.wait_ge(self.tables, 32)
        for t in range(NT):
            for q in range(4):
                i = 4 * t + q
                dst = (self.hf if q < 2 else self.hb)[:, t, 512 * (q % 2):512 * (q % 2) + 512]
                dve.wait_ge(self.raw, i + 1)
                ins = dve.tensor_tensor(dst, c.ps[:, i % 4, :], self.decay[:, t, 512 * (q % 2):512 * (q % 2) + 512],
                                        ALU.mult)
                if t == 0 and q >= 2:
                    dve.drain()
                    ins = dve.memset(dst[0:1, :], 0.0)
                ins.then_inc(self.windowed, 1)
        for t in range(NT):
            dve.wait_ge(self.absolute, t + 1)
            dve.tensor_tensor(self.absum[:, t, :], self.absum[:, t, :], self.abs_b, ALU.add)\
                .then_inc(self.summed, 1)
            s = c.view(Y_HID, D)
            dve.drain()
            dve.tensor_tensor(s, self.hf[:, t, :], self.hb[:, t, :], ALU.add)
            dve.tensor_tensor(self.hb[:, t, :], self.hb[:, t, :], self.hf[:, t, :], ALU.subtract)
            dve.drain()
            dve.tensor_copy(self.hf[:, t, :], s).then_inc(self.sumdiff, 1)
        dve.wait_ge(self.spec, 1)
        dve.reciprocal(c.hy_norm, c.ps[:, 7, 0:KD])
        for j in range(16):
            part, f, half = j // 8, j // 2 % 4, j % 2
            dve.wait_ge(self.spec, j + 2)
            dve.tensor_copy(self.k[:, part, f, 512 * half:512 * half + 512], c.ps[:, j % 4, :]).then_inc(self.spec_out, 1)

    def tensor(self, pe):
        c = self.c
        pe.wait_ge(self.inputs, 16 * 9)
        pe.matmul(c.ps[0:HID, 0, :], self.w1[0:33, :], self.z[0:33, :], start=True, stop=True).then_inc(self.lin, 1)
        for layer in range(2):
            pe.wait_ge(self.sine, layer + 1)
            pe.matmul(c.ps[0:HID, 0, :], self.w23[0:HID, layer, :], self.hid[0:HID, :], start=True, stop=True)\
                .then_inc(self.lin, 1)
        pe.wait_ge(self.sine, 3)
        for i in range(16):
            t, q = i // 4, i % 4
            if i >= 4:
                pe.wait_ge(self.windowed, i - 3)
            pe.matmul(c.ps[:, i % 4, :], self.hid[0:HID, P * t:P * t + P], self.w4[0:HID, 512 * q:512 * q + 512],
                      start=True, stop=True).then_inc(self.raw, 1)
        pe.wait_ge(self.summed, NT)
        for m in range(KD):
            for t in range(NT):
                ins = pe.matmul(c.ps[:, 7, m:m + 1], self.absum[:, t, P * m:P * m + P], c.const("ones")[:, 0:1],
                                start=(t == 0), stop=(t == NT - 1))
        ins.then_inc(self.spec, 1)
        pe.wait_ge(self.sumdiff, NT)
        for j in range(16):
            part, f, half = j // 8, j // 2 % 4, j % 2
            if j >= 4:
                pe.wait_ge(self.spec_out, j - 3)
            src = self.hf if part == 0 else self.hb
            for t in range(NT):
                ins = pe.matmul(c.ps[:, j % 4, :], self.tab[:, part, t, P * f:P * f + P],
                                src[:, t, 512 * half:512 * half + 512], start=(t == 0), stop=(t == NT - 1))
            ins.then_inc(self.spec, 1)


class HyenaIn(Stage):

    def __init__(self, core, side):
        super().__init__(core)
        self.side = side
        w = core.d["hy_w_in"][0]
        self.order = [m for part in (1, 2, 0) for m in range(8 * part, 8 * part + 8)]
        self.n = []
        side.add_slab()
        for s in range(6):
            self.n.append(core.slab(k_slab(w, P * self.order[4 * s], P * self.order[4 * s] + 512)))
            side.add_slab()
            if s < 5:
                side.add_slab()
        self.full, self.full0 = core.shared("tile_full", 24)
        self.centre, self.centre0 = core.shared("tile_centre", 24)
        self.conv, self.conv0 = core.shared("tile_used", 24)

    def dst(self, j):
        c = self.c
        if j < 8:
            return c.view(Y_HB + T * j, T)
        if j < 16:
            return c.view(Y_BUF + T * (j % 2), T)
        return c.view(Y_HF + T * (j - 16), T)

    def tensor(self, pe):
        c = self.c
        for j, m in enumerate(self.order):
            n = self.n[j // 4]
            if j % 4 == 0:
                c.arrived(pe, n)
            w = c.slot(n, KD, 512)
            if j >= 7:
                pe.wait_ge(self.conv, self.conv0 + j - 6)
            for k in range(KD):
                ins = pe.matmul(c.ps[:, j % 7, :], w[:, k, P * (j % 4):P * (j % 4) + P], c.h[:, k, :],
                                start=(k == 0), stop=(k == KD - 1))
            ins.then_inc(self.full, 1)
            if j % 4 == 3:
                c.used(pe.drain(), n)
            if j % 2 == 0 and j >= 4:
                self.side.tensor_slab(pe, j // 2 - 2)
        for s in (10, 11):
            self.side.tensor_slab(pe, s)

    def scalar(self, act):
        c = self.c
        for j, m in enumerate(self.order):
            act.wait_ge(self.full, self.full0 + j + 1)
            if 10 <= j < 16:
                act.wait_ge(self.conv, self.conv0 + j - 1)
            act.activation(self.dst(j), c.ps[:, j % 7, :], ACT.Identity, scale=c.par("hy_conv_w1", m),
                           bias=c.par("hy_conv_b", m)).then_inc(self.centre, 1)

    def vector(self, dve):
        c = self.c
        self.side.vector_slab(dve, 0)
        for j, m in enumerate(self.order):
            dve.wait_ge(self.centre, self.centre0 + j + 1)
            ins = conv3(dve, self.dst(j), c.ps[:, j % 7, :], c.par("hy_conv_w0", m), c.par("hy_conv_w2", m), T)
            if 8 <= j < 16:
                dve.drain()
                x1 = self.dst(j - 8)
                ins = dve.tensor_tensor(x1, x1, self.dst(j), ALU.mult)
            ins.then_inc(self.conv, 1)
            if j % 2 == 1 and j < 22:
                self.side.vector_slab(dve, j // 2 + 1)
        self.side.finish(dve)


class HyenaConv(Stage):

    def __init__(self, core):
        super().__init__(core)
        (self.table, self.turned, self.turned_out, self.spec, self.prod, self.y, self.y_out) = (
            core.sem("hyc_" + n) for n in ("table", "turned", "turned_out", "spec", "prod", "y", "y_out"))
        self.v, self.x0 = core.view(Y_HB, KD, T), core.view(Y_HF, KD, T)
        self.vt = core.view(Y_VT, NT, D)
        self.tab = core.view(Y_TAB, 2, NT, T)
        self.k = core.view(Y_K, 2, NT, D)
        core.mix = self.x0

    def scalar(self, act):
        act.wait_ge(self.prod, 8)
        act.dma_start(self.tab, self.c.d["hy_back"].rearrange("p (a k n) -> p a k n", a=2, k=NT)).then_inc(self.table, 16)

    def tensor(self, pe):
        c = self.c
        for i in range(8):
            t, half = i // 2, i % 2
            if i >= 4:
                pe.wait_ge(self.turned_out, i - 3)
            for m in range(4):
                ins = pe.transpose(c.ps[:, i % 4, P * m:P * m + P], self.v[:, 4 * half + m, P * t:P * t + P],
                                   c.const("ident"))
            ins.then_inc(self.turned, 1)
        pe.wait_ge(self.turned_out, 8)
        for i in range(8):
            f, half = i // 2, i % 2
            if i >= 2:
                pe.wait_ge(self.prod, i - 1)
            for part in range(2):
                for t in range(NT):
                    ins = pe.matmul(c.ps[:, 4 + 2 * (i % 2) + part, :], self.tab[:, part, t, P * f:P * f + P],
                                    self.vt[:, t, 512 * half:512 * half + 512], start=(t == 0), stop=(t == NT - 1))
            ins.then_inc(self.spec, 1)
        pe.wait_ge(self.table, 16)
        for m in range(KD):
            if m >= 4:
                pe.wait_ge(self.y_out, m - 3)
            for f in range(NT):
                for part in range(2):
                    ins = pe.matmul(c.ps[:, m % 4, :], self.k[:, part, f, P * m:P * m + P], self.tab[:, part, f, :],
                                    start=(f + part == 0), stop=(f == NT - 1 and part == 1))
            ins.then_inc(self.y, 1)

    def vector(self, dve):
        c = self.c
        for i in range(8):
            t, half = i // 2, i % 2
            dve.wait_ge(self.turned, i + 1)
            dve.tensor_copy(self.vt[:, t, 512 * half:512 * half + 512], c.ps[:, i % 4, :]).then_inc(self.turned_out, 1)
        t1, t2 = c.view(Y_BUF, T), c.view(Y_BUF + T, T)
        for i in range(8):
            f, half = i // 2, i % 2
            cols = slice(512 * half, 512 * half + 512)
            kre, kim = self.k[:, 0, f, cols], self.k[:, 1, f, cols]
            vre, vs = c.ps[:, 4 + 2 * (i % 2), :], c.ps[:, 5 + 2 * (i % 2), :]
            dve.wait_ge(self.spec, i + 1)
            dve.tensor_tensor(t1, kim, vs, ALU.mult)
            dve.tensor_tensor(t2, kim, vre, ALU.mult)
            dve.drain()
            dve.tensor_tensor(kim, kre, vs, ALU.mult)
            dve.tensor_tensor(kre, kre, vre, ALU.mult)
            dve.drain()
            dve.tensor_tensor(kre, kre, t1, ALU.add)
            dve.tensor_tensor(kim, kim, t2, ALU.subtract)
            dve.drain().then_inc(self.prod, 1)
        for m in range(KD):
            dve.wait_ge(self.y, m + 1)
            dve.tensor_scalar(t1, c.ps[:, m % 4, :], c.hy_norm[:, m:m + 1], None, ALU.mult)
            dve.drain()
            dve.scalar_tensor_tensor(out=t1, in0=self.v[:, m, :], scalar=c.par("hy_d", m), in1=t1,
                                     op0=ALU.mult, op1=ALU.add)
            dve.drain()
            dve.tensor_tensor(self.x0[:, m, :], self.x0[:, m, :], t1, ALU.mult).then_inc(self.y_out, 1)
            dve.drain()



B_U = W0
B_Y = B_U + KD * T
B_END = B_Y + KD * T


class ShortConv(Stage):

    def __init__(self, core):
        super().__init__(core)
        w = core.d["w_in_b_2"][0]
        self.order = [m for part in (1, 2, 0) for m in range(8 * part, 8 * part + 8)]
        self.n = [core.slab(k_slab(w, P * self.order[4 * s], P * self.order[4 * s] + 512)) for s in range(6)]
        self.full, self.full0 = core.shared("tile_full", 24)
        self.free, self.free0 = core.shared("tile_used", 24)
        self.parts = Parts(core, B_END, core.h, 24)

    def unit(self, j):
        return self.c.slot(self.n[j // 4], KD, 512)[:, :, P * (j % 4):P * (j % 4) + P]

    def tensor(self, pe):
        c = self.c
        for j, m in enumerate(self.order):
            if j >= 8:
                pe.wait_ge(self.free, self.free0 + j - 7)
            self.parts.product(pe, c.ps[:, j % 8, :], j, self.unit(j)).then_inc(self.full, 1)
            if j % 4 == 3:
                c.used(pe.drain(), self.n[j // 4])

    def gpsimd(self, pool):
        for j in range(24):
            self.parts.make_low(pool, j, self.unit(j))

    def vector(self, dve):
        c = self.c
        rows = T // GRID_W

        def make_high(j):
            if j < 24:
                if j % 4 == 0:
                    c.arrived(dve, self.n[j // 4])
                self.parts.make_high(dve, j, self.unit(j), self.full, self.full0)

        for j in range(UNITS):
            make_high(j)
        self.parts.cut_source(dve)
        for j in range(24):
            m = j % 8
            ps = c.ps[:, j % 8, :]
            u, y = c.view(B_U + T * m, T), c.view(B_Y + T * m, T)
            dve.wait_ge(self.full, self.full0 + j + 1)
            make_high(j + UNITS)
            if j < 8:
                dve.tensor_copy(u, ps).then_inc(self.free, 1)
                continue
            dve.drain()
            if j >= 16:
                dve.tensor_tensor(y, y, ps, ALU.mult).then_inc(self.free, 1)
                continue
            dve.tensor_tensor(u, u, ps, ALU.mult).then_inc(self.free, 1)
            dve.drain()
            dve.tensor_scalar(y, u, c.par("conv_b1", m), None, ALU.mult)
            for tap, name in ((-1, "conv_b0"), (1, "conv_b2")):
                dve.drain()
                if m < 4:
                    uv = u.rearrange("p (r g) -> p r g", r=rows)
                    yv = y.rearrange("p (r g) -> p r g", r=rows)
                    src = uv[:, :, 0:GRID_W - 1] if tap < 0 else uv[:, :, 1:GRID_W]
                    dst = yv[:, :, 1:GRID_W] if tap < 0 else yv[:, :, 0:GRID_W - 1]
                else:
                    src = u[:, 0:T - GRID_W] if tap < 0 else u[:, GRID_W:T]
                    dst = y[:, GRID_W:T] if tap < 0 else y[:, 0:T - GRID_W]
                dve.scalar_tensor_tensor(out=dst, in0=src, scalar=c.par(name, m), in1=dst,
                                         op0=ALU.mult, op1=ALU.add)



G_MASK = W0
G_GATE = G_MASK + 14 * P
G_G, G_BETA, G_GC = G_GATE, G_GATE + 96, G_GATE + 192
G_T1, G_T2 = G_GATE + 288, G_GATE + 384
G_ROW = G_GATE + 480
G_Z = G_GATE + 512
G_Q = G_Z + T
G_K = G_Q + T
G_V = G_K + KEYS
G_KT = G_V + KEYS
G_VT = G_KT + KEYS
G_COL = G_VT + KEYS
G_TAPS = G_COL + 60
G_S = G_COL + 72
G_O = G_S + 2 * 4 * P
G_LANE = G_O + T
L_T, L_A, L_KBG, L_M, L_L, L_TT = (KEYS * i for i in range(6))
L_QD, L_QK = 6 * KEYS, 6 * KEYS + T
LANE = 6 * KEYS + 2 * T
G_MIX = G_LANE + 2 * LANE
LEVELS = 7


class DeltaGates(Stage):

    def __init__(self, core):
        super().__init__(core)
        self.n = core.slab(k_slab(core.d["w_in_a_2"][0], 4 * D, 4 * D + 32))
        (self.rows, self.full, self.sigmoid, self.shifted, self.soft, self.gate, self.summed) = (
            core.sem("gate_" + n) for n in ("rows", "full", "sigmoid", "shifted", "soft", "gate", "summed"))
        v = core.view
        self.g, self.beta, self.gcum = v(G_G, NTA, 16), v(G_BETA, NTA, 16), v(G_GC, NTA, 16)
        self.t1, self.t2 = v(G_T1, NTA, 16), v(G_T2, NTA, 16)
        self.alog, self.dt = v(G_ROW, 16), v(G_ROW + 16, 16)

    def tensor(self, pe):
        c = self.c
        c.arrived(pe, self.n)
        w = c.slot(self.n, KD, 32)
        for t in range(NTA):
            for k in range(KD):
                src = c.hc[:, k, P * t:P * t + P] if t < NTC else c.h[:, k, P * (t - NTC):P * (t - NTC) + P]
                ins = pe.matmul(c.ps[:, 0, 32 * t:32 * t + 32], src, w[:, k, :], start=(k == 0), stop=(k == KD - 1))
        ins.then_inc(self.full, 1)
        c.used(pe.drain(), self.n)
        pe.wait_ge(self.gate, 1)
        pe.matmul(c.ps[:, 1, 0:96], c.const("cum_f"), c.view(G_G, 96), start=True, stop=True)
        pe.matmul(c.ps[:, 2, 0:96], c.const("cum_b"), c.view(G_G, 96), start=True, stop=True).then_inc(self.summed, 1)

    def scalar(self, act):
        c, d = self.c, self.c.d
        act.dma_start(self.alog, d["a_log_a_2"].rearrange("a b c -> (a b c)").partition_broadcast(P)).then_inc(self.rows, 16)
        act.dma_start(self.dt, d["dt_bias_a_2"].rearrange("a b c -> (a b c)").partition_broadcast(P)).then_inc(self.rows, 16)
        act.dma_start(c.view(G_MASK, 14 * P), d["masks"]).then_inc(self.rows, 16)
        act.wait_ge(self.rows, 48)
        act.activation(self.alog, self.alog, ACT.Exp)
        act.wait_ge(self.full, 1)
        ba = c.ps[:, 0, 0:32 * NTA].rearrange("p (t n) -> p t n", n=32)
        act.activation(self.beta, ba[:, :, 0:16], ACT.Sigmoid).then_inc(self.sigmoid, 1)
        act.wait_ge(self.shifted, 1)
        act.activation(self.t2, self.t1, ACT.Abs)
        act.drain()
        act.activation(self.t2, self.t2, ACT.Exp, scale=-1.0)
        act.drain()
        act.activation(self.t2, self.t2, ACT.Ln, bias=c.eps(2)).then_inc(self.soft, 1)

    def vector(self, dve):
        c = self.c

        def row(v):
            return v.unsqueeze(1).to_broadcast([P, NTA, 16])

        dve.wait_ge(self.rows, 48)
        dve.wait_ge(self.sigmoid, 1)
        ba = c.ps[:, 0, 0:32 * NTA].rearrange("p (t n) -> p t n", n=32)
        dve.tensor_tensor(self.t1, ba[:, :, 16:32], row(self.dt), ALU.add).then_inc(self.shifted, 1)
        dve.wait_ge(self.soft, 1)
        dve.scalar_tensor_tensor(out=self.t1, in0=self.t1, scalar=0.0, in1=self.t2, op0=ALU.max, op1=ALU.add)
        dve.drain()
        dve.tensor_tensor(self.t1, self.t1, row(self.alog), ALU.mult)
        dve.drain()
        dve.tensor_scalar(self.g, self.t1, -1.0, None, ALU.mult).then_inc(self.gate, 1)
        dve.wait_ge(self.summed, 1)
        for b in range(2):
            dve.tensor_copy(self.gcum[:, :, 8 * b:8 * b + 8],
                            c.ps[:, 1 + b, 0:96].rearrange("p (t n) -> p t n", n=16)[:, :, 8 * b:8 * b + 8])


class DeltaHeads(Stage):
    PER = {"slab": 64, "full": 6, "centre": 5, "conv": 5, "silu": 5, "square": 3, "sumsq": 4,
           "std": 2, "root": 2, "unit": 2, "turned": 2, "turned_out": 2, "cols": 2, "rows": 2, "grown": 2, "kb": 2, "darg": 2,
           "dexp": 2, "kk": 2, "kdarg": 2, "mt": 14, "a": 14, "a_out": 12, "x": 12, "upd": 15,
           "z": 12, "r": 12, "vn": 12, "vn_out": 13, "vnd": 12, "su": 12, "s": 13, "o": 1,
           "end": 3}

    def __init__(self, core):
        super().__init__(core)
        self.s = {n: core.sem("dn_" + n) for n in self.PER}
        v = core.view
        self.z, self.q, self.k, self.v = v(G_Z, T), v(G_Q, T), v(G_K, KEYS), v(G_V, KEYS)
        self.kt, self.vt = v(G_KT, NTA, P), v(G_VT, NTA, P)
        self.g, self.beta, self.gcum, self.kd, self.gl = (v(G_COL + 12 * i, 2, NTA) for i in range(5))
        self.order = [[0, 1, 2, 3, 4, 5], [1, 0, 5, 4, 3, 2]]
        self.o = v(G_O, T)
        self.taps = v(G_TAPS, 3, 3)
        self.z_now = v(G_MIX + KD * T, T)
        self.root = v(G_MIX + KD * T + T, 14)
        core.mix = v(G_MIX, KD, T)
        self.before = len(core.slabs)

    def lane(self, l, at, *dims):
        return self.c.view(G_LANE + LANE * l + at, *dims)

    def st(self, l, i):
        return self.c.view(G_S + P * (4 * l + i), P)

    def wait(self, eng, h, name, n):
        eng.wait_ge(self.s[name], h * self.PER[name] + n)

    def wait_mixed(self, eng, h, name, n):
        first = {"cols": 1, "square": 2, "sumsq": 2, "std": 1, "root": 1}[name]
        eng.wait_ge(self.s[name], h * self.PER[name] + first + n)

    def end(self, eng, h):
        eng.drain().then_inc(self.s["end"], 1)
        self.wait(eng, h, "end", 3)

    TILES = [(0, False), (1, True), (1, False), (2, True), (2, False), (3, False)]

    def slab_dst(self):
        return self.c.view(RING0 + SLOT * (self.before % SLOTS), 4, KD, P)

    def sync(self, sp):
        c = self.c
        w = c.d["w_in_a_2"][0]
        slot = self.before % SLOTS
        if self.before >= SLOTS:
            sp.wait_ge(c.slab_out[slot], self.before // SLOTS)

        def load(h):
            for part in range(4):
                sp.dma_start(self.slab_dst()[:, part], w[:, ds(h * P + D * part, P)].rearrange("(k p) n -> p k n", p=P))\
                    .then_inc(self.s["slab"], 16)

        load(0)
        with sp.Fori(0, DHEADS - 1) as h:
            self.wait(sp, h, "full", 6)
            load(h + 1)
        self.wait(sp, DHEADS - 1, "full", 6)

    def tensor(self, pe):
        for i in range(6):
            self.project(pe, 0, i, range(KD))
        self.lengths(pe, 0, 0, 0)
        with pe.Fori(0, DHEADS - 1) as h:
            self.tensor_head(pe, h, True)
        self.tensor_head(pe, DHEADS - 1, False)

    def vector(self, dve):
        self.load_taps(dve, 0)
        for i in range(5):
            self.convolve(dve, 0, i)
        self.unit(dve, 0, 0)
        with dve.Fori(0, DHEADS - 1) as h:
            self.vector_head(dve, h, True)
        self.vector_head(dve, DHEADS - 1, False)

    def scalar(self, act):
        for i in range(6):
            self.evacuate(act, 0, i)
        self.squares(act, 0)
        self.roots(act, 0, 6, slice(0, NTA + NT))
        with act.Fori(0, DHEADS - 1) as h:
            self.scalar_head(act, h, True)
        self.scalar_head(act, DHEADS - 1, False)

    def project(self, pe, h, i, ks):
        c = self.c
        part, ctx = self.TILES[i]
        src, n = (c.hc, TC) if ctx else (c.h, T)
        if ks[0] == 0:
            if i == 0:
                self.wait(pe, h, "slab", 64)
            if i >= 4:
                self.wait(pe, h, "conv", i - 3)
        for k in ks:
            ins = pe.matmul(c.ps[:, 4 + i % 4, 0:n], self.slab_dst()[:, part, k, :], src[:, k, :],
                            start=(k == 0), stop=(k == KD - 1))
        if ks[-1] == KD - 1:
            ins.then_inc(self.s["full"], 1)

    def lengths(self, pe, h, squares, roots):
        c, ident = self.c, self.c.const("ident")
        self.wait(pe, h, "conv", 5)
        for i, (at, n) in enumerate(((0, NTA), (NTA, NT))):
            pe.wait_ge(self.s["square"], squares + i + 1)
            for t in range(n):
                ins = pe.matmul(c.ps[:, 6, at + t:at + t + 1], self.lane(i, L_L, n, P)[:, t, :],
                                c.const("ones")[:, 0:1], start=True, stop=True)
        ins.then_inc(self.s["sumsq"], 1)
        pe.wait_ge(self.s["root"], roots + 1)
        for t in range(NTA + NT):
            out = c.pair(6, KEYS)[:, P * t:P * t + P] if t < NTA else c.ps[:, 4, P * (t - NTA):P * (t - NTA) + P]
            ins = pe.matmul(out, self.root[:, t:t + 1].to_broadcast([P, P]), ident, start=True, stop=True)
        ins.then_inc(self.s["sumsq"], 1)

    def evacuate(self, act, h, i):
        c, s = self.c, self.s
        part, ctx = self.TILES[i]
        if i == 0:
            act.wait_ge(s["cols"], 2 * h + 1)
        self.wait(act, h, "full", i + 1)
        if i < 5:
            act.activation(self.dest(i), c.ps[:, 4 + i % 4, 0:TC if ctx else T], ACT.Copy, scale=self.col(1, part))\
                .then_inc(s["centre"], 1)
        else:
            act.activation(self.z, c.ps[:, 5, :], ACT.Silu)
        if i:
            self.wait(act, h, "conv", i)
            act.activation(self.dest(i - 1), self.dest(i - 1), ACT.Silu).then_inc(s["silu"], 1)

    def convolve(self, dve, h, i):
        part, ctx = self.TILES[i]
        self.wait(dve, h, "centre", i + 1)
        conv3(dve, self.dest(i), self.c.ps[:, 4 + i % 4, :], self.col(0, part), self.col(2, part), TC if ctx else T)\
            .then_inc(self.s["conv"], 1)

    def load_taps(self, dve, h):
        taps = self.c.view(PAR0 + PAR["conv_a0"][0], 3, 3, DHEADS)
        for tap in range(3):
            dve.tensor_copy(self.taps[:, tap, :].unsqueeze(2), taps[:, tap, :, ds(h, 1)])
        dve.drain().then_inc(self.s["cols"], 1)

    def squares(self, act, h):
        act.drain()
        for i, v in enumerate((self.k, self.q)):
            act.activation(self.lane(i, L_L, (KEYS, T)[i]), v, ACT.Square).then_inc(self.s["square"], 1)

    def roots(self, act, sums, bank, cols):
        act.wait_ge(self.s["sumsq"], sums + 1)
        n = cols.stop - cols.start
        act.activation(self.root[:, cols], self.c.ps[:, bank, 0:n], ACT.Sqrt, bias=self.c.eps(1)).then_inc(self.s["std"], 1)

    def invert(self, dve, std, cols):
        dve.wait_ge(self.s["std"], std + 1)
        dve.reciprocal(self.root[:, cols], self.root[:, cols])
        dve.drain().then_inc(self.s["root"], 1)

    def unit(self, dve, sums, std):
        c = self.c
        self.invert(dve, std, slice(0, NTA + NT))
        dve.wait_ge(self.s["sumsq"], sums + 2)
        for v, rows, scale in ((self.k, c.pair(6, KEYS), 1.0), (self.q, c.ps[:, 4, :], P ** -0.5)):
            dve.scalar_tensor_tensor(out=v, in0=v, scalar=scale, in1=rows, op0=ALU.mult, op1=ALU.mult)\
                .then_inc(self.s["unit"], 1)

    def tensor_head(self, pe, h, more):
        c, s = self.c, self.s
        ident = c.const("ident")
        self.wait(pe, h, "unit", 2)
        for t in range(NTA):
            ins = pe.transpose(c.pair(4, KEYS)[:, P * t:P * t + P], self.v[:, P * t:P * t + P], ident)
        ins.then_inc(s["turned"], 1)
        for t in range(NTA):
            ins = pe.transpose(c.pair(6, KEYS)[:, P * t:P * t + P], self.k[:, P * t:P * t + P], ident)
        ins.then_inc(s["turned"], 1)
        self.wait_mixed(pe, h, "cols", 1)
        self.wait(pe, h, "turned_out", 2)
        for l in range(2):
            for t in range(NTA):
                pe.matmul(c.pair(4 * l, KEYS)[:, P * t:P * t + P], self.g[:, l, t:t + 1].to_broadcast([P, P]),
                          c.const(("cum_f", "cum_b")[l]), start=True, stop=True)
                ins = pe.matmul(c.pair(4 * l + 2, KEYS)[:, P * t:P * t + P],
                                self.beta[:, l, t:t + 1].to_broadcast([P, P]), ident, start=True, stop=True)
            ins.then_inc(s["rows"], 1)
        for l in range(2):
            self.wait(pe, h, "kb", l + 1)
            self.wait(pe, h, "grown", l + 1)
            self.wait(pe, h, "kdarg", l + 1)
            for t in range(NTA):
                cols = slice(P * t, P * t + P)
                ins = pe.matmul(c.pair(4 * l, KEYS)[:, cols], self.k[:, cols], self.lane(l, L_T, KEYS)[:, cols],
                                start=True, stop=True)
                if t >= NTC:
                    ins = pe.matmul(c.ps[:, 4 * l + 2, P * (t - NTC):P * (t - NTC) + P], self.k[:, cols],
                                    self.q[:, P * (t - NTC):P * (t - NTC) + P], start=True, stop=True)
            ins.then_inc(s["kk"], 1)
        for v in range(LEVELS):
            for l in range(2):
                i = 2 * v + l
                T_, TT, A, M = (self.lane(l, a, NTA, P) for a in (L_T, L_TT, L_A, L_M))
                self.wait(pe, h, "mt", i + 1)
                if v:
                    self.wait(pe, h, "upd", i - 1)
                for t in range(NTA):
                    ins = pe.matmul(c.pair(4 * l, KEYS)[:, P * t:P * t + P], M[:, t, :], T_[:, t, :] if v else ident,
                                    start=True, stop=True)
                ins.then_inc(s["a"], 1)
            if v == 0:
                continue
            for l in range(2):
                i = 2 * v + l
                T_, TT, A, M = (self.lane(l, a, NTA, P) for a in (L_T, L_TT, L_A, L_M))
                self.wait(pe, h, "a_out", i - 1)
                for t in range(NTA):
                    if v < LEVELS - 1:
                        pe.matmul(c.pair(4 * l + 2, KEYS)[:, P * t:P * t + P], TT[:, t, :], A[:, t, :], start=True, stop=True)
                    ins = pe.matmul(c.pair(4 * l, KEYS)[:, P * t:P * t + P], A[:, t, :], TT[:, t, :], start=True, stop=True)
                ins.then_inc(s["x"], 1)
        for step in range(NTA):
            for l in range(2):
                i = 2 * step + l
                t = self.order[l][step]
                if step == 0:
                    self.wait(pe, h, "upd", 13 + l)
                    self.wait(pe, h, "upd", 15)
                else:
                    self.wait(pe, h, "s", i - 1)
                pe.matmul(c.ps[:, 2 * l, 0:P], self.lane(l, L_KBG, NTA, P)[:, t, :], self.st(l, 0), start=True, stop=True)\
                    .then_inc(s["z"], 1)
            if more:
                self.project(pe, h + 1, step, range(0, 2))
            for l in range(2):
                i = 2 * step + l
                t = self.order[l][step]
                self.wait(pe, h, "r", i + 1)
                pe.matmul(c.ps[:, 2 * l, P:2 * P], self.lane(l, L_TT, NTA, P)[:, t, :], self.st(l, 1), start=True, stop=True)\
                    .then_inc(s["vn"], 1)
            if more:
                self.project(pe, h + 1, step, range(2, 5))
            for l in range(2):
                i = 2 * step + l
                t = self.order[l][step]
                if t >= NTC:
                    out = c.ps[:, 2 * l + 1, P * (t - NTC):P * (t - NTC) + P]
                    cols = slice(P * (t - NTC), P * (t - NTC) + P)
                    pe.matmul(out, self.st(l, 0), self.lane(l, L_QD, T)[:, cols], start=True, stop=False)
                self.wait(pe, h, "vn_out", i + 1)
                if t >= NTC:
                    pe.matmul(out, self.st(l, 2), self.lane(l, L_QK, T)[:, cols], start=False, stop=True)
                self.wait(pe, h, "vnd", i + 1)
                pe.matmul(c.ps[:, 2 * l, 2 * P:3 * P], self.kt[:, t, :], self.st(l, 3), start=True, stop=True)\
                    .then_inc(s["su"], 1)
            if more:
                self.project(pe, h + 1, step, range(5, KD))
        pe.drain().then_inc(s["o"], 1)
        if more:
            self.lengths(pe, h + 1, 3 * h + 2, 2 * h + 1)
        self.wait_mixed(pe, h, "square", 3 if more else 1)
        for t in range(NT):
            ins = pe.matmul(c.ps[:, 0, t:t + 1], self.lane(0, L_T, NT, P)[:, t, :], c.const("one_over_p")[:, 0:1],
                            start=True, stop=True)
        ins.then_inc(s["sumsq"], 1)
        self.wait_mixed(pe, h, "root", 2 if more else 1)
        for t in range(NT):
            ins = pe.matmul(c.ps[:, 2, P * t:P * t + P], self.root[:, NTA + NT + t:NTA + NT + t + 1].to_broadcast([P, P]),
                            ident, start=True, stop=True)
        ins.then_inc(s["sumsq"], 1)
        self.end(pe, h)

    def dest(self, i):
        return (self.q, self.k[:, 0:TC], self.k[:, TC:KEYS], self.v[:, 0:TC], self.v[:, TC:KEYS])[i]

    def col(self, tap, part):
        return self.taps[:, tap, part:part + 1]

    def scalar_head(self, act, h, more):
        c, s = self.c, self.s
        self.wait(act, h, "turned", 2)
        act.activation(self.kt.rearrange("p t n -> p (t n)"), c.pair(6, KEYS), ACT.Copy).then_inc(s["turned_out"], 1)
        for l in range(2):
            self.wait(act, h, "rows", l + 1)
            act.activation(self.lane(l, L_A, KEYS), c.pair(4 * l, KEYS), ACT.Exp)
            act.drain().then_inc(s["grown"], 1)
        for l in range(2):
            self.wait(act, h, "darg", l + 1)
            m = self.lane(l, L_M, KEYS)
            act.activation(m, m, ACT.Exp)
            self.wait(act, h, "kdarg", l + 1)
            act.activation(self.kd[:, l, :], self.kd[:, l, :], ACT.Exp)
            act.drain().then_inc(s["dexp"], 1)
        for v in range(1, LEVELS):
            for l in range(2):
                i = 2 * v + l
                self.wait(act, h, "a", i + 1)
                act.activation(self.lane(l, L_A, KEYS), c.pair(4 * l, KEYS), ACT.Copy).then_inc(s["a_out"], 1)
        for i in range(2 * NTA):
            l = i % 2
            self.wait(act, h, "vn", i + 1)
            act.activation(self.st(l, 2), c.ps[:, 2 * l, P:2 * P], ACT.Copy).then_inc(s["vn_out"], 1)
            if more and l:
                if i > 1:
                    self.evacuate(act, h + 1, i // 2 - 1)
        if more:
            self.evacuate(act, h + 1, 5)
            self.squares(act, h + 1)
        self.wait(act, h, "o", 1)
        act.activation(self.o, c.ps[:, 1, :], ACT.Copy).then_inc(s["vn_out"], 1)
        if more:
            self.roots(act, 4 * h + 2, 6, slice(0, NTA + NT))
        self.wait(act, h, "s", 13)
        act.activation(self.lane(0, L_T, T), self.o, ACT.Square).then_inc(s["square"], 1)
        self.roots(act, 4 * h + (4 if more else 2), 0, slice(NTA + NT, NTA + 2 * NT))
        self.end(act, h)

    def vector_head(self, dve, h, more):
        c, s = self.c, self.s
        for dst, src in ((self.g, G_G), (self.beta, G_BETA), (self.gcum, G_GC)):
            v = c.view(src, NTA, 2, DHEADS)
            for l in range(2):
                dve.tensor_copy(dst[:, l, :].unsqueeze(2), v[:, :, l, ds(h, 1)])
        dve.drain().then_inc(s["cols"], 1)
        self.wait(dve, h, "silu", 5)
        dve.tensor_copy(self.z_now, self.z)
        self.wait(dve, h, "turned", 1)
        dve.tensor_copy(self.vt.rearrange("p t n -> p (t n)"), c.pair(4, KEYS)).then_inc(s["turned_out"], 1)
        for l in range(2):
            kb, m = self.lane(l, L_T, KEYS), self.lane(l, L_M, NTA, P)
            rows = c.pair(4 * l, KEYS).rearrange("p (t n) -> p t n", n=P)
            self.wait(dve, h, "rows", l + 1)
            dve.tensor_tensor(kb, self.k, c.pair(4 * l + 2, KEYS), ALU.mult).then_inc(s["kb"], 1)
            self.wait(dve, h, "grown", l + 1)
            for t in range(NTA):
                dve.tensor_scalar(m[:, t, :], rows[:, t, :], self.gcum[:, l, t:t + 1], 0.0, ALU.subtract, ALU.min)
            dve.drain().then_inc(s["darg"], 1)
            last = P - 1 if l == 0 else 0
            dve.tensor_tensor(self.kd[:, l, :], rows[:, :, last], self.gcum[:, l, :], ALU.subtract)
            dve.drain().then_inc(s["kdarg"], 1)
        ident = c.const("ident").unsqueeze(1).to_broadcast([P, NTA, P])

        def mask(v, l):
            m = c.view(G_MASK + P * (7 * l + v), P).unsqueeze(1).to_broadcast([P, NTA, P])
            dve.tensor_tensor(self.lane(l, L_M, NTA, P), self.lane(l, L_L, NTA, P), m, ALU.mult).then_inc(s["mt"], 1)

        for l in range(2):
            self.wait(dve, h, "dexp", l + 1)
            m = self.lane(l, L_M, NTA, P)
            tri = c.const(("cum_f", "cum_b")[l]).unsqueeze(1).to_broadcast([P, NTA, P])
            dve.tensor_tensor(m, m, tri, ALU.mult)
            dve.drain()
            self.wait(dve, h, "kk", l + 1)
            flat = self.lane(l, L_M, KEYS)
            dve.tensor_tensor(self.lane(l, L_L, KEYS), flat, c.pair(4 * l, KEYS), ALU.mult)
            dve.tensor_tensor(self.lane(l, L_QK, T), flat[:, TC:KEYS], c.ps[:, 4 * l + 2, :], ALU.mult)
            dve.drain()
            mask(0, l)
        for l in range(2):
            kb, kbg, grown = self.lane(l, L_T, KEYS), self.lane(l, L_KBG, KEYS), self.lane(l, L_A, KEYS)
            last = P - 1 if l == 0 else 0
            dve.tensor_tensor(kbg, kb, grown, ALU.mult)
            dve.tensor_tensor(self.lane(l, L_QD, T), self.q, grown[:, TC:KEYS], ALU.mult)
            dve.tensor_copy(self.gl[:, l, :], grown.rearrange("p (t n) -> p t n", n=P)[:, :, last])
        dve.drain()
        for v in range(LEVELS):
            if 0 < v < LEVELS - 1:
                for l in range(2):
                    self.wait(dve, h, "a", 2 * v + l + 1)
                    mask(v + 1, l)
            for l in range(2):
                i = 2 * v + l
                T_, TT, M = (self.lane(l, a, NTA, P) for a in (L_T, L_TT, L_M))
                ax, xx = (c.pair(4 * l + b, KEYS).rearrange("p (t n) -> p t n", n=P) for b in (0, 2))
                if v == 0:
                    self.wait(dve, h, "a", i + 1)
                    dve.tensor_tensor(TT, ident, M, ALU.subtract)
                    dve.tensor_tensor(T_, ident, ax, ALU.subtract)
                else:
                    self.wait(dve, h, "x", i - 1)
                    if v < LEVELS - 1:
                        dve.tensor_tensor(T_, T_, xx, ALU.subtract)
                    dve.tensor_tensor(TT, TT, ax, ALU.subtract)
                dve.drain().then_inc(s["upd"], 1)
                if v == 0:
                    mask(1, l)
        for l in range(2):
            dve.memset(self.st(l, 0), 0.0)
        dve.drain().then_inc(s["upd"], 1)
        if more:
            self.load_taps(dve, h + 1)
        for step in range(NTA):
            for l in range(2):
                i = 2 * step + l
                t = self.order[l][step]
                self.wait(dve, h, "z", i + 1)
                dve.scalar_tensor_tensor(out=self.st(l, 1), in0=self.vt[:, t, :], scalar=self.beta[:, l, t:t + 1],
                                         in1=c.ps[:, 2 * l, 0:P], op0=ALU.mult, op1=ALU.subtract).then_inc(s["r"], 1)
            for l in range(2):
                i = 2 * step + l
                t = self.order[l][step]
                self.wait(dve, h, "vn_out", i + 1)
                dve.tensor_scalar(self.st(l, 3), self.st(l, 2), self.kd[:, l, t:t + 1], None, ALU.mult)\
                    .then_inc(s["vnd"], 1)
            if more and step:
                self.convolve(dve, h + 1, step - 1)
            for l in range(2):
                i = 2 * step + l
                t = self.order[l][step]
                self.wait(dve, h, "su", i + 1)
                dve.scalar_tensor_tensor(out=self.st(l, 0), in0=self.st(l, 0), scalar=self.gl[:, l, t:t + 1],
                                         in1=c.ps[:, 2 * l, 2 * P:3 * P], op0=ALU.mult, op1=ALU.add).then_inc(s["s"], 1)
        self.wait(dve, h, "vn_out", 13)
        dve.tensor_tensor(self.o, self.o, c.ps[:, 3, :], ALU.add).then_inc(s["s"], 1)
        if more:
            self.unit(dve, 4 * h + 2, 2 * h + 1)
        self.invert(dve, 2 * h + (2 if more else 1), slice(NTA + NT, NTA + 2 * NT))
        self.wait_mixed(dve, h, "sumsq", 4 if more else 2)
        dve.tensor_tensor(self.o, self.o, c.ps[:, 2, :], ALU.mult)
        dve.drain()
        dve.scalar_tensor_tensor(out=c.view(G_MIX, KD * T)[:, ds(h * T, T)], in0=self.o, scalar=c.par("onorm_a"),
                                 in1=self.z_now, op0=ALU.mult, op1=ALU.mult)
        self.end(dve, h)



R_HT = W0
R_W = R_HT + NT * D
R_SM = R_W + KD * 36
R_END = R_SM + 3600
M_KEEP = W0 + WORK - 256
M_WT = M_KEEP
M_PLAN = M_KEEP + 8
M_IDX = M_KEEP + 112
M_GI = M_KEEP + 200
M_SLOT = W0
M_G = M_SLOT + 2 * SLOT
M_GT = M_G + 2 * D
M_S = M_GT + D
M_HH = M_S + 512
M_HT = M_HH + 512
M_Y = M_HT + 512
PAD = 1 << 20
TABLE = (BLOCKS + 2) * P


class Route(Stage):

    def __init__(self, core, i):
        super().__init__(core)
        self.i = i
        self.per = {"w": 32, "turned": 8, "turned_out": 8, "stored": 16, "logits": 1, "gsub": 1, "gexp": 1,
                    "esub": 1, "eexp": 1, "rank": 1, "filled": 16, "placed": 128, "back": 16,
                    "hot_done": 1, "dest_done": 1, "vals_done": 1}
        self.base = {}
        for n, k in self.per.items():
            self.base[n] = core.shared("route_" + n, k)[1]
        (self.w, self.turned, self.turned_out, self.stored, self.logits, self.gsub, self.gexp, self.esub,
         self.eexp, self.rank, self.filled, self.placed, self.back, self.hot_done, self.dest_done,
         self.vals_done) = (
            core.shared("route_" + n, 0)[0] for n in ("w", "turned", "turned_out", "stored", "logits",
                "gsub", "gexp", "esub", "eexp", "rank", "filled", "placed", "back", "hot_done",
                "dest_done", "vals_done"))
        v = core.view
        at = [R_SM]

        def new(*dims):
            a = at[0]
            at[0] += int(np.prod(dims))
            return v(a, *dims)

        self.new = new
        self.lg = new(NT, 36)
        self.eg, self.e8 = new(NT, GROUPS), new(NT, PER_GROUP)
        self.hot = new(2, NT, EXPERTS)
        self.both = new(NT, EXPERTS)
        self.destf = new(2, NT)
        self.dest = new(2, NT).bitcast(U32)
        self.vals = new(2, NT, 2).bitcast(I32)
        self.padv = new(2 * (BLOCKS + 2)).bitcast(I32)
        self.ht = v(R_HT, NT, D)
        self.rw = v(R_W, KD, 36)

    def scalar(self, act):
        c, d = self.c, self.c.d
        act.dma_start(self.rw[:, :, 0:GROUPS], d["router_g_2"][self.i].rearrange("(k p) n -> p k n", p=P)).then_inc(self.w, 16)
        act.dma_start(self.rw[:, :, GROUPS:36], d["router_e_2"][self.i].rearrange("(k p) n -> p k n", p=P)).then_inc(self.w, 16)
        act.wait_ge(self.gsub, self.base["gsub"] + 1)
        act.activation(self.eg, self.eg, ACT.Exp).then_inc(self.gexp, 1)
        act.wait_ge(self.esub, self.base["esub"] + 1)
        act.activation(self.e8, self.e8, ACT.Exp).then_inc(self.eexp, 1)
        act.wait_ge(self.turned_out, self.base["turned_out"] + 8)
        act.dma_start(c.d["h_rows"].rearrange("(t p) n -> p t n", p=P), self.ht).then_inc(self.stored, 16)
        act.wait_ge(self.stored, self.base["stored"] + 16)
        act.wait_ge(self.placed, self.base["placed"] + 16 * 8)
        act.dma_start(c.view(M_IDX, BLOCKS + 2, 2).bitcast(I32), c.d["table"].rearrange("(b p) c -> p b c", p=P))\
            .then_inc(self.back, 16)
        act.wait_ge(self.back, self.base["back"] + 16)

    def gpsimd(self, pool):
        c = self.c
        for k in range(2):
            for j in range(2):
                pool.iota(self.vals[:, k, :, j], [[P, NT]], base=T * k * j, channel_multiplier=1)
        pool.memset(self.padv, PAD)
        pool.memset(c.view(M_G, 2, D), 0.0)
        if self.i == 0:
            pool.memset(c.view(M_Y, 2, D), 0.0)
        pool.drain().then_inc(self.vals_done, 1)
        pool.wait_ge(self.vals_done, self.base["vals_done"] + 1)
        pool.dma_start(c.d["table"].rearrange("(p b) c -> p (b c)", p=P), self.padv).then_inc(self.filled, 16)
        pool.wait_ge(self.filled, self.base["filled"] + 16)
        pool.wait_ge(self.dest_done, self.base["dest_done"] + 1)
        for k in range(2):
            for t in range(NT):
                pool.indirect_dma_start(c.d["table"], bass.IndirectOffsetOnAxis(ap=self.dest[:, k, t:t + 1], axis=0),
                                        self.vals[:, k, t, :], None).then_inc(self.placed, 16)
        pool.wait_ge(self.placed, self.base["placed"] + 16 * 8)

    def tensor(self, pe):
        c = self.c
        pe.wait_ge(self.w, self.base["w"] + 32)
        for t in range(NT):
            for k in range(KD):
                ins = pe.matmul(c.ps[:, 6, 36 * t:36 * t + 36], c.h[:, k, P * t:P * t + P], self.rw[:, k, :],
                                start=(k == 0), stop=(k == KD - 1))
        ins.then_inc(self.logits, 1)
        for i in range(8):
            t, half = i // 2, i % 2
            if i >= 4:
                pe.wait_ge(self.turned_out, self.base["turned_out"] + i - 3)
            for m in range(4):
                ins = pe.transpose(c.ps[:, i % 4, P * m:P * m + P], c.h[:, 4 * half + m, P * t:P * t + P], c.const("ident"))
            ins.then_inc(self.turned, 1)
        pe.wait_ge(self.hot_done, self.base["hot_done"] + 1)
        for t in range(NT):
            for b in range(t + 1):
                pe.matmul(c.ps[:, 7, 32 * t:32 * t + 32], c.const("before" if b == t else "ones"), self.both[:, b, :],
                          start=(b == 0), stop=(b == t))
        for t in range(NT):
            ins = pe.matmul(c.ps[:, 7, 128:160], c.const("ones"), self.both[:, t, :], start=(t == 0), stop=(t == NT - 1))
        ins.then_inc(self.rank, 1)

    def vector(self, dve):
        c, new = self.c, self.new
        iota = c.const("iota")

        def row(v, n, m):
            return v.unsqueeze(1).to_broadcast([P, n, m])

        def col(v, m):
            return v.unsqueeze(2).to_broadcast([P, v.shape[1], m])

        def tt(out, a, b, op):
            dve.tensor_tensor(out, a, b, op)
            dve.drain()

        def ts(out, a, s1, s2, op0, op1=ALU.bypass):
            if s2 is None:
                dve.tensor_scalar(out, a, s1, None, op0)
            else:
                dve.tensor_scalar(out, a, s1, s2, op0, op1)
            dve.drain()

        def reduce(out, a, op):
            dve.tensor_reduce(out, a, AX.X, op)
            dve.drain()

        def first_max(e, n):
            top, idx, hot = new(NT), new(NT), new(NT, n)
            reduce(top, e, ALU.max)
            tt(hot, e, col(top, n), ALU.is_ge)
            ts(hot, hot, -100.0, 100.0, ALU.mult, ALU.add)
            tt(hot, hot, row(iota[:, 0:n], NT, n), ALU.add)
            reduce(idx, hot, ALU.min)
            tt(hot, row(iota[:, 0:n], NT, n), col(idx, n), ALU.is_equal)
            return top, idx, hot

        dve.wait_ge(self.logits, self.base["logits"] + 1)
        dve.tensor_copy(self.lg, c.ps[:, 6, 0:36 * NT].rearrange("p (t n) -> p t n", t=NT))
        dve.drain()
        mg, sg, group_w = new(NT), new(NT), new(NT)
        reduce(mg, self.lg[:, :, 0:GROUPS], ALU.max)
        dve.tensor_tensor(self.eg, self.lg[:, :, 0:GROUPS], col(mg, GROUPS), ALU.subtract).then_inc(self.gsub, 1)
        for i in range(8):
            dve.wait_ge(self.turned, self.base["turned"] + i + 1)
            dve.tensor_copy(self.ht[:, i // 2, 512 * (i % 2):512 * (i % 2) + 512], c.ps[:, i % 4, :]).then_inc(self.turned_out, 1)
        dve.wait_ge(self.gexp, self.base["gexp"] + 1)
        reduce(sg, self.eg, ALU.add)
        top, gi, ghot = first_max(self.eg, GROUPS)
        dve.reciprocal(sg, sg)
        dve.drain()
        tt(group_w, top, sg, ALU.mult)
        pick, le, m8 = new(NT, GROUPS, PER_GROUP), new(NT, PER_GROUP), new(NT)
        for t in range(NT):
            dve.tensor_tensor(pick[:, t], self.lg[:, t, GROUPS:36].rearrange("p (g e) -> p g e", g=GROUPS),
                              ghot[:, t, :].unsqueeze(2).to_broadcast([P, GROUPS, PER_GROUP]), ALU.mult)
        dve.drain()
        for t in range(NT):
            dve.tensor_reduce(le[:, t, :], pick[:, t].rearrange("p g e -> p e g"), AX.X, ALU.add)
        dve.drain()
        reduce(m8, le, ALU.max)
        dve.tensor_tensor(self.e8, le, col(m8, PER_GROUP), ALU.subtract).then_inc(self.esub, 1)
        dve.wait_ge(self.eexp, self.base["eexp"] + 1)
        e1, i1, h1 = first_max(self.e8, PER_GROUP)
        ts(h1, h1, -2.0, None, ALU.mult)
        tt(self.e8, self.e8, h1, ALU.add)
        e2, i2, h2 = first_max(self.e8, PER_GROUP)
        den = new(NT)
        tt(den, e1, e2, ALU.add)
        dve.reciprocal(den, den)
        dve.drain()
        tt(den, den, group_w, ALU.mult)
        wt = c.view(M_WT, NT, 2)
        tt(wt[:, :, 0], den, e1, ALU.mult)
        tt(wt[:, :, 1], den, e2, ALU.mult)
        for k, idx in enumerate((i1, i2)):
            eid = new(NT)
            dve.scalar_tensor_tensor(out=eid, in0=gi, scalar=float(PER_GROUP), in1=idx, op0=ALU.mult, op1=ALU.add)
            dve.drain()
            tt(self.hot[:, k], row(iota[:, 0:EXPERTS], NT, EXPERTS), col(eid, EXPERTS), ALU.is_equal)
        tt(self.both, self.hot[:, 0], self.hot[:, 1], ALU.add)
        dve.drain().then_inc(self.hot_done, 1)
        dve.wait_ge(self.rank, self.base["rank"] + 1)
        cnt, nb, part, ends, base = new(EXPERTS), new(EXPERTS), new(EXPERTS), new(EXPERTS), new(NT, EXPERTS)
        dve.tensor_copy(cnt, c.ps[:, 7, 128:160])
        dve.tensor_copy(base, c.ps[:, 7, 0:128].rearrange("p (t e) -> p t e", t=NT))
        dve.drain()
        ts(nb, cnt, 0.0, None, ALU.is_gt)
        for b in range(1, NT):
            ts(part, cnt, float(P * b), None, ALU.is_gt)
            tt(nb, nb, part, ALU.add)
        dve.tensor_tensor_scan(ends, c.const("ones")[:, 0:EXPERTS], nb, 0.0, ALU.mult, ALU.add)
        dve.drain()
        tt(part, ends, nb, ALU.subtract)
        ts(part, part, float(P), None, ALU.mult)
        tt(base, base, row(part, NT, EXPERTS), ALU.add)
        for k in range(2):
            tt(self.hot[:, k], self.hot[:, k], base, ALU.mult)
            reduce(self.destf[:, k, :], self.hot[:, k], ALU.add)
        dve.tensor_copy(self.dest, self.destf)
        dve.drain().then_inc(self.dest_done, 1)
        planf, cmp = new(48), c.view(R_HT, BLOCKS, EXPERTS)
        dve.wait_ge(self.stored, self.base["stored"] + 16)
        tt(cmp, row(ends, BLOCKS, EXPERTS), col(iota[:, 0:BLOCKS], EXPERTS), ALU.is_le)
        reduce(planf[:, 0:BLOCKS], cmp, ALU.add)
        ts(planf[:, 0:BLOCKS], planf[:, 0:BLOCKS], float(EXPERTS - 1), None, ALU.min)
        even = new(BLOCKS // 2)
        ts(even, iota[:, 0:BLOCKS:2], ends[:, EXPERTS - 1:EXPERTS], None, ALU.is_lt)
        reduce(planf[:, BLOCKS:BLOCKS + 1], even, ALU.add)
        dve.tensor_copy(c.view(M_PLAN + 48 * self.i, BLOCKS + 1).bitcast(I32), planf[:, 0:BLOCKS + 1])


class Experts(Stage):

    def __init__(self, core, i, weights, before):
        super().__init__(core)
        self.i, self.before = i, before
        self.w1, self.w3, self.w2 = (core.d[w][i] for w in weights)
        self.w_in = [core.shared(f"expert_in{j}", 0)[0] for j in range(6)]
        self.w_out = [core.shared(f"expert_out{j}", 0)[0] for j in range(6)]
        self.gather = [core.shared(f"expert_gather{b}", 0)[0] for b in range(2)]
        self.scatter = [core.shared(f"expert_scatter{b}", 0)[0] for b in range(2)]
        (self.clear, self.turned, self.gt, self.h1, self.h3, self.silu, self.prod, self.hturned, self.ht,
         self.y, self.y_out, self.gidx, self.sidx, self.settled) = (
            core.shared("expert_" + n, 0)[0] for n in ("clear", "turned", "gt", "h1", "h3", "silu", "prod",
                "hturned", "ht", "y", "y_out", "gidx", "sidx", "settled"))
        v = core.view
        self.g, self.y_sb = v(M_G, 2, D), v(M_Y, 2, D)
        self.gt_sb, self.s_sb, self.hh, self.ht_sb = v(M_GT, KD, P), v(M_S, 512), v(M_HH, 512), v(M_HT, 4, P)
        self.plan = v(M_PLAN + 48 * i, BLOCKS + 1).bitcast(I32)
        self.plan_first = v(M_PLAN, BLOCKS + 1).bitcast(I32)
        self.idx = v(M_IDX, BLOCKS + 2, 2).bitcast(I32)
        self.gi = v(M_GI, 2).bitcast(I32)
        self.si = v(M_GI + 2, 2).bitcast(I32)

    def slot(self, j, *dims):
        return self.c.view(RING0 + SLOT * j if j < SLOTS else M_SLOT + SLOT * (j - SLOTS), *dims)

    def steps(self, eng):
        n = eng.value_load(self.plan[0:1, BLOCKS:BLOCKS + 1], min_val=1, max_val=BLOCKS // 2)
        if self.i == 0:
            return 0, n
        first = eng.value_load(self.plan_first[0:1, BLOCKS:BLOCKS + 1], min_val=1, max_val=BLOCKS // 2)
        return first, n

    def sync(self, sp):
        sp.wait_ge(self.c.stage_end, 4 * self.before)
        first, n = self.steps(sp)
        with sp.Fori(0, n) as step:
            i = first + step
            for b in range(2):
                e = sp.value_load(self.plan[0:1, ds(2 * step + b, 1)], min_val=0, max_val=EXPERTS - 1)
                for j, w in enumerate((self.w1, self.w3, self.w2)):
                    s = 3 * b + j
                    sp.wait_ge(self.w_out[s], i + 1)
                    src = w[ds(e, 1)].rearrange("a (k p) n -> p (a k) n", p=P)
                    sp.dma_start(self.slot(s, *((KD, 512) if j < 2 else (4, D))), src).then_inc(self.w_in[s], 16)
                    if b == 0 and j == 0:
                        sp.wait_ge(self.gather[0], 16 * (i + self.i) + 16)

    def open_room(self, eng, *sems):
        if self.i == 0:
            for s in sems:
                eng.sem_inc(s, 1)

    def settle(self, pool):
        pool.sem_inc(self.settled, 1)

    def gather_block(self, pool, b, block, i):
        pool.tensor_copy(self.gi[:, b:b + 1].unsqueeze(1), self.idx[:, ds(block, 1), 0:1]).then_inc(self.gidx, 1)
        pool.wait_ge(self.gidx, 2 * (i + self.i) + b + 1)
        self.settle(pool)
        pool.indirect_dma_start(self.g[:, b, :], None, self.c.d["h_rows"],
                                bass.IndirectOffsetOnAxis(ap=self.gi[:, b:b + 1].bitcast(U32), axis=0),
                                bounds_check=T - 1, oob_is_err=False).then_inc(self.gather[b], 16)

    def scatter_block(self, pool, b):
        pool.indirect_dma_start(self.c.d["pair_rows"],
                                bass.IndirectOffsetOnAxis(ap=self.si[:, b:b + 1].bitcast(U32), axis=0),
                                self.y_sb[:, b, :], None,
                                bounds_check=2 * T - 1, oob_is_err=False).then_inc(self.scatter[b], 16)

    def gpsimd(self, pool):
        if self.i == 0:
            pool.memset(self.si, PAD)
            pool.drain().then_inc(self.clear, 1)
            pool.wait_ge(self.clear, 1)
        first, n = self.steps(pool)
        if self.i == 0:
            for b in range(2):
                self.scatter_block(pool, b)
        for b in range(2):
            self.gather_block(pool, b, b, first)
        with pool.Fori(0, n) as step:
            i = first + step
            for b in range(2):
                pool.wait_ge(self.gather[b], 16 * (i + self.i) + 16)
                pool.wait_ge(self.turned, 2 * (2 * i + b + 1 + self.i))
                self.gather_block(pool, b, 2 * step + 2 + b, i + 1)
                pool.wait_ge(self.scatter[b], 16 * i + 16)
                pool.tensor_copy(self.si[:, b:b + 1].unsqueeze(1), self.idx[:, ds(2 * step + b, 1), 1:2]).then_inc(self.sidx, 1)
                pool.wait_ge(self.sidx, 2 * i + b + 1)
                pool.wait_ge(self.y_out, 4 * i + 2 * b + 3)
                self.settle(pool)
                self.scatter_block(pool, b)
        for b in range(2):
            pool.wait_ge(self.gather[b], 16 * (first + n + self.i) + 16)
            pool.wait_ge(self.scatter[b], 16 * (first + n) + 16)
        self.settle(pool)

    def tensor(self, pe):
        c = self.c
        ident = c.const("ident")

        def turn(b, i, r, half):
            if half == 0:
                pe.wait_ge(self.gather[b], 16 * (i + self.i) + 16)
                pe.wait_ge(self.gt, 2 * (r + self.i) + 1)
            for k in range(4):
                ins = pe.transpose(c.ps[:, half, P * k:P * k + P], self.g[:, b, P * (4 * half + k):P * (4 * half + k + 1)],
                                   ident)
            ins.then_inc(self.turned, 1)

        first, n = self.steps(pe)
        self.open_room(pe, *self.w_out, self.hturned)
        for half in range(2):
            turn(0, first, 2 * first, half)
        with pe.Fori(0, n) as step:
            i = first + step
            for b in range(2):
                r = 2 * i + b
                pe.wait_ge(self.gt, 2 * (r + self.i) + 3)
                for j, full in enumerate((self.h1, self.h3)):
                    s = 3 * b + j
                    w = self.slot(s, KD, 512)
                    pe.wait_ge(self.w_in[s], 16 * i + 16)
                    pe.wait_ge((self.silu, self.prod)[j], r + 1)
                    for k in range(KD):
                        ins = pe.matmul(c.ps[:, 2 + j, :], self.gt_sb[:, k, :], w[:, k, :], start=(k == 0), stop=(k == KD - 1))
                    ins.then_inc(full, 1)
                following = (1, i) if b == 0 else (0, i + 1)
                turn(*following, r + 1, 0)
                pe.wait_ge(self.prod, r + 2)
                pe.sem_inc(self.w_out[3 * b], 1)
                pe.sem_inc(self.w_out[3 * b + 1], 1)
                pe.wait_ge(self.ht, r + 1)
                for k in range(4):
                    ins = pe.transpose(c.ps[:, 4, P * k:P * k + P], self.hh[:, P * k:P * k + P], ident)
                ins.then_inc(self.hturned, 1)
                turn(*following, r + 1, 1)
                s = 3 * b + 2
                w = self.slot(s, 4, D)
                pe.wait_ge(self.w_in[s], 16 * i + 16)
                pe.wait_ge(self.ht, r + 2)
                pe.wait_ge(self.y_out, 2 * r + 1)
                for half in range(2):
                    for k in range(4):
                        ins = pe.matmul(c.ps[:, 5 + half, :], self.ht_sb[:, k, :], w[:, k, 512 * half:512 * half + 512],
                                        start=(k == 0), stop=(k == 3))
                    ins.then_inc(self.y, 1)
                pe.drain().then_inc(self.w_out[s], 1)

    def scalar(self, act):
        c = self.c
        first, n = self.steps(act)

        def gt(r):
            act.wait_ge(self.turned, 2 * (r + self.i) + 1)
            act.activation(self.gt_sb[:, 0:4, :].rearrange("p k n -> p (k n)"), c.ps[:, 0, :], ACT.Copy).then_inc(self.gt, 1)

        self.open_room(act, self.silu, self.gt, self.ht, self.y_out)
        gt(2 * first)
        with act.Fori(0, n) as step:
            i = first + step
            for b in range(2):
                r = 2 * i + b
                act.wait_ge(self.h1, r + 1)
                act.wait_ge(self.prod, r + 1)
                act.activation(self.s_sb, c.ps[:, 2, :], ACT.Silu).then_inc(self.silu, 1)
                gt(r + 1)
                act.wait_ge(self.hturned, r + 2)
                act.activation(self.ht_sb.rearrange("p k n -> p (k n)"), c.ps[:, 4, :], ACT.Copy).then_inc(self.ht, 1)
                act.wait_ge(self.y, 2 * r + 2)
                act.wait_ge(self.scatter[b], 16 * i + 16)
                act.activation(self.y_sb[:, b, 512:D], c.ps[:, 6, :], ACT.Copy).then_inc(self.y_out, 1)

    def vector(self, dve):
        c = self.c
        first, n = self.steps(dve)

        def gt(r):
            dve.wait_ge(self.turned, 2 * (r + self.i) + 2)
            dve.tensor_copy(self.gt_sb[:, 4:8, :].rearrange("p k n -> p (k n)"), c.ps[:, 1, :]).then_inc(self.gt, 1)

        self.open_room(dve, self.prod)
        gt(2 * first)
        with dve.Fori(0, n) as step:
            i = first + step
            for b in range(2):
                r = 2 * i + b
                dve.wait_ge(self.silu, r + 2)
                dve.wait_ge(self.h3, r + 1)
                dve.wait_ge(self.hturned, r + 1)
                dve.tensor_tensor(self.hh, self.s_sb, c.ps[:, 3, :], ALU.mult).then_inc(self.prod, 1)
                gt(r + 1)
                dve.wait_ge(self.y, 2 * r + 1)
                dve.wait_ge(self.scatter[b], 16 * i + 16)
                dve.tensor_copy(self.y_sb[:, b, 0:512], c.ps[:, 5, :]).then_inc(self.y_out, 1)


class Combine(Stage):

    def __init__(self, core, i, gate):
        super().__init__(core)
        self.i, self.gate = i, gate
        self.rows, self.rows0 = core.shared("combine_rows", 16 * NT)
        self.sum, self.sum0 = core.shared("combine_sum", NT)
        self.turned, self.turned0 = core.shared("combine_turned", KD)
        self.y = core.view(W0, NT, 2, D)

    def scalar(self, act):
        rows = self.c.d["pair_rows"].rearrange("(k t p) n -> p t k n", k=2, t=NT)
        for t in range(NT):
            act.dma_start(self.y[:, t], rows[:, t]).then_inc(self.rows, 16)

    def vector(self, dve):
        c = self.c
        wt = c.view(M_WT, NT, 2)
        dve.wait_ge(self.rows, self.rows0 + 16 * NT)
        for t in range(NT):
            a, b = self.y[:, t, 0, :], self.y[:, t, 1, :]
            dve.tensor_scalar(a, a, wt[:, t, 0:1], None, ALU.mult)
            dve.drain()
            dve.scalar_tensor_tensor(out=a, in0=b, scalar=wt[:, t, 1:2], in1=a, op0=ALU.mult, op1=ALU.add).then_inc(self.sum, 1)
        for m in range(KD):
            dve.wait_ge(self.turned, self.turned0 + m + 1)
            dve.scalar_tensor_tensor(out=c.x[:, m, :], in0=c.ps[:, m, :], scalar=self.gate(m), in1=c.x[:, m, :],
                                     op0=ALU.mult, op1=ALU.add)

    def tensor(self, pe):
        c = self.c
        pe.wait_ge(self.sum, self.sum0 + NT)
        for m in range(KD):
            for t in range(NT):
                ins = pe.transpose(c.ps[:, m, P * t:P * t + P], self.y[:, t, 0, P * m:P * m + P], c.const("ident"))
            ins.then_inc(self.turned, 1)


class Store(Stage):

    def __init__(self, core):
        super().__init__(core)
        self.stored, self.base = core.shared("loaded", 16)

    def scalar(self, act):
        act.dma_start(self.c.d["out"].rearrange("(k p) t -> p k t", p=P), self.c.h).then_inc(self.stored, 16)
        act.wait_ge(self.stored, self.base + 16)


def stages(core):
    c, d = core, core.d
    out = []

    def add(s):
        s.number = len(out)
        out.append(s)

    def g(layer, what):
        return lambda m: c.ada(layer, what, m)

    def p(name):
        return lambda m: c.par(name, m)

    add(Load(c))
    for i in range(2):
        if i == 0:
            add(Modulation(c, 0, d["mod_w"][0], "mod_b0", "c", "c_ctx", slabs=(0, 4)))
            add(Loaded(c))
        if i == 1:
            add(HyenaFilter(c))
        add(Norm(c, c.x, c.h, T, True, g(i, 1), g(i, 0), scratch=Y_HF if i else W0))
        if i == 0:
            add(Norm(c, c.hc, c.hc, TC, True, g(0, 7), g(0, 6)))
            add(AttentionIn(c, Modulation(c, 0, d["mod_w"][0], "mod_b0", "c", None, acc=A_P, slabs=(4, 12))))
            add(Attention(c))
            add(FourierMix(c))
            mix, w = c.view(A_MIX, KD, T), d["da_w_out"][0]
        else:
            add(HyenaIn(c, Modulation(c, 3, d["ada_w_2"][1], "ada_b1", "c_2", None, acc=Y_ACC)))
            add(HyenaConv(c))
            mix, w = c.mix, d["hy_w_out"][0]
        add(Project(c, w, mix, g(i, 2), ALPHA, room=W0))
        add(Norm(c, c.x, c.x, T, True, p(f"ln1_g{i}"), p(f"ln1_b{i}")))
        add(Norm(c, c.x, c.h, T, True, g(i, 4), g(i, 3)))
        if i == 0:
            side = Modulation(c, 1, d["mod_w"][1], "mod_b1", "c", None, acc=F_ACC)
        else:
            side = Modulation(c, 2, d["ada_w_2"][0], "ada_b0", "c_2", "c_ctx_2", acc=F_ACC)
        add(FfnIn(c, i, side))
        add(FfnOut(c, i, g(i, 5)))
        add(Norm(c, c.x, c.x, T, True, p(f"ln2_g{i}"), p(f"ln2_b{i}")))
    for i in range(2):
        l = 2 + i
        add(Gains(c, l, f"norm_mix{i}", 1))
        add(Gains(c, l, f"norm_ffn{i}", 4))
        if i == 0:
            add(Gains(c, l, "norm_mix0", 7))
            add(LoadContext(c))
            add(Norm(c, c.hc, c.hc, TC, False, g(l, 7), g(l, 6)))
        add(Norm(c, c.x, c.h, T, False, g(l, 1), g(l, 0)))
        if i == 0:
            add(DeltaGates(c))
            add(DeltaHeads(c))
            mix, w = c.mix, d["w_out_a_2"][0]
        else:
            add(ShortConv(c))
            mix, w = c.view(B_Y, KD, T), d["w_out_b_2"][0]
        add(Project(c, w, mix, g(l, 2), 1.0, room=B_END if i else W0))
        add(Norm(c, c.x, c.h, T, False, g(l, 4), g(l, 3)))
        add(Route(c, i))
        ex = Experts(c, i, ("w1_2", "w3_2", "w2_2"), len(out))
        ex.at = len(c.slabs)
        add(ex)
        add(Combine(c, i, g(l, 5)))
    add(Norm(c, c.x, c.h, T, False, p("final_norm"), None))
    add(Store(c))
    return out


def build(nc, d):
    with ExitStack() as stack:
        core = Core(nc, d, stack)
        plan = stages(core)
        block = stack.enter_context(nc.Block())

        def meet(eng, s):
            eng.drain().then_inc(core.stage_end, 1)
            eng.wait_ge(core.stage_end, 4 * (s.number + 1))

        @block.sync
        def _(sp):
            n = 0
            for s in plan:
                if isinstance(s, DeltaHeads):
                    while n < s.before:
                        core.load_slab(sp, n)
                        n += 1
                    s.sync(sp)
                if isinstance(s, Experts):
                    while n < s.at:
                        core.load_slab(sp, n)
                        n += 1
                    s.sync(sp)
                    sp.wait_ge(core.stage_end, 4 * (s.number + 1))
                    combine = plan[s.number + 1]
                    sp.wait_ge(combine.rows, combine.rows0 + 16 * NT)
            while n < len(core.slabs):
                core.load_slab(sp, n)
                n += 1

        @block.tensor
        def _(pe):
            for s in plan:
                s.tensor(pe)
                meet(pe, s)

        @block.scalar
        def _(act):
            for s in plan:
                s.scalar(act)
                meet(act, s)

        @block.vector
        def _(dve):
            for s in plan:
                s.vector(dve)
                meet(dve, s)

        @block.gpsimd
        def _(pool):
            for s in plan:
                s.gpsimd(pool)
                meet(pool, s)


_WEIGHTS = ("mod_w", "ffn_w_in", "ffn_w_out", "da_w_in", "da_w_out", "da_lam_q1", "da_lam_k1", "da_lam_q2",
            "da_lam_k2", "hy_w_in", "hy_f_w1", "hy_f_b1", "hy_f_w2", "hy_f_b2", "hy_f_w3", "hy_f_b3",
            "hy_f_freq", "hy_f_w4", "hy_w_out", "ada_w_2", "w_in_a_2", "a_log_a_2", "dt_bias_a_2",
            "w_out_a_2", "w_in_b_2", "w_out_b_2", "router_g_2", "router_e_2", "w1_2", "w3_2", "w2_2")


def layout(inputs):
    a = {k: np.asarray(v) for k, v in inputs.items()}
    vec = {}
    for i in range(2):
        vec[f"mod_b{i}"], vec[f"ada_b{i}"] = a["mod_b"][i], a["ada_b_2"][i]
        for n in ("ln1_g", "ln1_b", "ln2_g", "ln2_b"):
            vec[f"{n}{i}"] = a[n][i]
        for t in range(3):
            vec[f"ffn_conv_w{i}{t}"] = a["ffn_conv_w"][i, t]
        vec[f"ffn_conv_b{i}"] = a["ffn_conv_b"][i]
        vec[f"norm_mix{i}"], vec[f"norm_ffn{i}"] = a["norm_mix_2"][i], a["norm_ffn_2"][i]
    for t in range(3):
        vec[f"hy_conv_w{t}"], vec[f"conv_a{t}"], vec[f"conv_b{t}"] = (
            a["hy_conv_w"][0, t], a["conv_a_2"][0, t], a["conv_b_2"][0, t])
    vec["da_subln_g"], vec["hy_conv_b"], vec["hy_d"] = a["da_subln_g"][0], a["hy_conv_b"][0], a["hy_d"][0]
    vec["onorm_a"], vec["final_norm"] = a["onorm_a_2"][0], a["final_norm_2"]
    vec["c"], vec["c_ctx"], vec["c_2"], vec["c_ctx_2"] = a["c"][0], a["c_ctx"], a["c_2"][0], a["c_ctx_2"]
    rows = np.concatenate([vec[n].reshape(k, P) for n, k in _VECTORS])
    arrays = {n: np.ascontiguousarray(a[n]) for n in _WEIGHTS}
    arrays["vectors"] = np.ascontiguousarray(rows.T)
    arrays["x_t"] = np.ascontiguousarray(a["x"][0].T)
    arrays["ctx_t"] = np.ascontiguousarray(a["ctx"][0].T)
    arrays["ctx2_t"] = np.ascontiguousarray(a["ctx_2"][0].T)
    arrays.update(_constants())
    return arrays


def tensors(nc, arrays):
    d = {n: nc.dram_tensor(f"in_{n}", a.shape, mybir.dt.from_np(a.dtype), kind="ExternalInput").ap()
         for n, a in arrays.items()}
    d["out"] = nc.dram_tensor("out_t", (D, T), F32, kind="ExternalOutput").ap()
    d["h_rows"] = nc.dram_tensor("h_rows", (T, D), F32).ap()
    d["pair_rows"] = nc.dram_tensor("pair_rows", (2 * T, D), F32).ap()
    d["table"] = nc.dram_tensor("table", (TABLE, 2), I32).ap()
    return d


def kernel(**inputs):
    import concourse.bacc as _bacc
    from concourse.bass_utils import run_bass_kernel_spmd as _run

    nc = _bacc.Bacc("TRN2", target_bir_lowering=False, num_devices=1)
    arrays = layout(inputs)
    d = tensors(nc, arrays)
    build(nc, d)
    r = _run(nc, [{f"in_{n}": a for n, a in arrays.items()}], core_ids=[0])
    return np.ascontiguousarray(r.results[0]["out_t"].T)[None]
```
